# Optimizing a Trainium2 kernel written in Bass

```python
import math
import jax
import jax.numpy as jnp
from jax import lax
import numpy as np

D_MODEL = 1024
BATCH = 1
SEQ = 256
DEPTH = 2

N_MIXERS = 4
EPS = 1e-6
MACARON_W = 0.5
D_FF = 2816
ROPE_BASE = 10000.0
REL_BUCKETS = 32
REL_MAX_DIST = 128
MLA_HEADS = 16
MLA_Q_RANK = 384
MLA_KV_RANK = 256
MLA_NOPE = 64
MLA_ROPE = 32
MLA_V = 64
MLA_Q_BLOCK = 128
RWKV_HEAD = 64
RWKV_HEADS = D_MODEL // RWKV_HEAD
RWKV_DECAY_LORA = 64
RWKV_A_LORA = 64
RWKV_GATE_LORA = 160
RWKV_GN_EPS = 64e-5
MOBA_HEADS = 16
MOBA_HEAD_DIM = D_MODEL // MOBA_HEADS
MOBA_BLOCK = 256
MOBA_TOPK = 3
MOBA_Q_CHUNK = 32
RET_HEADS = 4
RET_DK = D_MODEL // RET_HEADS
RET_DV = 2 * D_MODEL // RET_HEADS
RET_CHUNK = 128
RET_GN_EPS = 1e-5


def _rmsnorm(x, g):
    xf = x.astype(jnp.float32)
    y = xf * lax.rsqrt(jnp.mean(xf * xf, axis=-1, keepdims=True) + EPS)
    return (y * g.astype(jnp.float32)).astype(x.dtype)

def _modulate(x, g, shift, scale):
    return _rmsnorm(x, g) * (1 + scale[:, None, :]) + shift[:, None, :]

def _groupnorm_heads(y, w, b, eps):
    B, S, H, N = y.shape
    yf = y.astype(jnp.float32)
    mu = jnp.mean(yf, axis=-1, keepdims=True)
    var = jnp.mean(jnp.square(yf - mu), axis=-1, keepdims=True)
    yn = ((yf - mu) * lax.rsqrt(var + eps)).reshape(B, S, H * N)
    return yn * w.astype(jnp.float32) + b.astype(jnp.float32)

def _swiglu(h, w_in, w_out):
    gt, up = jnp.split(h @ w_in, 2, axis=-1)
    return (jax.nn.silu(gt) * up) @ w_out

def _rope_tables(seq, dim):
    inv = ROPE_BASE ** (-jnp.arange(0, dim, 2, dtype=jnp.float32) / dim)
    ang = jnp.arange(seq, dtype=jnp.float32)[:, None] * inv[None, :]
    return jnp.cos(ang), jnp.sin(ang)

def _apply_rope(x, cos, sin):
    half = x.shape[-1] // 2
    x1 = x[..., :half].astype(jnp.float32)
    x2 = x[..., half:].astype(jnp.float32)
    c = cos[None, :, None, :]
    s = sin[None, :, None, :]
    return jnp.concatenate([x1 * c - x2 * s, x1 * s + x2 * c], axis=-1).astype(x.dtype)

def _t5_bucket(dist):
    n = jnp.maximum(dist, 0)
    max_exact = REL_BUCKETS // 2
    nf = jnp.maximum(n, max_exact).astype(jnp.float32)
    large = max_exact + (jnp.log(nf / max_exact) / math.log(REL_MAX_DIST / max_exact)
                         * (REL_BUCKETS - max_exact)).astype(jnp.int32)
    large = jnp.minimum(large, REL_BUCKETS - 1)
    return jnp.where(n < max_exact, n, large)

def _dense_causal_attention(q, k, v):
    B, S, H, dq = q.shape
    dv = v.shape[-1]
    nq = S // MLA_Q_BLOCK
    qb = q.reshape(B, nq, MLA_Q_BLOCK, H, dq).transpose(1, 0, 3, 2, 4)
    kpos = jnp.arange(S)

    def one_block(args):
        qi, bi = args
        s = jnp.einsum('bhqd,bkhd->bhqk', qi, k).astype(jnp.float32)
        qpos = bi * MLA_Q_BLOCK + jnp.arange(MLA_Q_BLOCK)
        s = jnp.where(kpos[None, :] <= qpos[:, None], s, -jnp.inf)
        p = jax.nn.softmax(s, axis=-1).astype(v.dtype)
        return jnp.einsum('bhqk,bkhd->bqhd', p, v)

    o = lax.map(one_block, (qb, jnp.arange(nq)))
    return o.transpose(1, 0, 2, 3, 4).reshape(B, S, H * dv)

def _mla_mixer(h, w_in, q_norm, w_uq, kv_norm, w_ukv, w_out):
    B, S, _ = h.shape
    H = MLA_HEADS
    cq, ckv, k_rope = jnp.split(h @ w_in, [MLA_Q_RANK, MLA_Q_RANK + MLA_KV_RANK], axis=-1)
    q = (_rmsnorm(cq, q_norm) @ w_uq).reshape(B, S, H, MLA_NOPE + MLA_ROPE)
    kv = (_rmsnorm(ckv, kv_norm) @ w_ukv).reshape(B, S, H, MLA_NOPE + MLA_V)
    cos, sin = _rope_tables(S, MLA_ROPE)
    q = jnp.concatenate([q[..., :MLA_NOPE], _apply_rope(q[..., MLA_NOPE:], cos, sin)], axis=-1)
    k_rope = jnp.broadcast_to(_apply_rope(k_rope[:, :, None, :], cos, sin), (B, S, H, MLA_ROPE))
    k = jnp.concatenate([kv[..., :MLA_NOPE], k_rope], axis=-1)
    v = kv[..., MLA_NOPE:]
    o = _dense_causal_attention(q * (MLA_NOPE + MLA_ROPE) ** -0.5, k, v)
    return o @ w_out

def _rwkv7_mixer(h, mu, w_rkv, w0, wd1, wd2, a0, wa1, wa2, wg1, wg2, k_k, k_a, r_k, gn_w, gn_b, w_out):
    B, S, D = h.shape
    H, N = RWKV_HEADS, RWKV_HEAD
    xx = jnp.pad(h, ((0, 0), (1, 0), (0, 0)))[:, :-1] - h
    xs = h[:, :, None, :] + xx[:, :, None, :] * mu
    rkv = jnp.einsum('bsnd,nde->bsne', xs[:, :, :3], w_rkv)
    r, k, v = rkv[:, :, 0], rkv[:, :, 1], rkv[:, :, 2]
    xw, xa, xg = xs[:, :, 3], xs[:, :, 4], xs[:, :, 5]
    w = -jax.nn.softplus(-(w0 + jnp.tanh(xw @ wd1) @ wd2)) - 0.5
    decay = jnp.exp(-jnp.exp(w.astype(jnp.float32)))
    a = jax.nn.sigmoid((a0 + (xa @ wa1) @ wa2).astype(jnp.float32))
    g = jax.nn.sigmoid(xg @ wg1) @ wg2
    kk = (k * k_k).astype(jnp.float32).reshape(B, S, H, N)
    kk = kk / jnp.maximum(jnp.sqrt(jnp.sum(kk * kk, axis=-1, keepdims=True)), 1e-12)
    k_mod = k.astype(jnp.float32) * (1 + (a - 1) * k_a.astype(jnp.float32))

    def heads(t):
        return t.astype(jnp.float32).reshape(B, S, H, N)

    r_h, k_h, v_h, a_h, w_h = heads(r), heads(k_mod), heads(v), heads(a), heads(decay)

    def tm(t):
        return t.transpose(1, 0, 2, 3)

    def step(state, inp):
        r_t, w_t, k_t, v_t, ka_t, kb_t = inp
        sa = jnp.einsum('bhvk,bhk->bhv', state, ka_t)
        state = (state * w_t[:, :, None, :] + sa[..., None] * kb_t[:, :, None, :]
                 + v_t[..., None] * k_t[:, :, None, :])
        return state, jnp.einsum('bhvk,bhk->bhv', state, r_t)

    state0 = jnp.zeros((B, H, N, N), jnp.float32)
    _, y = lax.scan(step, state0, (tm(r_h), tm(w_h), tm(k_h), tm(v_h), tm(-kk), tm(kk * a_h)))
    y = y.transpose(1, 0, 2, 3)
    yn = _groupnorm_heads(y, gn_w, gn_b, RWKV_GN_EPS)
    bonus = (jnp.sum(r_h * k_h * r_k.astype(jnp.float32), axis=-1, keepdims=True) * v_h).reshape(B, S, D)
    return ((yn + bonus) * g.astype(jnp.float32)).astype(h.dtype) @ w_out

def _moba_mixer(h, w_in, rel_table, w_out):
    B, S, _ = h.shape
    H, dh, BLK, QC = MOBA_HEADS, MOBA_HEAD_DIM, MOBA_BLOCK, MOBA_Q_CHUNK
    qkv = (h @ w_in).reshape(B, S, 3, H, dh)
    q = qkv[:, :, 0].transpose(0, 2, 1, 3) * dh ** -0.5
    k = qkv[:, :, 1].transpose(0, 2, 1, 3)
    v = qkv[:, :, 2].transpose(0, 2, 1, 3)
    nb = -(-S // BLK)
    K = min(MOBA_TOPK, nb)
    pad = nb * BLK - S
    kb = jnp.pad(k, ((0, 0), (0, 0), (0, pad), (0, 0))).reshape(B, H, nb, BLK, dh)
    vb = jnp.pad(v, ((0, 0), (0, 0), (0, pad), (0, 0))).reshape(B, H, nb, BLK, dh)
    kmean = jnp.mean(kb.astype(jnp.float32), axis=3)
    table_t = rel_table.astype(jnp.float32).T
    nc = S // QC
    qc = q.reshape(B, H, nc, QC, dh).transpose(2, 0, 1, 3, 4)
    b_ix = jnp.arange(B)[:, None, None, None]
    h_ix = jnp.arange(H)[None, :, None, None]
    blk_ids = jnp.arange(nb)
    offs = jnp.arange(BLK)

    def chunk(args):
        qi, ci = args
        start = ci * QC
        qpos = start + jnp.arange(QC)
        own = start // BLK
        gate = jnp.einsum('bhqd,bhnd->bhqn', qi.astype(jnp.float32), kmean)
        gate = jnp.where(blk_ids < own, gate, -jnp.inf)
        top_s, top_i = lax.top_k(gate, K)
        valid = jnp.isfinite(top_s)
        k_sel = kb[b_ix, h_ix, top_i]
        v_sel = vb[b_ix, h_ix, top_i]
        pos_sel = top_i[..., None] * BLK + offs
        bias_sel = table_t[h_ix[..., None], _t5_bucket(qpos[:, None, None] - pos_sel)]
        s_sel = jnp.einsum('bhqd,bhqjkd->bhqjk', qi, k_sel).astype(jnp.float32) + bias_sel
        s_sel = jnp.where(valid[..., None], s_sel, -jnp.inf).reshape(B, H, QC, K * BLK)
        k_own = lax.dynamic_index_in_dim(kb, own, axis=2, keepdims=False)
        v_own = lax.dynamic_index_in_dim(vb, own, axis=2, keepdims=False)
        dist_own = qpos[:, None] - (own * BLK + offs)[None, :]
        s_own = jnp.einsum('bhqd,bhkd->bhqk', qi, k_own).astype(jnp.float32) + table_t[:, _t5_bucket(dist_own)]
        s_own = jnp.where(dist_own >= 0, s_own, -jnp.inf)
        p = jax.nn.softmax(jnp.concatenate([s_sel, s_own], axis=-1), axis=-1).astype(v.dtype)
        p_sel = p[..., :K * BLK].reshape(B, H, QC, K, BLK)
        p_own = p[..., K * BLK:]
        return (jnp.einsum('bhqjk,bhqjkd->bhqd', p_sel, v_sel)
                + jnp.einsum('bhqk,bhkd->bhqd', p_own, v_own))

    o = lax.map(chunk, (qc, jnp.arange(nc)))
    o = o.transpose(1, 0, 3, 2, 4).reshape(B, S, H * dh)
    return o @ w_out

def _retnet_mixer(h, w_in, gn_w, gn_b, w_out):
    B, S, D = h.shape
    H, DK, DV, C = RET_HEADS, RET_DK, RET_DV, RET_CHUNK
    q, k, v, g = jnp.split(h @ w_in, [D, 2 * D, 4 * D], axis=-1)
    cos, sin = _rope_tables(S, DK)
    q = _apply_rope(q.reshape(B, S, H, DK), cos, sin).astype(jnp.float32)
    k = _apply_rope(k.reshape(B, S, H, DK) * DK ** -0.5, cos, sin).astype(jnp.float32)
    v = v.reshape(B, S, H, DV).astype(jnp.float32)
    log_gamma = jnp.log1p(-jnp.exp2(-5.0 - jnp.arange(H, dtype=jnp.float32)))
    idx = jnp.arange(C, dtype=jnp.float32)
    diff = idx[:, None] - idx[None, :]
    dmask = jnp.where(diff >= 0, jnp.exp(jnp.maximum(diff, 0.0)[None] * log_gamma[:, None, None]), 0.0)
    zeta = jnp.exp((C - 1 - idx)[None, :] * log_gamma[:, None])
    xi = jnp.exp((idx + 1)[None, :] * log_gamma[:, None])
    gamma_c = jnp.exp(C * log_gamma)
    nc = S // C

    def chunks(t):
        return t.reshape(B, nc, C, H, t.shape[-1]).transpose(1, 0, 3, 2, 4)

    def step(R, inp):
        qc, kc, vc = inp
        inner = jnp.einsum('bhnd,bhmd->bhnm', qc, kc) * dmask
        o = (jnp.einsum('bhnm,bhme->bhne', inner, vc)
             + jnp.einsum('bhnd,bhde->bhne', qc, R) * xi[None, :, :, None])
        R = gamma_c[None, :, None, None] * R + jnp.einsum('bhmd,hm,bhme->bhde', kc, zeta, vc)
        return R, o

    R0 = jnp.zeros((B, H, DK, DV), jnp.float32)
    _, o = lax.scan(step, R0, (chunks(q), chunks(k), chunks(v)))
    o = o.transpose(1, 0, 3, 2, 4).reshape(B, S, H, DV)
    yn = _groupnorm_heads(o, gn_w, gn_b, RET_GN_EPS)
    return (jax.nn.silu(g.astype(jnp.float32)) * yn).astype(h.dtype) @ w_out

def first_inputs(seed: int = 0) -> dict:
    key = jax.random.key(seed)
    ks = iter(jax.random.split(key, 48))
    f32 = jnp.float32

    def nrm(shape, scale):
        return scale * jax.random.normal(next(ks), shape, f32)

    def uni(shape, lo, hi):
        return jax.random.uniform(next(ks), shape, f32, lo, hi)

    D = D_MODEL
    n_mla, n_rwkv, n_moba, n_ret = [len(range(m, DEPTH, N_MIXERS)) for m in range(N_MIXERS)]
    gate_offset = jnp.zeros((3,), f32).at[2].set(1.0)
    return {
        'x': nrm((BATCH, SEQ, D), 1.0),
        'c': nrm((BATCH, D), 1.0),
        'ada_w': nrm((DEPTH, D, 9 * D), 0.2 * D ** -0.5),
        'ada_b': (nrm((DEPTH, 3, 3, D), 0.02) + gate_offset[None, None, :, None]).reshape(DEPTH, 9 * D),
        'norm_g': 1.0 + nrm((DEPTH, 3, D), 0.05),
        'ffn_w_in': nrm((DEPTH, 2, D, 2 * D_FF), D ** -0.5),
        'ffn_w_out': nrm((DEPTH, 2, D_FF, D), D_FF ** -0.5),
        'final_g': 1.0 + nrm((D,), 0.05),
        'rel_table': nrm((REL_BUCKETS, MOBA_HEADS), 0.5),
        'mla_w_in': nrm((n_mla, D, MLA_Q_RANK + MLA_KV_RANK + MLA_ROPE), D ** -0.5),
        'mla_q_norm': 1.0 + nrm((n_mla, MLA_Q_RANK), 0.05),
        'mla_w_uq': nrm((n_mla, MLA_Q_RANK, MLA_HEADS * (MLA_NOPE + MLA_ROPE)), MLA_Q_RANK ** -0.5),
        'mla_kv_norm': 1.0 + nrm((n_mla, MLA_KV_RANK), 0.05),
        'mla_w_ukv': nrm((n_mla, MLA_KV_RANK, MLA_HEADS * (MLA_NOPE + MLA_V)), MLA_KV_RANK ** -0.5),
        'mla_w_out': nrm((n_mla, MLA_HEADS * MLA_V, D), (MLA_HEADS * MLA_V) ** -0.5),
        'rwkv_mu': uni((n_rwkv, 6, D), 0.0, 1.0),
        'rwkv_w_rkv': nrm((n_rwkv, 3, D, D), D ** -0.5),
        'rwkv_w0': uni((n_rwkv, D), -6.5, -1.5),
        'rwkv_wd1': nrm((n_rwkv, D, RWKV_DECAY_LORA), D ** -0.5),
        'rwkv_wd2': nrm((n_rwkv, RWKV_DECAY_LORA, D), 0.5 * RWKV_DECAY_LORA ** -0.5),
        'rwkv_a0': nrm((n_rwkv, D), 0.1),
        'rwkv_wa1': nrm((n_rwkv, D, RWKV_A_LORA), D ** -0.5),
        'rwkv_wa2': nrm((n_rwkv, RWKV_A_LORA, D), RWKV_A_LORA ** -0.5),
        'rwkv_wg1': nrm((n_rwkv, D, RWKV_GATE_LORA), D ** -0.5),
        'rwkv_wg2': nrm((n_rwkv, RWKV_GATE_LORA, D), RWKV_GATE_LORA ** -0.5),
        'rwkv_k_k': 0.85 + nrm((n_rwkv, D), 0.05),
        'rwkv_k_a': 1.0 + nrm((n_rwkv, D), 0.05),
        'rwkv_r_k': nrm((n_rwkv, RWKV_HEADS, RWKV_HEAD), 0.1),
        'rwkv_gn_w': 1.0 + nrm((n_rwkv, D), 0.05),
        'rwkv_gn_b': nrm((n_rwkv, D), 0.02),
        'rwkv_w_out': nrm((n_rwkv, D, D), D ** -0.5),
        'moba_w_in': nrm((n_moba, D, 3 * D), D ** -0.5),
        'moba_w_out': nrm((n_moba, D, D), D ** -0.5),
        'ret_w_in': nrm((n_ret, D, 6 * D), D ** -0.5),
        'ret_gn_w': 1.0 + nrm((n_ret, 2 * D), 0.05),
        'ret_gn_b': nrm((n_ret, 2 * D), 0.02),
        'ret_w_out': nrm((n_ret, 2 * D, D), (2 * D) ** -0.5),
    }

def first_block(x, c, ada_w, ada_b, norm_g, ffn_w_in, ffn_w_out, final_g, rel_table,
              mla_w_in, mla_q_norm, mla_w_uq, mla_kv_norm, mla_w_ukv, mla_w_out,
              rwkv_mu, rwkv_w_rkv, rwkv_w0, rwkv_wd1, rwkv_wd2, rwkv_a0, rwkv_wa1, rwkv_wa2,
              rwkv_wg1, rwkv_wg2, rwkv_k_k, rwkv_k_a, rwkv_r_k, rwkv_gn_w, rwkv_gn_b, rwkv_w_out,
              moba_w_in, moba_w_out, ret_w_in, ret_gn_w, ret_gn_b, ret_w_out):
    B = x.shape[0]
    c_act = jax.nn.silu(c)
    for i in range(DEPTH):
        mods = (c_act @ ada_w[i] + ada_b[i]).reshape(B, 3, 3, D_MODEL)
        h = _modulate(x, norm_g[i, 0], mods[:, 0, 0], mods[:, 0, 1])
        x = x + MACARON_W * mods[:, 0, 2][:, None, :] * _swiglu(h, ffn_w_in[i, 0], ffn_w_out[i, 0])
        h = _modulate(x, norm_g[i, 1], mods[:, 1, 0], mods[:, 1, 1])
        kind, j = i % N_MIXERS, i // N_MIXERS
        if kind == 0:
            y = _mla_mixer(h, mla_w_in[j], mla_q_norm[j], mla_w_uq[j], mla_kv_norm[j], mla_w_ukv[j], mla_w_out[j])
        elif kind == 1:
            y = _rwkv7_mixer(h, rwkv_mu[j], rwkv_w_rkv[j], rwkv_w0[j], rwkv_wd1[j], rwkv_wd2[j], rwkv_a0[j],
                             rwkv_wa1[j], rwkv_wa2[j], rwkv_wg1[j], rwkv_wg2[j], rwkv_k_k[j], rwkv_k_a[j],
                             rwkv_r_k[j], rwkv_gn_w[j], rwkv_gn_b[j], rwkv_w_out[j])
        elif kind == 2:
            y = _moba_mixer(h, moba_w_in[j], rel_table, moba_w_out[j])
        else:
            y = _retnet_mixer(h, ret_w_in[j], ret_gn_w[j], ret_gn_b[j], ret_w_out[j])
        x = x + mods[:, 1, 2][:, None, :] * y
        h = _modulate(x, norm_g[i, 2], mods[:, 2, 0], mods[:, 2, 1])
        x = x + MACARON_W * mods[:, 2, 2][:, None, :] * _swiglu(h, ffn_w_in[i, 1], ffn_w_out[i, 1])
    return _rmsnorm(x, final_g)


DEEPNORM_ALPHA = (2.0 * DEPTH) ** 0.25
DEEPNORM_BETA = (8.0 * DEPTH) ** -0.25
LN_EPS = 1e-5

N_ATTN_HEADS = 8
REL_MAX_DIST_2 = 2048

A_HEADS = 8
A_HEAD_DIM = D_MODEL // 16
A_WIDTH = A_HEADS * A_HEAD_DIM
A_PATTERNS = ((128, 1), (512, 4), (2048, 16))
A_BLOCK = 128

B_HEADS = 4
B_HEAD_DIM = D_MODEL // 8
B_WIDTH = B_HEADS * B_HEAD_DIM
B_CHUNK = 128
B_CONV = 4

AB_AQ = 0
AB_AK = AB_AQ + A_WIDTH
AB_AV = AB_AK + A_WIDTH
AB_BQ = AB_AV + A_WIDTH
AB_BK = AB_BQ + B_WIDTH
AB_BV = AB_BK + B_WIDTH
AB_BO = AB_BV + B_WIDTH
AB_BI = AB_BO + B_WIDTH
AB_BF = AB_BI + B_HEADS
AB_PROJ = AB_BF + B_HEADS
AB_MIX = A_WIDTH + B_WIDTH

C_HEADS = 8
C_GROUPS = 2
C_HPG = C_HEADS // C_GROUPS
C_HEAD_DIM = D_MODEL // 8
C_WIDTH = C_HEADS * C_HEAD_DIM
CMP_BLOCK = 32
CMP_STRIDE = 16
CMP_HIDDEN = 256
SLC_BLOCK = 64
SLC_TOP_N = 16
WIN = 512
C_QBLOCK = 64
C_OFF_KV = C_WIDTH
C_OFF_GATE = C_OFF_KV + 3 * 2 * C_GROUPS * C_HEAD_DIM
C_PROJ = C_OFF_GATE + 3 * C_HEADS

N_GROUPS = 4
EXPERTS_PER_GROUP = 4
N_EXPERTS = N_GROUPS * EXPERTS_PER_GROUP
EXPERT_HIDDEN = D_MODEL // 2
MOE_TOP_K = 2
MOE_CHUNK = 128


def layer_norm(x, g, b):
    xf = x.astype(jnp.float32)
    mu = xf.mean(-1, keepdims=True)
    var = jnp.square(xf - mu).mean(-1, keepdims=True)
    y = (xf - mu) * lax.rsqrt(var + LN_EPS) * g.astype(jnp.float32) + b.astype(jnp.float32)
    return y.astype(x.dtype)

def _t5_bucket_2(dist):
    n = jnp.maximum(dist, 0)
    exact = REL_BUCKETS // 2
    nf = jnp.maximum(n, 1).astype(jnp.float32)
    large = exact + (jnp.log(nf / exact) / math.log(REL_MAX_DIST_2 / exact)
                     * (REL_BUCKETS - exact)).astype(jnp.int32)
    return jnp.where(n < exact, n, jnp.minimum(large, REL_BUCKETS - 1))

def _t5_bias(table, dist):
    return table.astype(jnp.float32)[_t5_bucket_2(dist)]

def masked_softmax(logits, valid):
    masked = jnp.where(valid, logits.astype(jnp.float32), -jnp.inf)
    m = jnp.max(masked, axis=-1, keepdims=True)
    m = jnp.where(jnp.isfinite(m), m, 0.0)
    p = jnp.exp(masked - m)
    s = p.sum(-1, keepdims=True)
    return p / jnp.maximum(s, 1e-30)

def causal_conv(x, w):
    K, C = w.shape
    return lax.conv_general_dilated(x, w[:, None, :].astype(x.dtype), window_strides=(1,),
                                    padding=[(K - 1, 0)],
                                    dimension_numbers=('NWC', 'WIO', 'NWC'),
                                    feature_group_count=C)

def _dilated_branch(q, k, v, rel_bias, window, dilation):
    Bn, S, H, E = q.shape
    nk = window // dilation
    L = -(-S // dilation)
    nb = -(-L // A_BLOCK)
    Lp = nb * A_BLOCK
    pad = Lp * dilation - S

    def to_res(t):
        t = jnp.pad(t, ((0, 0), (0, pad), (0, 0), (0, 0)))
        t = t.reshape(Bn, Lp, dilation, H, E).transpose(0, 2, 1, 3, 4)
        return t.reshape(Bn, dilation, nb, A_BLOCK, H, E)

    def with_prev(t):
        prev = jnp.pad(t, ((0, 0), (0, 0), (1, 0), (0, 0), (0, 0), (0, 0)))[:, :, :-1]
        return jnp.concatenate([prev, t], axis=3)

    qb = to_res(q)
    kk = with_prev(to_res(k))
    vv = with_prev(to_res(v))
    logits = jnp.einsum('brnqhe,brnkhe->brnhqk', qb, kk).astype(jnp.float32) * (E ** -0.5)
    qi = jnp.arange(A_BLOCK)[:, None]
    ki = jnp.arange(2 * A_BLOCK)[None, :]
    j = qi + A_BLOCK - ki
    valid = (j >= 0) & (j <= nk)
    bias = _t5_bias(rel_bias, jnp.maximum(j, 0) * dilation).transpose(2, 0, 1)
    first = (jnp.arange(nb)[:, None, None] > 0) | (ki[None] >= A_BLOCK)
    valid = valid[None] & first
    logits = jnp.where(valid[None, None, :, None], logits + bias, -jnp.inf)
    m = logits.max(-1, keepdims=True)
    p = jnp.exp(logits - m)
    s = p.sum(-1)
    o = jnp.einsum('brnhqk,brnkhe->brnhqe', p, vv.astype(jnp.float32)) / s[..., None]
    lse = m[..., 0] + jnp.log(s)
    o = o.transpose(0, 2, 4, 1, 3, 5).reshape(Bn, Lp * dilation, H, E)[:, :S]
    lse = lse.transpose(0, 2, 4, 1, 3).reshape(Bn, Lp * dilation, H)[:, :S]
    return o, lse

def dilated_attention(q, k, v, rel_bias):
    outs, lses = [], []
    for window, dilation in A_PATTERNS:
        o, lse = _dilated_branch(q, k, v, rel_bias, window, dilation)
        outs.append(o)
        lses.append(lse)
    wts = jax.nn.softmax(jnp.stack(lses, 0), axis=0)
    return jnp.einsum('pbsh,pbshe->bshe', wts, jnp.stack(outs, 0))

def mlstm(q, k, v, i_pre, f_pre):
    f32 = jnp.float32
    Bn, S, H, dk = q.shape
    dv = v.shape[-1]
    L = B_CHUNK
    nc = S // L

    def chunks(t):
        t = t.astype(f32).reshape((Bn, nc, L) + t.shape[2:])
        return t.transpose((1, 0, 3, 2) + tuple(range(4, t.ndim)))

    qc = chunks(q) * (dk ** -0.5)
    kc, vc = chunks(k), chunks(v)
    ic = chunks(i_pre)
    fc = chunks(jax.nn.log_sigmoid(f_pre.astype(f32)))
    tri = jnp.tril(jnp.ones((L, L), bool))

    def step(carry, inp):
        C, n, m = carry
        qt, kt, vt, it, ft = inp
        b = jnp.cumsum(ft, axis=-1)
        Dm = jnp.where(tri, b[..., :, None] - b[..., None, :] + it[..., None, :], -jnp.inf)
        inter = b + m[..., None]
        m_t = jnp.maximum(inter, Dm.max(-1))
        P = jnp.exp(Dm - m_t[..., None])
        Sqk = jnp.einsum('bhtd,bhsd->bhts', qt, kt) * P
        sc = jnp.exp(inter - m_t)
        num = sc[..., None] * jnp.einsum('bhtd,bhdv->bhtv', qt, C) + jnp.einsum('bhts,bhsv->bhtv', Sqk, vt)
        den = sc * jnp.einsum('bhtd,bhd->bht', qt, n) + Sqk.sum(-1)
        h = num / jnp.maximum(jnp.abs(den), jnp.exp(-m_t))[..., None]
        bL = b[..., -1]
        g = bL[..., None] - b + it
        m_new = jnp.maximum(bL + m, g.max(-1))
        wk = jnp.exp(g - m_new[..., None])
        decay = jnp.exp(bL + m - m_new)
        C_new = decay[..., None, None] * C + jnp.einsum('bhs,bhsd,bhsv->bhdv', wk, kt, vt)
        n_new = decay[..., None] * n + jnp.einsum('bhs,bhsd->bhd', wk, kt)
        return (C_new, n_new, m_new), h

    init = (jnp.zeros((Bn, H, dk, dv), f32), jnp.zeros((Bn, H, dk), f32), jnp.zeros((Bn, H), f32))
    _, hs = lax.scan(step, init, (qc, kc, vc, ic, fc))
    return hs.transpose(1, 0, 3, 2, 4).reshape(Bn, S, H, dv)

def head_norm(h, g):
    mu = h.mean(-1, keepdims=True)
    var = jnp.square(h - mu).mean(-1, keepdims=True)
    y = (h - mu) * lax.rsqrt(var + LN_EPS)
    return y.reshape(h.shape[0], h.shape[1], -1) * g.astype(jnp.float32)

def mixer_ab(x, w_in, gate_b, conv_w, head_g, w_out, rel_bias):
    Bn, S, _ = x.shape
    p = jnp.einsum('bsd,de->bse', x, w_in)
    aq = p[..., AB_AQ:AB_AK].reshape(Bn, S, A_HEADS, A_HEAD_DIM)
    ak = p[..., AB_AK:AB_AV].reshape(Bn, S, A_HEADS, A_HEAD_DIM)
    av = p[..., AB_AV:AB_BQ].reshape(Bn, S, A_HEADS, A_HEAD_DIM)
    qk = jax.nn.silu(causal_conv(p[..., AB_BQ:AB_BV], conv_w))
    bq = qk[..., :B_WIDTH].reshape(Bn, S, B_HEADS, B_HEAD_DIM)
    bk = qk[..., B_WIDTH:].reshape(Bn, S, B_HEADS, B_HEAD_DIM)
    bv = p[..., AB_BV:AB_BO].reshape(Bn, S, B_HEADS, B_HEAD_DIM)
    bo = p[..., AB_BO:AB_BI]
    bi = p[..., AB_BI:AB_BF] + gate_b[:B_HEADS]
    bf = p[..., AB_BF:AB_PROJ] + gate_b[B_HEADS:]
    ya = dilated_attention(aq, ak, av, rel_bias).reshape(Bn, S, A_WIDTH)
    yb = jax.nn.sigmoid(bo.astype(jnp.float32)) * head_norm(mlstm(bq, bk, bv, bi, bf), head_g)
    y = jnp.concatenate([ya.astype(x.dtype), yb.astype(x.dtype)], axis=-1)
    return jnp.einsum('bse,ed->bsd', y, w_out)

def mixer_c(x, w_in, gate_b, cmp_pos, cmp_w1, cmp_w2, w_out, rel_bias):
    f32 = jnp.float32
    Bn, S, _ = x.shape
    G, J, E = C_GROUPS, C_HPG, C_HEAD_DIM
    p = jnp.einsum('bsd,de->bse', x, w_in)
    q = p[..., :C_OFF_KV].reshape(Bn, S, G, J, E).transpose(0, 2, 3, 1, 4).astype(f32) * (E ** -0.5)
    kv = p[..., C_OFF_KV:C_OFF_GATE].reshape(Bn, S, 3, 2, G, E).astype(f32)
    gates = jax.nn.sigmoid((p[..., C_OFF_GATE:] + gate_b).astype(f32)).reshape(Bn, S, 3, G, J)

    n_cmp = (S - CMP_BLOCK) // CMP_STRIDE + 1
    cidx = jnp.arange(n_cmp)[:, None] * CMP_STRIDE + jnp.arange(CMP_BLOCK)[None, :]
    cmp_start, cmp_end = cidx[:, 0], cidx[:, -1]

    def compress(t, pos, w1, w2):
        blocks = t[:, cidx] + pos[None, None, :, None, :]
        flat = blocks.transpose(0, 3, 1, 2, 4).reshape(Bn, G, n_cmp, CMP_BLOCK * E)
        return (jax.nn.gelu(flat @ w1) @ w2).astype(f32)

    k_cmp = compress(kv[:, :, 0, 0], cmp_pos[0], cmp_w1[0], cmp_w2[0])
    v_cmp = compress(kv[:, :, 0, 1], cmp_pos[1], cmp_w1[1], cmp_w2[1])

    n_slc = S // SLC_BLOCK
    top_n = min(SLC_TOP_N, n_slc)
    slc_start = jnp.arange(n_slc) * SLC_BLOCK

    def blocks_of(t):
        return t.transpose(0, 2, 1, 3).reshape(Bn, G, n_slc, SLC_BLOCK * E)

    k_sb, v_sb = blocks_of(kv[:, :, 1, 0]), blocks_of(kv[:, :, 1, 1])
    overlap = ((cmp_start[:, None] < slc_start[None, :] + SLC_BLOCK)
               & (cmp_end[:, None] >= slc_start[None, :])).astype(f32)

    def pad_win(t):
        return jnp.pad(t.transpose(0, 2, 1, 3), ((0, 0), (0, 0), (WIN, 0), (0, 0)))

    k_w, v_w = pad_win(kv[:, :, 2, 0]), pad_win(kv[:, :, 2, 1])

    tb = rel_bias.astype(f32).reshape(REL_BUCKETS, G, J)
    tb_g = tb.transpose(1, 0, 2)
    gsel = jnp.arange(G)[None, :, None, None]

    def grouped_bias(dist2d):
        return tb[_t5_bucket_2(dist2d)].transpose(2, 3, 0, 1)

    def block(blk):
        s0 = blk * C_QBLOCK
        qpos = s0 + jnp.arange(C_QBLOCK)
        qb = lax.dynamic_slice_in_dim(q, s0, C_QBLOCK, axis=3)
        dist_c = qpos[:, None] - cmp_end[None, :]
        lc = jnp.einsum('bgjqe,bgne->bgjqn', qb, k_cmp) + grouped_bias(dist_c)
        p_c = masked_softmax(lc, dist_c >= 0)
        o_c = jnp.einsum('bgjqn,bgne->bgjqe', p_c, v_cmp)
        imp = jnp.einsum('bgjqn,nm->bgqm', p_c, overlap)
        mblk = jnp.arange(n_slc)[None, :]
        qblk = (qpos // SLC_BLOCK)[:, None]
        forced = (mblk == 0) | (mblk == qblk) | (mblk == qblk - 1)
        score = jnp.where(forced, jnp.inf,
                          jnp.where(slc_start[None, :] <= qpos[:, None], imp, -jnp.inf))
        _, sel = lax.top_k(score, top_n)
        flat_sel = sel.reshape(Bn, G, C_QBLOCK * top_n, 1)
        T = top_n * SLC_BLOCK
        ks = jnp.take_along_axis(k_sb, flat_sel, axis=2).reshape(Bn, G, C_QBLOCK, T, E)
        vs = jnp.take_along_axis(v_sb, flat_sel, axis=2).reshape(Bn, G, C_QBLOCK, T, E)
        kpos_s = (sel[..., None] * SLC_BLOCK + jnp.arange(SLC_BLOCK)).reshape(Bn, G, C_QBLOCK, T)
        dist_s = qpos[None, None, :, None] - kpos_s
        bias_s = jnp.moveaxis(tb_g[gsel, _t5_bucket_2(dist_s)], -1, 2)
        ls = jnp.einsum('bgjqe,bgqte->bgjqt', qb, ks) + bias_s
        p_s = masked_softmax(ls, (dist_s >= 0)[:, :, None])
        o_s = jnp.einsum('bgjqt,bgqte->bgjqe', p_s, vs)
        kw = lax.dynamic_slice_in_dim(k_w, s0, WIN + C_QBLOCK, axis=2)
        vw = lax.dynamic_slice_in_dim(v_w, s0, WIN + C_QBLOCK, axis=2)
        kpos_w = s0 - WIN + jnp.arange(WIN + C_QBLOCK)
        dist_w = qpos[:, None] - kpos_w[None, :]
        valid_w = (dist_w >= 0) & (dist_w < WIN) & (kpos_w[None, :] >= 0)
        lw = jnp.einsum('bgjqe,bgte->bgjqt', qb, kw) + grouped_bias(dist_w)
        p_w = masked_softmax(lw, valid_w)
        o_w = jnp.einsum('bgjqt,bgte->bgjqe', p_w, vw)
        g = lax.dynamic_slice_in_dim(gates, s0, C_QBLOCK, axis=1).transpose(2, 0, 3, 4, 1)
        return g[0][..., None] * o_c + g[1][..., None] * o_s + g[2][..., None] * o_w

    out = lax.map(block, jnp.arange(S // C_QBLOCK))
    out = out.transpose(1, 0, 4, 2, 3, 5).reshape(Bn, S, C_WIDTH)
    return jnp.einsum('bse,ed->bsd', out.astype(x.dtype), w_out)

def hier_moe(x, wr_g, br_g, wr_e, br_e, w_gate, w_up, w_down):
    f32 = jnp.float32
    Bn, S, D = x.shape
    xt = x.reshape(-1, D)
    g_logits = (xt @ wr_g + br_g).astype(f32)
    g_prob = jax.nn.softmax(g_logits, axis=-1)
    _, g_idx = lax.top_k(g_logits, 1)
    g_w = jnp.take_along_axis(g_prob, g_idx, axis=-1)[:, 0]
    e_all = (jnp.einsum('nd,gde->nge', xt, wr_e) + br_e).astype(f32)
    e_logits = jnp.take_along_axis(e_all, g_idx[:, :, None], axis=1)[:, 0]
    top_v, top_i = lax.top_k(e_logits, MOE_TOP_K)
    e_w = jax.nn.softmax(top_v, axis=-1) * g_w[:, None]
    expert_id = g_idx * EXPERTS_PER_GROUP + top_i
    gates = jnp.einsum('nk,nke->ne', e_w, jax.nn.one_hot(expert_id, N_EXPERTS, dtype=f32))
    wg = w_gate.transpose(1, 0, 2).reshape(D, N_EXPERTS * EXPERT_HIDDEN)
    wu = w_up.transpose(1, 0, 2).reshape(D, N_EXPERTS * EXPERT_HIDDEN)
    wd = w_down.reshape(N_EXPERTS * EXPERT_HIDDEN, D)

    def chunk_fn(args):
        xc, gc = args
        h = jax.nn.silu(xc @ wg) * (xc @ wu)
        h = (h.reshape(-1, N_EXPERTS, EXPERT_HIDDEN) * gc[..., None]).reshape(-1, N_EXPERTS * EXPERT_HIDDEN)
        return h @ wd

    out = lax.map(chunk_fn, (xt.reshape(-1, MOE_CHUNK, D), gates.reshape(-1, MOE_CHUNK, N_EXPERTS)))
    return out.reshape(Bn, S, D).astype(x.dtype)

def second_inputs(seed: int = 0) -> dict:
    key = jax.random.key(seed)
    ks = iter(jax.random.split(key, 32))

    def nrm(shape, scale):
        return jax.random.normal(next(ks), shape, jnp.float32) * scale

    n_even = (DEPTH + 1) // 2
    n_odd = DEPTH // 2
    D = D_MODEL
    ab_col = np.ones(AB_PROJ, np.float32)
    ab_col[AB_AV:AB_AV + A_WIDTH] = DEEPNORM_BETA
    ab_col[AB_BV:AB_BV + B_WIDTH] = DEEPNORM_BETA
    kv_col = np.ones((3, 2, C_GROUPS * C_HEAD_DIM), np.float32)
    kv_col[:, 1] = DEEPNORM_BETA
    c_col = np.concatenate([np.ones(C_WIDTH, np.float32), kv_col.ravel(), np.ones(3 * C_HEADS, np.float32)])
    return {
        "x": nrm((BATCH, SEQ, D), 1.0),
        "rel_bias": nrm((REL_BUCKETS, N_ATTN_HEADS), 0.2),
        "ln_g": 1.0 + nrm((DEPTH, 2, D), 0.02),
        "ln_b": nrm((DEPTH, 2, D), 0.02),
        "ab_w_in": nrm((n_even, D, AB_PROJ), D ** -0.5) * jnp.asarray(ab_col),
        "ab_gate_b": jnp.concatenate([nrm((n_even, B_HEADS), 0.1),
                                      3.0 + nrm((n_even, B_HEADS), 0.5)], axis=-1),
        "ab_conv": nrm((n_even, B_CONV, 2 * B_WIDTH), B_CONV ** -0.5),
        "ab_head_norm": 1.0 + nrm((n_even, B_WIDTH), 0.02),
        "ab_w_out": nrm((n_even, AB_MIX, D), AB_MIX ** -0.5 * DEEPNORM_BETA),
        "c_w_in": nrm((n_odd, D, C_PROJ), D ** -0.5) * jnp.asarray(c_col),
        "c_gate_b": nrm((n_odd, 3 * C_HEADS), 0.1),
        "c_cmp_pos": nrm((n_odd, 2, CMP_BLOCK, C_HEAD_DIM), 0.1),
        "c_cmp_w1": nrm((n_odd, 2, CMP_BLOCK * C_HEAD_DIM, CMP_HIDDEN), (CMP_BLOCK * C_HEAD_DIM) ** -0.5),
        "c_cmp_w2": nrm((n_odd, 2, CMP_HIDDEN, C_HEAD_DIM), CMP_HIDDEN ** -0.5),
        "c_w_out": nrm((n_odd, C_WIDTH, D), C_WIDTH ** -0.5 * DEEPNORM_BETA),
        "moe_wr_g": nrm((DEPTH, D, N_GROUPS), D ** -0.5),
        "moe_br_g": nrm((DEPTH, N_GROUPS), 0.01),
        "moe_wr_e": nrm((DEPTH, N_GROUPS, D, EXPERTS_PER_GROUP), D ** -0.5),
        "moe_br_e": nrm((DEPTH, N_GROUPS, EXPERTS_PER_GROUP), 0.01),
        "moe_w_gate": nrm((DEPTH, N_EXPERTS, D, EXPERT_HIDDEN), D ** -0.5),
        "moe_w_up": nrm((DEPTH, N_EXPERTS, D, EXPERT_HIDDEN), D ** -0.5),
        "moe_w_down": nrm((DEPTH, N_EXPERTS, EXPERT_HIDDEN, D), EXPERT_HIDDEN ** -0.5 * DEEPNORM_BETA),
    }

def second_block(x, rel_bias, ln_g, ln_b, ab_w_in, ab_gate_b, ab_conv, ab_head_norm, ab_w_out,
              c_w_in, c_gate_b, c_cmp_pos, c_cmp_w1, c_cmp_w2, c_w_out,
              moe_wr_g, moe_br_g, moe_wr_e, moe_br_e, moe_w_gate, moe_w_up, moe_w_down):
    h = x
    for layer in range(DEPTH):
        j = layer // 2
        if layer % 2 == 0:
            y = mixer_ab(h, ab_w_in[j], ab_gate_b[j], ab_conv[j], ab_head_norm[j], ab_w_out[j], rel_bias)
        else:
            y = mixer_c(h, c_w_in[j], c_gate_b[j], c_cmp_pos[j], c_cmp_w1[j], c_cmp_w2[j], c_w_out[j], rel_bias)
        h = layer_norm(DEEPNORM_ALPHA * h + y, ln_g[layer, 0], ln_b[layer, 0])
        y = hier_moe(h, moe_wr_g[layer], moe_br_g[layer], moe_wr_e[layer], moe_br_e[layer],
                     moe_w_gate[layer], moe_w_up[layer], moe_w_down[layer])
        h = layer_norm(DEEPNORM_ALPHA * h + y, ln_g[layer, 1], ln_b[layer, 1])
    return h


def setup_inputs(seed=0):
    out = dict(first_inputs(seed))
    for name, value in second_inputs(seed + 1).items():
        if name != "x":
            out[name + "_2"] = value
    return out


def reference(
    x, c, ada_w, ada_b, norm_g, ffn_w_in, ffn_w_out, final_g, rel_table, mla_w_in, mla_q_norm,
    mla_w_uq, mla_kv_norm, mla_w_ukv, mla_w_out, rwkv_mu, rwkv_w_rkv, rwkv_w0, rwkv_wd1,
    rwkv_wd2, rwkv_a0, rwkv_wa1, rwkv_wa2, rwkv_wg1, rwkv_wg2, rwkv_k_k, rwkv_k_a, rwkv_r_k,
    rwkv_gn_w, rwkv_gn_b, rwkv_w_out, moba_w_in, moba_w_out, ret_w_in, ret_gn_w, ret_gn_b,
    ret_w_out, rel_bias_2, ln_g_2, ln_b_2, ab_w_in_2, ab_gate_b_2, ab_conv_2, ab_head_norm_2,
    ab_w_out_2, c_w_in_2, c_gate_b_2, c_cmp_pos_2, c_cmp_w1_2, c_cmp_w2_2, c_w_out_2,
    moe_wr_g_2, moe_br_g_2, moe_wr_e_2, moe_br_e_2, moe_w_gate_2, moe_w_up_2, moe_w_down_2,
):
    x = first_block(
        x, c, ada_w, ada_b, norm_g, ffn_w_in, ffn_w_out, final_g, rel_table, mla_w_in,
        mla_q_norm, mla_w_uq, mla_kv_norm, mla_w_ukv, mla_w_out, rwkv_mu, rwkv_w_rkv, rwkv_w0,
        rwkv_wd1, rwkv_wd2, rwkv_a0, rwkv_wa1, rwkv_wa2, rwkv_wg1, rwkv_wg2, rwkv_k_k, rwkv_k_a,
        rwkv_r_k, rwkv_gn_w, rwkv_gn_b, rwkv_w_out, moba_w_in, moba_w_out, ret_w_in, ret_gn_w,
        ret_gn_b, ret_w_out,
    )
    return second_block(
        x, rel_bias_2, ln_g_2, ln_b_2, ab_w_in_2, ab_gate_b_2, ab_conv_2, ab_head_norm_2,
        ab_w_out_2, c_w_in_2, c_gate_b_2, c_cmp_pos_2, c_cmp_w1_2, c_cmp_w2_2, c_w_out_2,
        moe_wr_g_2, moe_br_g_2, moe_wr_e_2, moe_br_e_2, moe_w_gate_2, moe_w_up_2, moe_w_down_2,
    )


_drawn_inputs = setup_inputs


def setup_inputs(seed=0):
    import zlib

    import numpy as np

    out = dict(_drawn_inputs(seed))
    spreads = {}
    factors = {'mla_q_norm': 3.713,
     'rwkv_wd1': 3.268,
     'rwkv_wd2': 3.368,
     'rwkv_a0': 2.77,
     'rwkv_gn_b': 4.109,
     'rel_bias_2': 5.915,
     'ab_head_norm_2': 23.821,
     'c_gate_b_2': 8.0,
     'c_cmp_pos_2': 6.115,
     'moe_br_g_2': 8.0,
     'moe_br_e_2': 21.314}
    for name, (base, spread) in spreads.items():
        noise = np.random.default_rng([zlib.crc32(name.encode()), seed]).standard_normal(out[name].shape)
        drawn = base * np.exp(spread * noise) if base else spread * noise
        out[name] = jnp.asarray(drawn.astype(out[name].dtype))
    for name, factor in factors.items():
        out[name] = (out[name] * factor).astype(out[name].dtype)
    return out
```

```python
import math
from contextlib import ExitStack

import numpy as np

import concourse.bass as bass
from concourse import mybir

F32 = mybir.dt.float32
ALU = mybir.AluOpType
ACT = mybir.ActivationFunctionType
AX = mybir.AxisListType

P = 128
T = 256
D = 1024
KT = D // P
FF_TILES = 2816 // P
EXPERTS = 16
E_TILES = 512 // P
RING = 4
SLOT = 4096
NEG = -1.0e30
ALPHA = (2.0 * 2) ** 0.25
ATT = 384
NCMP = 15
STOP = None



def stream_plan():
    def swiglu(tag, n):
        return [(f"{tag}.{m}", 3072) for m in range(n)]

    def cols(tag, widths):
        return [(f"{tag}.{i}", 8 * w) for i, w in enumerate(widths)]

    p = cols("ada0", [512] * 18) + swiglu("ffn0", FF_TILES)
    p += [("mla_in.0", 4096), ("mla_in.1", 8 * 224), ("mla_uq.0", 2304), ("mla_uq.1", 2304), ("mla_ukv", 4096)]
    p += cols("mla_out", [512] * 2) + swiglu("ffn1", FF_TILES)
    p += cols("ada1", [512] * 18) + swiglu("ffn2", FF_TILES)
    p += [("rwkv_lora1", 8 * 288), ("rwkv_lora2", 4096)]
    p += cols("rwkv_r", [512] * 2) + cols("rwkv_k", [512] * 2) + cols("rwkv_v", [512] * 2)
    p += cols("rwkv_out", [512] * 2) + swiglu("ffn3", FF_TILES)
    p += cols("ab_in", [512] * 6) + [("ab_in.6", 8 * 512), ("ab_gates", 8 * 8)] + cols("ab_out", [512] * 2)
    p += [("router0", 160)] + swiglu("moe0", EXPERTS * E_TILES)
    p += cols("c_in", [512] * 5) + [("c_gates", 8 * 24)]
    p += [("cmp_w1.0", 4096), ("cmp_w1.1", 4096), ("cmp_w1.2", 4096), ("cmp_w1.3", 4096), ("cmp_w2", 512)]
    p += cols("c_out", [512] * 2)
    p += [("router1", 160)] + swiglu("moe1", EXPERTS * E_TILES)
    return p


STREAM = stream_plan()
INDEX = {name: i for i, (name, _) in enumerate(STREAM)}

CONST_PLAN = [("ident", P), ("flip", P), ("ones", P), ("rot", 32), ("causal", ATT), ("dilated", ATT),
              ("strict", P), ("incl", P), ("level", 7 * P), ("hsel", KT * 16), ("hselT", KT * P),
              ("dist", 512), ("cmpmask", 2 * NCMP), ("iota", 4), ("eps", 3)]
VEC_PLAN = [("c", 8), ("ada_b", 144), ("norm_g", 48), ("final_g", 8), ("q_norm", 3), ("kv_norm", 2), ("mu", 48),
            ("w0", 8), ("a0", 8), ("k_k", 8), ("k_a", 8), ("r_k", 8), ("gn_w", 8), ("gn_b", 8),
            ("ln_g", 32), ("ln_b", 32), ("conv", 32), ("head_norm", 4), ("cmp_pos", 64), ("rel_bias", 8),
            ("ab_gate_b", 8), ("c_gate_b", 24), ("moe_b", 40)]


def offsets(plan):
    out, at = {}, 0
    for name, n in plan:
        out[name] = (at, n)
        at += n
    return out, at


CONST, NCONST = offsets(CONST_PLAN)
CONST["cos"], CONST["sin"] = (CONST["hselT"][0], T), (CONST["hselT"][0] + T, T)
VEC, NVEC = offsets(VEC_PLAN)


def build(nc, stream, const_d, vec_d, x_d, out_d, bias_scratch):
    with ExitStack() as ctx:
        def sb(name, n):
            return ctx.enter_context(nc.sbuf_tensor(name, [P, n], F32))

        ring = [sb(f"ring{i}", SLOT) for i in range(RING)]
        const = sb("const", NCONST)
        vec = sb("vec", NVEC)
        xT = sb("xT", KT * T)
        hT = sb("hT", KT * T)
        mods = sb("mods", 144)
        cact = sb("cact", 8)
        gain = sb("gain", 8)
        gate = sb("gate", 8)
        small = sb("small", 512)
        zeros = sb("zeros", 512)
        WORK = 26880
        work = sb("work", WORK)
        PS = ctx.enter_context(nc.psum_tensor("PS", [P, 8, 512], F32))

        sems = {}

        def S(name):
            if name not in sems:
                sems[name] = ctx.enter_context(nc.semaphore(name))
            return sems[name]

        slot_full = [S(f"slot_full{i}") for i in range(RING)]
        slot_free = S("slot_free")

        def C(name, rows=P, lo=0):
            at, n = CONST[name]
            return const[lo:rows, at:at + n]

        def V(name, i=0, n=1, rows=P):
            at, _ = VEC[name]
            return vec[0:rows, at + i:at + i + n]

        def tiles(ap, n=T):
            return ap.rearrange("p (k t) -> p k t", t=n)

        x3, h3 = tiles(xT[:, :]), tiles(hT[:, :])
        ident = C("ident")
        ones = C("ones")

        def W(at, n, lo=0, hi=P):
            assert at + n <= WORK, (at, n)
            return work[lo:hi, at:at + n]

        U = KT * T

        def unit(i, n=U):
            return W(i * U, n)

        def bank(b, n=512, at=0, lo=0, hi=P):
            return PS[lo:hi, b, at:at + n]

        def out_tile(m):
            return bank(m // 2, T, (m % 2) * T)

        def piece(name):
            return ring[INDEX[name] % RING]

        def arrived(name):
            i = INDEX[name]
            return slot_full[i % RING], 16 * (i // RING + 1)

        class Line:

            def __init__(self, eng, chain):
                self.eng, self.chain, self.added, self.seen = eng, chain, {}, {}

            def done(self, ins, name=None):
                name = name or self.chain
                self.added[name] = self.added.get(name, 0) + 1
                ins.then_inc(S(name), 1)
                self.eng.wait_ge(S(name), self.added[name])

            def next(self, name, k=1):
                self.seen[name] = self.seen.get(name, 0) + k
                self.eng.wait_ge(S(name), self.seen[name])

        mla_items = [dict(h=h, kind="full", first=True, last=True) for h in range(16)]
        ab_items = [dict(h=h, kind="full", first=True, last=True) for h in range(8)]
        c_items = [dict(h=h, kind=k, first=(b == 0), last=(b == 2), branch=b)
                   for h in range(8) for b, k in enumerate(("cmp", "full", "full"))]

        RW_LORA = 9 * U
        RL_AT = ({"AK": 0, "RK": 1024, "X": 2 * U, "XT": 2 * U + 512, "Y": 2 * U + 1024, "MTL": 2 * U + 1536},
                 {"AK": 3 * U, "RK": 3 * U + 1024, "X": 8 * U, "XT": 8 * U + 512, "Y": 8 * U + 1024,
                  "MTL": 8 * U + 1536})
        RB = ({"y": 4, "z": 5, "zt": 6}, {"y": 7, "z": 2, "zt": 3})

        def RL(lane, name):
            return W(RL_AT[lane][name], 1024 if name in ("AK", "RK") else 512)

        M_LAT, M_KR, M_Q, M_K, M_V, M_O, M_TMP, M_ATT = 0, 1280, 1536, 5632, 9728, 11776, 13824, 17920
        A_Q, A_K, A_V, A_BQ, A_BK, A_BV, A_BO, A_RAW, A_BM, A_Y = (
            0, 1024, 2048, 3072, 4096, 5120, 6144, 7168, 9248, 12320)
        A_LS, A_ATT = 14368, 25000
        C_Q, C_KV, C_BM, C_BC, C_CMPB, C_HID, C_KC, C_VC, C_G, C_O = (
            0, 2048, 5120, 8192, 8448, 14400, 10432, 10464, 10720, 10784)
        C_SRC = 4096
        C_ATT = 12832
        R_AT, R_GT, R_PICK = 8192, 9216, 10240
        ATT_SIZE = 2 * ATT + 2 * ATT + 16

        def att_place(items, base, o_banks=(4, 5)):
            def s(i):
                return W(base + (i % 2) * ATT, ATT)

            def pt(i):
                return W(base + 2 * ATT + (i % 2) * ATT, ATT)

            def stat(i, k):
                return W(base + 4 * ATT + (i % 2) * 8 + 2 * k, 2)
            return s, pt, stat

        def operands(phase, it):
            h = it["h"]
            if phase == "mla":
                q = tiles(W(M_Q, 16 * T, 0, 96))[:, h, :]
                k = tiles(W(M_K, 16 * T, 0, 96))[:, h, :]
                v = W(M_V, 2 * D).rearrange("p (s c) -> p s c", s=2)[:, :, h * 64:(h + 1) * 64]
                lo = 64 * (h % 2)
                o = tiles(W(M_O, U))[lo:lo + 64, h // 2, :]
                return q, k, v, o, lo, 64
            if phase == "ab":
                lo = 64 * (h % 2)
                q = tiles(W(A_Q, 4 * T))[lo:lo + 64, h // 2, :]
                k = tiles(W(A_K, 4 * T))[lo:lo + 64, h // 2, :]
                v = W(A_V, 2 * 512).rearrange("p (s c) -> p s c", s=2)[:, :, h * 64:(h + 1) * 64]
                o = tiles(W(A_Y, U))[lo:lo + 64, h // 2, :]
                return q, k, v, o, lo, 64
            g = h // 4
            q = tiles(W(C_Q, U))[:, h, :]
            o = tiles(W(C_O, U))[:, h, :]
            if it["kind"] == "cmp":
                k = W(C_KC, 2 * NCMP)[:, g * NCMP:(g + 1) * NCMP]
                v = W(C_VC, 2 * P, 0, NCMP).rearrange("p (g c) -> p g c", g=2)[:, g:g + 1, :]
                return q, k, v, o, 0, P
            b = it["branch"]
            k = tiles(W(C_KV + 512 * (b - 1), 2 * T))[:, g, :]
            v = W(C_KV + 1024 + 512 * (b - 1), 4 * P).rearrange("p (s c) -> p s c", s=2)[:, :, g * P:(g + 1) * P]
            return q, k, v, o, 0, P

        def score_bias(phase, it):
            if phase == "mla":
                return C("causal")
            if phase == "ab":
                return W(A_BM + ATT * it["h"], ATT)
            if it["kind"] == "cmp":
                return W(C_BC + 2 * NCMP * it["h"], 2 * NCMP)
            return W(C_BM + ATT * it["h"], ATT)

        SCALE = {"mla": 96 ** -0.5, "ab": 64 ** -0.5, "c": P ** -0.5}
        ITEMS = {"mla": mla_items, "ab": ab_items, "c": c_items}
        IT0 = {"mla": 0, "ab": 16, "c": 24}
        EV0 = {"mla": 0, "ab": 16, "c": 24}
        ABASE = {"mla": M_ATT, "ab": A_ATT, "c": C_ATT}
        SW = {"ffn0": (FF_TILES, 0), "ffn1": (FF_TILES, 22), "ffn2": (FF_TILES, 44), "ffn3": (FF_TILES, 66),
              "moe0": (64, 88), "moe1": (64, 152)}
        SW_SILU, SW_ACT, SW_G, SW_SQ, SW_TMP = 0, 512, 1024, 5120, 7168
        NSQ, NTMP = W(WORK - 2 * U, U), W(WORK - U, U)
        STD, RSTD = small[:, 0:T], small[:, T:2 * T]

        order = ["ffn0", "mla", "ffn1", "ffn2", "rwkv", "ffn3", "final", "ab", "moe0", "c", "moe1"]
        n_stop = len(order) if STOP is None else STOP

        XR = {ph: n for n, ph in enumerate(order[:n_stop])}
        XR["end"] = n_stop

        block = ctx.enter_context(nc.Block())

        @block.sync
        def _(sp):
            def load(i):
                w = STREAM[i][1]
                if i >= RING:
                    sp.wait_ge(slot_free, i - RING + 1)
                sp.dma_start(ring[i % RING][:, 0:w], stream[i, :, 0:w]).then_inc(slot_full[i % RING], 16)

            def load_run(first, n):
                w = STREAM[first][1]
                head = max(0, RING - first)
                for i in range(first, first + head):
                    load(i)
                first, n = first + head, n - head
                rounds = n // RING
                if rounds:
                    with sp.Fori(0, rounds) as r:
                        for j in range(RING):
                            i = first + j
                            sp.wait_ge(slot_free, r * RING + (i - RING + 1))
                            sp.dma_start(ring[i % RING][:, 0:w],
                                         stream[bass.ds(r * RING + i, 1), :, 0:w].rearrange("a p n -> (a p) n")
                                         ).then_inc(slot_full[i % RING], 16)
                for i in range(first + rounds * RING, first + n):
                    load(i)

            last_tag = None
            end = len(STREAM)
            if n_stop < len(order):
                tags = {"ffn0": "mla_in", "mla": "ffn1", "ffn1": "ada1", "ffn2": "rwkv_lora1", "rwkv": "ffn3",
                        "ffn3": "ab_in", "final": "ab_in", "ab": "router0", "moe0": "c_in", "c": "router1"}
                tag = tags[order[n_stop - 1]]
                end = next(i for i, (n, _) in enumerate(STREAM) if n.split(".")[0] == tag)
            i = 0
            while i < end:
                tag = STREAM[i][0].split(".")[0]
                n = 1
                while i + n < end and STREAM[i + n][0].split(".")[0] == tag and STREAM[i + n][1] == STREAM[i][1]:
                    n += 1
                if n >= 2 * RING:
                    load_run(i, n)
                else:
                    for j in range(i, i + n):
                        load(j)
                i += n
            sp.wait_ge(S("x_ready"), XR["end"])
            sp.dma_start(out_d[:, :], xT[:, :]).then_inc(S("out_stored"), 16)
            sp.wait_ge(S("out_stored"), 16)

        def piece_cols(name, k, lo, n, width=512):
            return piece(name)[:, k * width + lo:k * width + lo + n]

        @block.tensor
        def _(pe):
            mm = nc.tensor.matmul
            line = Line(pe, "pe_chain")

            def take(name):
                sem, value = arrived(name)
                pe.wait_ge(sem, value)

            def sums(parts, at=0, name="ss_ready"):
                for i, ap in enumerate(parts):
                    last = mm(bank(7, T, at), ones, ap, start=(i == 0), stop=(i == len(parts) - 1))
                last.then_inc(S(name), 1)

            def norm_sums():
                line.next("sq_ready")
                sq = tiles(NSQ)
                sums([sq[:, k, :] for k in range(KT)])

            def layer_norm_sums():
                line.next("pre_ready")
                sums([x3[:, k, :] for k in range(KT)], name="mean_ready")
                line.next("sq_ready")
                sq = tiles(NSQ)
                sums([sq[:, k, :] for k in range(KT)])

            def ada(layer):
                first = INDEX[f"ada{layer}.0"]
                base = 18 * layer

                def one(j, wait_full, wait_ps):
                    s = (first + j) % RING
                    pe.wait_ge(slot_full[s], wait_full)
                    if wait_ps is not None:
                        pe.wait_ge(S("ada_read"), wait_ps)
                    for m in range(4):
                        for k in range(KT):
                            last = mm(bank(s, 4)[:, m:m + 1], ring[s][:, k * 512 + m * P:k * 512 + (m + 1) * P],
                                      cact[:, k:k + 1], start=(k == 0), stop=(k == KT - 1))
                    last.then_inc(slot_free, 1)

                rounds = 4
                for j in range(RING):
                    i = first + j
                    one(j, 16 * (i // RING + 1), base + j - 3 if base + j >= 4 else None)
                with pe.Fori(1, rounds) as r:
                    for j in range(RING):
                        i = first + j
                        one(j, r * 16 + 16 * (i // RING + 1), r * RING + (base + j - 3))
                for j in range(rounds * RING, 18):
                    i = first + j
                    one(j, 16 * (i // RING + 1), base + j - 3)

            def swiglu(tag):
                n, base = SW[tag]
                first = INDEX[f"{tag}.0"]
                rhs = x3 if tag.startswith("moe") else h3
                zero = zeros[0:1, 0:512]

                def up(s, b, wait_full):
                    pe.wait_ge(slot_full[s], wait_full)
                    for half in range(2):
                        for k in range(KT):
                            last = mm(bank(b, T, half * T), ring[s][:, k * 256 + half * P:k * 256 + half * P + P],
                                      rhs[:, k, :], start=(k == 0), stop=(k == KT - 1))
                    last.then_inc(S("gu_ready"), 1)

                def down(s, parity, wait_act):
                    pe.wait_ge(S("hid_ready"), wait_act)
                    a = W(SW_ACT + parity * T, T)
                    for m in range(KT):
                        last = mm(out_tile(m), ring[s][:, 2048 + m * P:2048 + (m + 1) * P], a,
                                  start=False, stop=False, skip_group_check=True)
                    last.then_inc(slot_free, 1)

                for b in range(4):
                    mm(bank(b), zeros[0:1, 0:P], zero, start=True, stop=False, skip_group_check=True)

                def full_at(i):
                    return 16 * (i // RING + 1)

                def bnk(m):
                    return 4 + m % 4
                up(first % RING, bnk(0), full_at(first))
                for j in range(1, RING):
                    up((first + j) % RING, bnk(j), full_at(first + j))
                    down((first + j - 1) % RING, (j - 1) % 2, base + j)
                rounds = n // RING
                with pe.Fori(1, rounds) as r:
                    for j in range(RING):
                        up((first + j) % RING, bnk(j), r * 16 + full_at(first + j))
                        down((first + j - 1) % RING, (j - 1) % 2, r * RING + (base + j))
                for j in range(rounds * RING, n):
                    up((first + j) % RING, bnk(j), full_at(first + j))
                    down((first + j - 1) % RING, (j - 1) % 2, base + j)
                down((first + n - 1) % RING, (n - 1) % 2, base + n)

            def project(name, i0, rhs, mtiles, width=512, lo=0, rows=P, free=True):
                for j, m in enumerate(mtiles):
                    for k in range(KT):
                        last = mm(bank(m // 2, T, (m % 2) * T, 0, rows), piece_cols(name, k, lo + j * P, rows, width),
                                  rhs[:, k, :], start=(k == 0), stop=(k == KT - 1))
                if free:
                    last.then_inc(slot_free, 1)
                return last

            def out_proj(tag, src):
                for i in range(2):
                    take(f"{tag}.{i}")
                    project(f"{tag}.{i}", i, src, range(4 * i, 4 * i + 4))

            def attention(phase):
                items, base, ev0 = ITEMS[phase], IT0[phase], EV0[phase]
                s_of, pt_of, _ = att_place(items, ABASE[phase])
                n = len(items)

                def scores(i):
                    q, k, v, o, lo, dv = operands(phase, items[i])
                    b = i % 2
                    if items[i]["kind"] == "cmp":
                        for tt in range(2):
                            last = mm(bank(b, NCMP, tt * NCMP), q[:, tt * P:(tt + 1) * P], k, start=True, stop=True)
                    else:
                        mm(bank(b, P), q[:, 0:P], k[:, 0:P], start=True, stop=True)
                        last = mm(bank(b, T, P), q[:, P:T], k, start=True, stop=True)
                    last.then_inc(S("score_ready"), 1)

                def turn(i):
                    pe.wait_ge(S("prob_ready"), base + i + 1)
                    b, pr = 2 + i % 2, s_of(i)
                    if items[i]["kind"] == "cmp":
                        for tt in range(2):
                            last = nc.tensor.transpose(bank(b, P, tt * P, 0, NCMP), pr[:, tt * NCMP:(tt + 1) * NCMP],
                                                       ident)
                    else:
                        for c in range(3):
                            last = nc.tensor.transpose(bank(b, P, c * P), pr[:, c * P:(c + 1) * P], ident)
                    last.then_inc(S("turned"), 1)

                def values(i):
                    pe.wait_ge(S("pt_ready"), base + i + 1)
                    it = items[i]
                    q, k, v, o, lo, dv = operands(phase, it)
                    b = 4 + it["h"] % 2
                    if it["first"] and it["h"] >= 2:
                        pe.wait_ge(S("att_out"), ev0 + it["h"] - 1)
                    pt = pt_of(i)
                    if it["kind"] == "cmp":
                        last = mm(bank(b, T, 0, lo, lo + dv), v[:, 0, :], pt[0:NCMP, 0:T], start=it["first"],
                                  stop=it["last"])
                    else:
                        mm(bank(b, T, 0, lo, lo + dv), v[:, 0, :], pt[:, 0:T], start=it["first"], stop=False)
                        last = mm(bank(b, P, P, lo, lo + dv), v[:, 1, :], pt[:, T:T + P], start=False,
                                  stop=it["last"])
                    last.then_inc(S("pv_ready"), 1)

                for step in range(n + 2):
                    if step < n:
                        scores(step)
                    if 1 <= step <= n:
                        turn(step - 1)
                    if step >= 2:
                        values(step - 2)

            def mla():
                norm_sums()
                line.next("h_ready")
                take("mla_in.0")
                project("mla_in.0", 0, h3, range(0, 4))
                take("mla_in.1")
                project("mla_in.1", 0, h3, [4], width=224, free=False)
                last = project("mla_in.1", 0, h3, [5], width=224, lo=P, rows=96)
                lat = tiles(W(M_LAT, 5 * T))
                line.next("lat_sq_ready")
                sq = tiles(W(M_TMP, 5 * T))
                for i in range(3):
                    mm(bank(7, T), ones, sq[:, i, :], start=(i == 0), stop=(i == 2))
                for i in range(2):
                    last = mm(bank(7, T, T), ones, sq[:, 3 + i, :], start=(i == 0), stop=(i == 1))
                last.then_inc(S("ss_ready"), 1)
                line.next("lat_ready")
                for half in range(2):
                    name = f"mla_uq.{half}"
                    take(name)
                    for h in range(8):
                        for k in range(3):
                            last = mm(bank(4 * half + h // 2, T, (h % 2) * T, 0, 96),
                                      piece(name)[:, k * 768 + h * 96:k * 768 + (h + 1) * 96], lat[:, k, :],
                                      start=(k == 0), stop=(k == 2))
                    last.then_inc(slot_free, 1)
                take("mla_ukv")
                for half in range(2):
                    line.next("q_copied")
                    for h in range(8):
                        for k in range(2):
                            c = k * D + (8 * half + h) * 64
                            last = mm(bank(4 * half + h // 2, T, (h % 2) * T, 0, 64), piece("mla_ukv")[:, c:c + 64],
                                      lat[:, 3 + k, :], start=(k == 0), stop=(k == 1))
                    last.then_inc(S("k_ready"), 1)
                line.next("k_copied")
                for tt in range(2):
                    for c in range(2):
                        for k in range(2):
                            at = 2 * D + k * D + c * 512
                            last = mm(bank(2 * tt + c), lat[:, 3 + k, tt * P:(tt + 1) * P],
                                      piece("mla_ukv")[:, at:at + 512], start=(k == 0), stop=(k == 1))
                last.then_inc(slot_free, 1)
                line.next("k_copied")
                rot = const[64:96, CONST["rot"][0]:CONST["rot"][0] + 32]
                qr = W(M_Q, 16 * T, 64, 96)
                for g in range(4):
                    last = mm(bank(4 + g, 512, 0, 64, 96), rot, qr[:, g * 512:(g + 1) * 512], start=True, stop=True)
                last.then_inc(S("rot_ready"), 1)
                line.next("v_copied")
                for g in range(4):
                    last = mm(bank(g, 512, 0, 64, 96), rot, qr[:, (4 + g) * 512:(5 + g) * 512], start=True, stop=True)
                last.then_inc(S("rot_ready"), 1)
                line.next("rot_read")
                mm(bank(4, T, 0, 64, 96), rot, W(M_KR, T, 64, 96), start=True,
                   stop=True).then_inc(S("rot_ready"), 1)
                line.next("qk_ready")
                attention("mla")
                pe.wait_ge(S("att_out"), 16)
                out_proj("mla_out", tiles(W(M_O, U)))

            BODY = {}
            BODY["mla"] = mla
            def head_sums(src):
                sel = C("hsel").rearrange("p (k h) -> p k h", h=16)
                s3 = tiles(src)
                for k in range(KT):
                    last = mm(bank(7, T, 0, 0, 16), sel[:, k, :], s3[:, k, :], start=(k == 0), stop=(k == KT - 1))
                last.then_inc(S("hs_ready"), 1)

            def head_spread():
                line.next("hb_in")
                at = CONST["hselT"][0]
                for k in range(KT):
                    last = mm(out_tile(k), const[0:16, at + k * P:at + (k + 1) * P], small[0:16, T:2 * T],
                              start=True, stop=True)
                last.then_inc(S("hb_ready"), 1)

            def rwkv():
                norm_sums()
                line.next("h_ready")
                take("rwkv_lora1")
                w1 = piece("rwkv_lora1")
                xs = [tiles(unit(1)), tiles(unit(2))]

                def low(c0, n, b, x):
                    for k in range(KT):
                        last = mm(bank(b, T, 0, 0, n), w1[:, k * 288 + c0:k * 288 + c0 + n], x[:, k, :],
                                  start=(k == 0), stop=(k == KT - 1))
                    return last
                line.next("xs_ready")
                low(0, 64, 0, xs[0]).then_inc(S("xs_used"), 1)
                line.next("xs_ready")
                low(64, 64, 1, xs[1]).then_inc(S("xs_used"), 1)
                line.next("xs_ready")
                low(128, P, 2, xs[0])
                low(256, 32, 3, xs[0]).then_inc(slot_free, 1)
                take("rwkv_lora2")
                w2 = piece("rwkv_lora2")
                la = RW_LORA
                line.next("lora_act")
                for m in range(KT):
                    last = mm(out_tile(8 + m), w2[0:64, m * P:(m + 1) * P], W(la, T, 0, 64), start=True, stop=True)
                last.then_inc(S("lora2_ready"), 1)
                line.next("lora_act", 2)
                for m in range(KT):
                    last = mm(out_tile(m), w2[0:64, D + m * P:D + (m + 1) * P], W(la + T, T, 0, 64), start=True,
                              stop=True)
                last.then_inc(S("lora2_ready"), 1)
                line.next("proj_copied")
                for m in range(KT):
                    mm(out_tile(8 + m), w2[:, 2 * D + m * P:2 * D + (m + 1) * P], W(la + 2 * T, T), start=True,
                       stop=False)
                    last = mm(out_tile(8 + m), w2[0:32, 3 * D + m * P:3 * D + (m + 1) * P], W(la + 3 * T, T, 0, 32),
                              start=False, stop=True)
                last.then_inc(slot_free, 1)
                for n, (tag, b0) in enumerate((("rwkv_r", 0), ("rwkv_k", 8), ("rwkv_v", 0))):
                    line.next("proj_copied")
                    line.next("xs_ready")
                    for i in range(2):
                        take(f"{tag}.{i}")
                        project(f"{tag}.{i}", i, xs[(n + 1) % 2], range(b0 + 4 * i, b0 + 4 * i + 4))
                line.next("proj_copied", 2)
                line.next("hs_in")
                head_sums(unit(9))
                head_spread()
                line.next("hs_in_dve")
                head_sums(unit(9))
                head_spread()
                line.next("tilde_ready")
                for n, (u, tts, b0) in enumerate(((8, (0, 1), 4), (4, (0,), 0), (7, (0,), 2))):
                    src = tiles(unit(u))
                    for tt in tts:
                        for k in range(KT):
                            last = nc.tensor.transpose(bank(b0 + 2 * tt + k // 4, P, (k % 4) * P),
                                                       src[:, k, tt * P:(tt + 1) * P], ident)
                    last.then_inc(S("tok_ready"), 1)
                line.next("tok_copied", 3)
                til = {n: tiles(unit(u)) for n, u in (("a", 1), ("r", 6), ("b", 4), ("k", 7))}
                vtok = unit(9).rearrange("p (s c) -> p s c", s=2)
                btok, ktok, spad = W(10 * U, 1024), W(11 * U, 1024), W(10 * U + 1024, 1024)
                for tt in range(2):
                    ts = slice(tt * P, (tt + 1) * P)
                    for pair in range(2):
                        lanes = [(ln, 2 * pair + ln) for ln in range(2)]
                        if tt or pair:
                            line.next("yt_copied", 2)
                            if tt == 0 or pair == 0:
                                line.next("s_copied", 2)
                        for ln, q in lanes:
                            for j in range(4):
                                lo, k, h2 = 64 * (j % 2), 2 * q + j // 2, j // 2
                                for o, (l, r) in enumerate((("b", "a"), ("k", "a"), ("b", "r"), ("k", "r"))):
                                    last = mm(bank(4 * ln + 2 * (j % 2) + o // 2, P, (o % 2) * T + h2 * P),
                                              til[l][lo:lo + 64, k, ts], til[r][lo:lo + 64, k, ts], start=True,
                                              stop=True)
                            last.then_inc(S("pair_scores"), 1)
                        for ln, q in lanes:
                            line.next("xt_ready")
                            xt = RL(ln, "XT")
                            for c in range(4):
                                last = nc.tensor.transpose(bank(RB[ln]["y"], P, c * P), xt[:, c * P:(c + 1) * P], ident)
                            last.then_inc(S("x1_ready"), 1)
                        line.next("lvl_ready", 2)
                        for lvl in range(1, 7):
                            for ln, q in lanes:
                                line.next("lvl_ready")
                                line.next("x_copied" if lvl == 1 else "x_upd")
                                mt, x = RL(ln, "MTL"), RL(ln, "X")
                                for c in range(4):
                                    last = mm(bank(RB[ln]["y"], P, c * P), mt[:, c * P:(c + 1) * P],
                                              x[:, c * P:(c + 1) * P], start=True, stop=True)
                                last.then_inc(S("y_ready"), 1)
                            for ln, q in lanes:
                                line.next("y_copied")
                                y, xt = RL(ln, "Y"), RL(ln, "XT")
                                if lvl < 6:
                                    for c in range(4):
                                        mm(bank(RB[ln]["z"], P, c * P), xt[:, c * P:(c + 1) * P],
                                           y[:, c * P:(c + 1) * P], start=True, stop=True)
                                for c in range(4):
                                    last = mm(bank(RB[ln]["zt"], P, c * P), y[:, c * P:(c + 1) * P],
                                              xt[:, c * P:(c + 1) * P], start=True, stop=True)
                                last.then_inc(S("z_ready"), 1)
                        for ln, q in lanes:
                            for j in range(4):
                                h, k, c = 4 * q + j, 2 * q + j // 2, (j % 2) * 2 + j // 2
                                ka = RL(ln, "AK")[:, (j % 2) * 512 + T + (j // 2) * P:][:, 0:P]
                                last = mm(bank(ln, 64, c * 64), ka, vtok[:, tt, h * 64:(h + 1) * 64], start=True,
                                          stop=(tt == 0))
                                if tt:
                                    last = mm(bank(ln, 64, c * 64), til["a"][:, k, ts], spad[:, h * 64:(h + 1) * 64],
                                              start=False, stop=True)
                            last.then_inc(S("t1_ready"), 1)
                        for ln, q in lanes:
                            line.next("t1_copied")
                            line.next("x_upd")
                            xt, y = RL(ln, "XT"), RL(ln, "Y")
                            for c in range(4):
                                last = mm(bank(ln, 64, T + c * 64), xt[:, c * P:(c + 1) * P], y[:, c * 64:(c + 1) * 64],
                                          start=True, stop=True)
                            last.then_inc(S("u_ready"), 1)
                        for ln, q in lanes:
                            line.next("u_copied")
                            y = RL(ln, "Y")
                            for j in range(4):
                                if tt:
                                    break
                                h, k, c = 4 * q + j, 2 * q + j // 2, (j % 2) * 2 + j // 2
                                mm(bank(RB[ln]["zt"], 64, j * 64), btok[:, k * P:(k + 1) * P],
                                   y[:, T + c * 64:T + (c + 1) * 64], start=True, stop=False)
                                last = mm(bank(RB[ln]["zt"], 64, j * 64), ktok[:, k * P:(k + 1) * P],
                                          vtok[:, 0, h * 64:(h + 1) * 64], start=False, stop=True)
                            if tt == 0:
                                last.then_inc(S("s_ready"), 1)
                            for j in range(4):
                                h, k, c, lo = 4 * q + j, 2 * q + j // 2, (j % 2) * 2 + j // 2, 64 * (j % 2)
                                br = RL(ln, "RK")[:, (j % 2) * 512 + (j // 2) * P:][:, 0:P]
                                kr = RL(ln, "RK")[:, (j % 2) * 512 + T + (j // 2) * P:][:, 0:P]
                                o = bank(RB[ln]["z"], P, (j // 2) * P, lo, lo + 64)
                                mm(o, vtok[:, tt, h * 64:(h + 1) * 64], kr, start=True, stop=False)
                                if tt:
                                    mm(o, spad[:, h * 64:(h + 1) * 64], til["r"][:, k, ts], start=False, stop=False)
                                last = mm(o, y[:, T + c * 64:T + (c + 1) * 64], br, start=False, stop=True)
                            last.then_inc(S("yt_ready"), 1)
                line.next("yt_copied", 2)
                head_sums(unit(12))
                head_spread()
                line.next("hs_in")
                head_sums(unit(9))
                head_spread()
                line.next("mix_ready")
                out_proj("rwkv_out", tiles(unit(12)))

            BODY["rwkv"] = rwkv

            def row_bias(out, name, at, n):
                a = VEC[name][0] + at
                return mm(out, ones[0:1, :], vec[0:1, a:a + n], start=False, stop=True)

            def by_token(name, b0, lo, n, width=512, step=None, bias=None):
                for tt in range(2):
                    o = bank(b0 + tt, n) if step is None else bank(b0, n, tt * step)
                    for k in range(KT):
                        last = mm(o, x3[:, k, tt * P:(tt + 1) * P], piece_cols(name, k, lo, n, width),
                                  start=(k == 0), stop=(k == KT - 1 and bias is None))
                    if bias is not None:
                        last = row_bias(o, bias[0], bias[1], n)
                return last

            def flip_bias(at, landed):
                pe.wait_ge(S("bias_in"), landed)
                for b in range(6):
                    last = mm(bank(b), C("flip"), W(at + b * 512, 512), start=True, stop=True)
                last.then_inc(S("bias_flipped"), 1)
                line.next("bias_used")

            def ab():
                pe.wait_ge(S("x_ready"), XR["ab"])
                mm(bank(7, 512, 0, 0, 8), V("rel_bias", 0, 8, 32), C("dist", 32), start=True,
                   stop=True).then_inc(S("bias_ready"), 1)
                for i in range(7):
                    name = f"ab_in.{i}"
                    take(name)
                    if i == 3:
                        pe.wait_ge(S("bias_copied"), 1)
                    if i >= 4:
                        pe.wait_ge(S("ab_copied"), i - 3)
                    if i in (2, 5):
                        by_token(name, (2 * i) % 8, 0, 512).then_inc(slot_free, 1)
                    else:
                        project(name, i, x3, range((4 * i) % 16, (4 * i) % 16 + 4))
                take("ab_gates")
                pe.wait_ge(S("ab_copied"), 4)
                by_token("ab_gates", 6, 0, 8, 8, 8, ("ab_gate_b", 0)).then_inc(slot_free, 1)
                pe.wait_ge(S("ab_copied"), 7)
                flip_bias(A_BM, 32)
                attention("ab")
                def ls(at, n, hi=P):
                    return W(A_LS + at, n, 0, hi)
                line.next("lf_ready")
                lf = ls(16, 8)
                mm(bank(6, 8), C("incl"), lf, start=True, stop=True)
                mm(bank(6, 8, 8), ones, lf, start=True, stop=True).then_inc(S("cumsum_ready"), 1)
                line.next("diag_ready")
                dd = ls(256, 1024)
                for tt in range(2):
                    last = mm(bank(7 if tt else 2), ones, dd[:, tt * 512:(tt + 1) * 512], start=True, stop=True)
                last.then_inc(S("rowbc_ready"), 1)
                pe.wait_ge(S("bqk_ready"), 1)
                q, k = tiles(W(A_BQ, 1024)), tiles(W(A_BK, 1024))
                for tt in range(2):
                    for h in range(4):
                        last = mm(bank(tt, P, h * P), q[:, h, tt * P:(tt + 1) * P], k[:, h, tt * P:(tt + 1) * P],
                                  start=True, stop=True)
                last.then_inc(S("lqk_ready"), 1)
                for h in range(4):
                    last = nc.tensor.transpose(bank(3, P, h * P), k[:, h, 0:P], ident)
                last.then_inc(S("ktok_ready"), 1)
                line.next("lprob_ready")
                ss, st = ls(1280, 1024), ls(2304, 1024)
                for i in range(8):
                    last = nc.tensor.transpose(bank(4 + i // 4, P, (i % 4) * P), ss[:, i * P:(i + 1) * P], ident)
                last.then_inc(S("lturned"), 1)
                bv = W(A_BV, 1024).rearrange("p (s c) -> p s c", s=2)
                kw, cc, nn = ls(3328, 512), ls(3840, 512), ls(104, 4)
                line.next("kw_ready")
                for h in range(4):
                    mm(bank(7, P, h * P), kw[:, h * P:(h + 1) * P], bv[:, 0, h * P:(h + 1) * P], start=True, stop=True)
                for h in range(4):
                    last = mm(bank(6, 1, 16 + h), kw[:, h * P:(h + 1) * P], ones[:, 0:1], start=True, stop=True)
                last.then_inc(S("state_ready"), 1)
                line.next("lt_copied")
                for tt in range(2):
                    for h in range(4):
                        last = mm(bank(tt, P, h * P), st[:, (4 * tt + h) * P:(4 * tt + h + 1) * P],
                                  bv[:, tt, h * P:(h + 1) * P], start=True, stop=True)
                last.then_inc(S("lnum_ready"), 1)
                line.next("state_copied")
                for h in range(4):
                    mm(bank(2, P, h * P), q[:, h, P:T], cc[:, h * P:(h + 1) * P], start=True, stop=True)
                for h in range(4):
                    last = mm(bank(6, 1, 32 + h), q[:, h, P:T], nn[:, h:h + 1], start=True, stop=True)
                last.then_inc(S("linter_ready"), 1)
                line.next("lnormed")
                hh = ls(4352, 1024)
                for tt in range(2):
                    for h in range(4):
                        last = nc.tensor.transpose(bank(4 + h // 2, P, (h % 2) * T + tt * P),
                                                   hh[:, (4 * tt + h) * P:(4 * tt + h + 1) * P], ident)
                last.then_inc(S("lout_ready"), 1)
                line.next("mix_ready")
                pe.wait_ge(S("att_out"), 24)
                out_proj("ab_out", tiles(W(A_Y, U)))
                layer_norm_sums()

            def moe(l):
                def run():
                    ph = f"moe{l}"
                    pe.wait_ge(S("x_ready"), XR[ph])
                    take(f"router{l}")
                    by_token(f"router{l}", 7, 0, 20, 20, 20, ("moe_b", 20 * l)).then_inc(slot_free, 1)
                    line.next("gates_ready")
                    g = W(R_AT, 32)
                    for tt in range(2):
                        last = nc.tensor.transpose(bank(7, P, tt * P, 0, 16), g[:, tt * 16:(tt + 1) * 16], ident)
                    last.then_inc(S("gates_turned"), 1)
                    line.next("gates_copied")
                    line.next("pick_ready")
                    gt, pick = W(R_GT, T, 0, 16), tiles(W(R_PICK, 2048, 0, 16), P)
                    for half in range(2):
                        for e in range(8):
                            last = mm(out_tile(8 * half + e), pick[:, 8 * half + e, :], gt, start=True, stop=True)
                        last.then_inc(S("spread_ready"), 1)
                    line.next("g_copied", 2)
                    swiglu(ph)
                    layer_norm_sums()
                return run

            def c():
                pe.wait_ge(S("x_ready"), XR["c"])
                for i in range(5):
                    name = f"c_in.{i}"
                    take(name)
                    if i < 3:
                        project(name, i, x3, range(4 * i, 4 * i + 4))
                    else:
                        if i == 4:
                            pe.wait_ge(S("c_copied"), 1)
                        b = 6 if i == 3 else 0
                        project(name, i, x3, [2 * b, 2 * b + 1], free=False)
                        by_token(name, b + 1, T, T, 512, T).then_inc(slot_free, 1)
                take("c_gates")
                pe.wait_ge(S("c_copied"), 2)
                by_token("c_gates", 2, 0, 24, 24, 24, ("c_gate_b", 0)).then_inc(slot_free, 1)
                pe.wait_ge(S("c_copied"), 4)
                line.next("cmpb_ready")
                for kv in range(2):
                    b3 = W(C_CMPB + 960 * kv, 960).rearrange("p (i n) -> p i n", n=2 * NCMP)
                    for half in range(2):
                        name = f"cmp_w1.{2 * kv + half}"
                        take(name)
                        for i in range(16):
                            for m in range(2):
                                last = mm(bank(4 + 2 * kv + m, 2 * NCMP), piece(name)[:, i * T + m * P:i * T + (m + 1) * P],
                                          b3[:, 16 * half + i, :], start=(half == 0 and i == 0),
                                          stop=(half == 1 and i == 15))
                        last.then_inc(slot_free, 1)
                take("cmp_w2")
                w2 = piece("cmp_w2").rearrange("p (a n) -> p a n", n=P)
                line.next("hid_gelu")
                hid = W(C_HID, 120).rearrange("p (a n) -> p a n", n=2 * NCMP)
                for m in range(2):
                    mm(bank(3, 2 * NCMP), w2[:, m, :], hid[:, m, :], start=(m == 0), stop=(m == 1))
                for g in range(2):
                    for m in range(2):
                        last = mm(bank(3, P, P + g * P, 0, NCMP), hid[:, 2 + m, g * NCMP:(g + 1) * NCMP], w2[:, 2 + m, :],
                                  start=(m == 0), stop=(m == 1))
                last.then_inc(slot_free, 1)
                pe.wait_ge(S("cmp_copied"), 1)
                pe.wait_ge(S("c_copied"), 6)
                flip_bias(C_BM, 64)
                attention("c")
                pe.wait_ge(S("att_out"), 32)
                out_proj("c_out", tiles(W(C_O, U)))
                layer_norm_sums()

            BODY.update(ab=ab, moe0=moe(0), c=c, moe1=moe(1))
            for ph in order[:n_stop]:
                if ph == "ffn0":
                    line.next("cact_ready")
                    ada(0)
                    pe.wait_ge(S("zeroed"), 1)
                if ph == "ffn2":
                    pe.wait_ge(S("x_ready"), XR[ph])
                    ada(1)
                if ph.startswith("ffn"):
                    norm_sums()
                    line.next("h_ready")
                    swiglu(ph)
                elif ph == "final":
                    norm_sums()
                else:
                    BODY[ph]()

        @block.scalar
        def _(act):
            fn = nc.scalar.activation
            line = Line(act, "act_chain")
            act.dma_start(const[:, :], const_d[:, :]).then_inc(S("const_in"), 16)
            act.dma_start(vec[:, :], vec_d[:, :]).then_inc(S("const_in"), 16)
            act.dma_start(xT[:, :], x_d[:, :]).then_inc(S("const_in"), 16)
            act.wait_ge(S("const_in"), 48)
            fn(cact[:, :], V("c", 0, 8), ACT.Silu).then_inc(S("cact_ready"), 1)

            def eps(i):
                return C("eps")[:, i:i + 1]

            def rms(ph):
                if XR[ph]:
                    act.wait_ge(S("x_ready"), XR[ph])
                fn(NSQ, xT[:, :], ACT.Square).then_inc(S("sq_ready"), 1)
                line.next("ss_ready")
                fn(STD, bank(7, T), ACT.Sqrt, bias=eps(0), scale=1.0 / D).then_inc(S("std_ready"), 1)

            def layer_norm():
                line.next("centred")
                fn(NSQ, xT[:, :], ACT.Square).then_inc(S("sq_ready"), 1)
                line.next("ss_ready")
                fn(STD, bank(7, T), ACT.Sqrt, bias=eps(1), scale=1.0 / D).then_inc(S("std_ready"), 1)

            def swiglu(tag):
                n, base = SW[tag]

                def one(j, wait_gu, wait_hid):
                    act.wait_ge(S("gu_ready"), wait_gu)
                    if wait_hid is not None:
                        act.wait_ge(S("hid_ready"), wait_hid)
                    fn(W(SW_SILU + (j % 2) * T, T), bank(4 + j % 4, T), ACT.Silu).then_inc(S("silu_ready"), 1)
                for j in range(RING):
                    one(j, base + j + 1, base + j - 1 if j >= 2 else None)
                rounds = n // RING
                with act.Fori(1, rounds) as r:
                    for j in range(RING):
                        one(j, r * RING + (base + j + 1), r * RING + (base + j - 1))
                for j in range(rounds * RING, n):
                    one(j, base + j + 1, base + j - 1)

            def attention(phase):
                items, base, ev0 = ITEMS[phase], IT0[phase], EV0[phase]
                s_of, pt_of, stat = att_place(items, ABASE[phase])
                n = len(items)

                def exps(i):
                    act.wait_ge(S("max_ready"), base + i + 1)
                    s = s_of(i)
                    w = (NCMP, 2 * NCMP) if items[i]["kind"] == "cmp" else (P, ATT)
                    for tt, (lo, hi) in enumerate(((0, w[0]), w)):
                        last = fn(s[:, lo:hi], s[:, lo:hi], ACT.Exp, bias=stat(i, 0)[:, tt:tt + 1],
                                  accum_out=stat(i, 1)[:, tt:tt + 1])
                    last.then_inc(S("exp_ready"), 1)

                def copy_turned(i):
                    act.wait_ge(S("turned"), base + i + 1)
                    if i >= 2:
                        act.wait_ge(S("pv_ready"), base + i - 1)
                    n_, hi = (T, NCMP) if items[i]["kind"] == "cmp" else (ATT, P)
                    fn(pt_of(i)[0:hi, 0:n_], bank(2 + i % 2, n_, 0, 0, hi), ACT.Copy).then_inc(S("pt_ready"), 1)

                def output(i):
                    it = items[i]
                    if not it["last"]:
                        return
                    act.wait_ge(S("pv_ready"), base + i + 1)
                    _, _, _, o, lo, dv = operands(phase, it)
                    line.done(fn(o, bank(4 + it["h"] % 2, T, 0, lo, lo + dv), ACT.Copy), "att_out")

                for step in range(n + 2):
                    if step < n:
                        exps(step)
                    if 1 <= step <= n:
                        copy_turned(step - 1)
                    if step >= 2:
                        output(step - 2)

            def mla():
                rms("mla")
                line.next("lat_copied")
                fn(W(M_TMP, 5 * T), W(M_LAT, 5 * T), ACT.Square).then_inc(S("lat_sq_ready"), 1)
                line.next("ss_ready")
                fn(W(M_TMP + 1536, T), bank(7, T), ACT.Sqrt, bias=eps(0), scale=1.0 / 384)
                fn(W(M_TMP + 1536 + T, T), bank(7, T, T), ACT.Sqrt, bias=eps(0),
                   scale=1.0 / 256).then_inc(S("std_ready"), 1)
                q = W(M_Q, 16 * T, 0, 96)
                for half in range(2):
                    act.wait_ge(slot_free, INDEX[f"mla_uq.{half}"] + 1)
                    fn(q[:, half * 2048:(half + 1) * 2048], PS[0:96, 4 * half:4 * half + 4, :].rearrange(
                        "p b t -> p (b t)"), ACT.Copy).then_inc(S("q_copied"), 1)
                k = W(M_K, 16 * T, 0, 64)
                for half in range(2):
                    line.next("k_ready")
                    fn(k[:, half * 2048:(half + 1) * 2048], PS[0:64, 4 * half:4 * half + 4, :].rearrange(
                        "p b t -> p (b t)"), ACT.Copy).then_inc(S("k_copied"), 1)
                act.wait_ge(slot_free, INDEX["mla_ukv"] + 1)
                fn(W(M_V, 2 * D), PS[:, 0:4, :].rearrange("p b t -> p (b t)"), ACT.Copy).then_inc(S("v_copied"), 1)
                attention("mla")

            BODY = {"mla": mla}
            def head_sqrt(scale, bias):
                src = bank(7, T, 0, 0, 16) if bias is not None else small[0:16, T:2 * T]
                fn(small[0:16, T:2 * T], src, ACT.Sqrt, scale=scale,
                   **({"bias": bias} if bias is not None else {})).then_inc(S("hstd_ready"), 1)

            def rwkv():
                rms("rwkv")
                la = RW_LORA
                act.wait_ge(S("xs_used"), 1)
                fn(W(la, T, 0, 64), bank(0, T, 0, 0, 64), ACT.Tanh).then_inc(S("lora_act"), 1)
                act.wait_ge(S("xs_used"), 2)
                fn(W(la + T, T, 0, 64), bank(1, T, 0, 0, 64), ACT.Copy).then_inc(S("lora_act"), 1)
                act.wait_ge(slot_free, INDEX["rwkv_lora1"] + 1)
                fn(W(la + 2 * T, T), bank(2, T), ACT.Sigmoid)
                fn(W(la + 3 * T, T, 0, 32), bank(3, T, 0, 0, 32), ACT.Sigmoid).then_inc(S("lora_act"), 1)
                for u, name, b0 in ((3, "w0", 8), (4, "a0", 0)):
                    line.next("lora2_ready")
                    for m in range(KT):
                        last = fn(tiles(unit(u))[:, m, :], out_tile(b0 + m), ACT.Sigmoid, bias=V(name, m))
                    last.then_inc(S("proj_copied"), 1)
                for u, name, b0 in ((5, "rwkv_lora2", 4), (6, "rwkv_r.1", 0), (7, "rwkv_k.1", 4), (8, "rwkv_v.1", 0)):
                    act.wait_ge(slot_free, INDEX[name] + 1)
                    fn(unit(u), PS[:, b0:b0 + 4, :].rearrange("p b t -> p (b t)"),
                       ACT.Copy).then_inc(S("proj_copied"), 1)
                line.next("kk_ready")
                fn(unit(9), unit(1), ACT.Square).then_inc(S("hs_in"), 1)
                line.next("hmax_ready")
                head_sqrt(1.0, None)
                line.next("cum_ready")
                fn(unit(10), unit(0), ACT.Exp)
                fn(unit(11), unit(11), ACT.Exp)
                fn(small[:, 0:8], small[:, 0:8], ACT.Exp)
                fn(unit(12), unit(0), ACT.Exp, scale=-1.0).then_inc(S("decay_ready"), 1)
                for n, (u, b0, w) in enumerate(((9, 4, U), (10, 0, 1024), (11, 2, 1024))):
                    line.next("tok_ready")
                    fn(unit(u)[:, 0:w], PS[:, b0:b0 + w // 512, :].rearrange("p b t -> p (b t)"),
                       ACT.Copy).then_inc(S("tok_copied"), 1)
                y12 = tiles(unit(12))
                for tt in range(2):
                    for pair in range(2):
                        for ln in range(2):
                            line.next("x1_ready")
                            fn(RL(ln, "X"), bank(RB[ln]["y"]), ACT.Copy).then_inc(S("x_copied"), 1)
                        for lvl in range(1, 7):
                            for ln in range(2):
                                line.next("y_ready")
                                fn(RL(ln, "Y"), bank(RB[ln]["y"]), ACT.Copy).then_inc(S("y_copied"), 1)
                        for ln in range(2):
                            line.next("t1_ready")
                            fn(RL(ln, "Y")[:, 0:T], bank(ln, T), ACT.Copy).then_inc(S("t1_copied"), 1)
                        for ln in range(2):
                            line.next("u_ready")
                            fn(RL(ln, "Y")[:, T:2 * T], bank(ln, T, T), ACT.Copy).then_inc(S("u_copied"), 1)
                        for ln in range(2):
                            q = 2 * pair + ln
                            line.next("yt_ready")
                            fn(y12[:, 2 * q:2 * q + 2, tt * P:(tt + 1) * P], tiles(bank(RB[ln]["z"], T), P),
                               ACT.Copy).then_inc(S("yt_copied"), 1)
                line.next("gn_centred")
                fn(unit(9), unit(12), ACT.Square).then_inc(S("hs_in"), 1)
                act.wait_ge(S("hs_ready"), 4)
                head_sqrt(1.0 / 64, C("eps", 16)[:, 2:3])

            BODY["rwkv"] = rwkv

            def flat(b0, n=1, width=512, lo=0):
                return PS[:, b0:b0 + n, lo:lo + width] if width < 512 else PS[:, b0:b0 + n, :].rearrange(
                    "p b t -> p (b t)")

            def load_bias(at):
                dst = W(at, 8 * ATT).rearrange("p (h c) -> p h c", c=ATT)
                for lo, hi, tok in ((0, P, 0), (P, ATT, P)):
                    src = bass.AP(tensor=bias_scratch.tensor, offset=P - tok, ap=[[1, P], [512, 8], [1, hi - lo]])
                    act.dma_start(dst[:, :, lo:hi], src).then_inc(S("bias_in"), 16)

            def ab():
                act.wait_ge(S("x_ready"), XR["ab"])
                line.next("bias_ready")
                row = W(A_LS + 512, 512, 0, 8)
                line.done(fn(row, bank(7, 512, 0, 0, 8), ACT.Copy), "bias_copied")
                act.dma_start(bias_scratch[:, :], row).then_inc(S("bias_stored"), 16)
                raw = W(A_RAW, 8 * 259).rearrange("p (i t) -> p i t", t=259)
                dst = {0: W(A_Q, 1024), 1: W(A_K, 1024), 2: W(A_V, 1024), 5: W(A_BV, 1024), 6: W(A_BO, 1024)}
                for i in range(7):
                    act.wait_ge(slot_free, INDEX[f"ab_in.{i}"] + 1)
                    b = (2 * i) % 8
                    if i == 1:
                        act.wait_ge(S("bias_stored"), 16)
                        load_bias(A_BM)
                    if i in dst:
                        last = fn(dst[i], flat(b, 2), ACT.Sigmoid if i == 6 else ACT.Copy)
                    else:
                        src = PS[:, b:b + 2, :].rearrange("p b (c t) -> p (b c) t", t=T)
                        last = fn(raw[:, 4 * (i - 3):4 * (i - 3) + 4, 3:259], src, ACT.Copy)
                    last.then_inc(S("ab_copied"), 1)
                act.wait_ge(slot_free, INDEX["ab_gates"] + 1)

                def ls(at, n, hi=P):
                    return W(A_LS + at, n, 0, hi)
                g, t = ls(0, 16), ls(160, 16)
                line.done(fn(g, bank(6, 16), ACT.Copy))
                line.done(fn(t, g, ACT.Abs))
                line.done(fn(t, t, ACT.Exp, scale=-1.0))
                fn(t, t, ACT.Ln, bias=ones[:, 0:1]).then_inc(S("softlog_ready"), 1)
                line.next("conv_ready")
                fn(W(A_BQ, 2048), W(A_BQ, 2048), ACT.Silu).then_inc(S("bqk_ready"), 1)
                attention("ab")
                line.next("stab_ready")
                dd = ls(256, 1024)
                for i in range(8):
                    fn(dd[:, i * P:(i + 1) * P], dd[:, i * P:(i + 1) * P], ACT.Exp, bias=ls(64 + i, 1))
                fn(ls(72, 8), ls(72, 8), ACT.Exp)
                fn(ls(80, 8), ls(64, 8), ACT.Exp)
                fn(ls(100, 4), ls(100, 4), ACT.Exp).then_inc(S("lexp_ready"), 1)
                line.next("state_ready")
                fn(ls(3840, 512), bank(7), ACT.Copy)
                fn(ls(104, 4), bank(6, 4, 16), ACT.Copy).then_inc(S("state_copied"), 1)
                line.next("lturned")
                fn(ls(2304, 1024), flat(4, 2), ACT.Copy).then_inc(S("lt_copied"), 1)
                line.next("lnum_ready")
                fn(ls(4352, 1024), flat(0, 2), ACT.Copy).then_inc(S("lnum_copied"), 1)
                line.next("lcentred")
                fn(ls(5376, 1024), ls(4352, 1024), ACT.Square).then_inc(S("lsq_ready"), 1)
                line.next("lvar_ready")
                fn(ls(120, 8), ls(120, 8), ACT.Sqrt, bias=eps(1), scale=1.0 / P).then_inc(S("lstd_ready"), 1)
                layer_norm()

            def moe(l):
                def run():
                    act.wait_ge(S("x_ready"), XR[f"moe{l}"])
                    line.next("route_in")
                    fn(W(R_AT + 96, 10), W(R_AT + 96, 10), ACT.Exp).then_inc(S("route_exp"), 1)
                    line.next("gates_turned")
                    fn(W(R_GT, T, 0, 16), bank(7, T, 0, 0, 16), ACT.Copy).then_inc(S("gates_copied"), 1)
                    for half in range(2):
                        line.next("spread_ready")
                        fn(W(SW_G + 2048 * half, 2048), flat(4 * half, 4), ACT.Copy).then_inc(S("g_copied"), 1)
                    swiglu(f"moe{l}")
                    layer_norm()
                return run

            def c():
                act.wait_ge(S("x_ready"), XR["c"])
                load_bias(C_BM)
                for i, (dst, b) in enumerate(((W(C_Q, 1024), 0), (W(C_Q + 1024, 1024), 2), (W(C_SRC, 1024), 4))):
                    act.wait_ge(slot_free, INDEX[f"c_in.{i}"] + 1)
                    fn(dst, flat(b, 2), ACT.Copy).then_inc(S("c_copied"), 1)
                for i, b in ((3, 6), (4, 0)):
                    act.wait_ge(slot_free, INDEX[f"c_in.{i}"] + 1)
                    fn(W(C_KV + 512 * (i - 3), 512), bank(b), ACT.Copy)
                    fn(W(C_KV + 1024 + 512 * (i - 3), 512), bank(b + 1), ACT.Copy).then_inc(S("c_copied"), 1)
                act.wait_ge(slot_free, INDEX["c_gates"] + 1)
                fn(W(C_G, 48), bank(2, 48), ACT.Sigmoid).then_inc(S("c_copied"), 1)
                act.wait_ge(slot_free, INDEX["cmp_w1.3"] + 1)
                for m in range(4):
                    last = fn(W(C_HID + 30 * m, 30), bank(4 + m, 30), ACT.Gelu_apprx_tanh)
                last.then_inc(S("hid_gelu"), 1)
                act.wait_ge(slot_free, INDEX["cmp_w2"] + 1)
                fn(W(C_KC, 30), bank(3, 30), ACT.Copy)
                fn(W(C_VC, 256, 0, NCMP), bank(3, 256, P, 0, NCMP), ACT.Copy).then_inc(S("cmp_copied"), 1)
                attention("c")
                layer_norm()

            BODY.update(ab=ab, moe0=moe(0), c=c, moe1=moe(1))
            for ph in order[:n_stop]:
                if ph.startswith("ffn"):
                    rms(ph)
                    swiglu(ph)
                elif ph == "final":
                    rms(ph)
                else:
                    BODY[ph]()

        @block.vector
        def _(dve):
            v = nc.vector
            line = Line(dve, "dve_chain")
            done = line.done
            tt_, ts_, stt = v.tensor_tensor, v.tensor_scalar, v.scalar_tensor_tensor

            def over_tiles(ap, n=KT):
                return ap.unsqueeze(1).broadcast_to([ap.shape[0], n, ap.shape[1]])

            def mod(layer, sub, which):
                at = ((layer * 3 + sub) * 3 + which) * 8
                return mods[:, at:at + 8]

            WHERE = {"ffn0": (0, 0), "mla": (0, 1), "ffn1": (0, 2), "ffn2": (1, 0), "rwkv": (1, 1), "ffn3": (1, 2)}

            done(v.memset(zeros[:, :], 0.0), "zeroed")
            dve.wait_ge(S("const_in"), 48)

            def ada(layer):
                first = INDEX[f"ada{layer}.0"]

                def one(j, wait, at):
                    dve.wait_ge(slot_free, wait)
                    bias = VEC["ada_b"][0]
                    s = (first + j) % RING
                    if isinstance(at, int):
                        a, b = mods[:, at:at + 4], vec[:, bias + at:bias + at + 4]
                    else:
                        a, b = mods[:, bass.ds(at, 4)], vec[:, bass.ds(at + bias, 4)]
                    tt_(a, bank(s, 4), b, ALU.add).then_inc(S("ada_read"), 1)
                for j in range(RING):
                    one(j, first + j + 1, layer * 72 + 4 * j)
                with dve.Fori(1, 4) as r:
                    for j in range(RING):
                        one(j, r * RING + (first + j + 1), r * (4 * RING) + (layer * 72 + 4 * j))
                for j in range(4 * RING, 18):
                    one(j, first + j + 1, layer * 72 + 4 * j)
                dve.wait_ge(S("ada_read"), 18 * (layer + 1))

            def rms(ph):
                if ph != "final":
                    layer, sub = WHERE[ph]
                    at = (layer * 3 + sub) * 8
                    stt(gain[:, :], mod(layer, sub, 1), 1.0, V("norm_g", at, 8), ALU.add, ALU.mult)
                    done(ts_(gate[:, :], mod(layer, sub, 2), 1.0 if sub == 1 else 0.5, None, ALU.mult))
                line.next("std_ready")
                done(v.reciprocal(RSTD, STD))
                done(tt_(tiles(NTMP), x3, over_tiles(RSTD), ALU.mult))
                tmp = tiles(NTMP)
                for k in range(KT):
                    if ph == "final":
                        last = ts_(x3[:, k, :], tmp[:, k, :], V("final_g", k), None, ALU.mult)
                    else:
                        last = ts_(h3[:, k, :], tmp[:, k, :], gain[:, k:k + 1], mod(layer, sub, 0)[:, k:k + 1],
                                   ALU.mult, ALU.add)
                done(last, "x_ready" if ph == "final" else "h_ready")

            def residual():
                for m in range(KT):
                    last = stt(x3[:, m, :], out_tile(m), gate[:, m:m + 1], x3[:, m, :], ALU.mult, ALU.add)
                done(last, "x_ready")

            def layer_norm(at):
                for b in range(4):
                    last = stt(xT[:, b * 512:(b + 1) * 512], xT[:, b * 512:(b + 1) * 512], ALPHA, bank(b), ALU.mult,
                               ALU.add)
                done(last, "pre_ready")
                line.next("mean_ready")
                done(ts_(RSTD, bank(7, T), 1.0 / D, None, ALU.mult))
                done(tt_(x3, x3, over_tiles(RSTD), ALU.subtract), "centred")
                line.next("std_ready")
                done(v.reciprocal(RSTD, STD))
                done(tt_(x3, x3, over_tiles(RSTD), ALU.mult))
                for k in range(KT):
                    last = ts_(x3[:, k, :], x3[:, k, :], V("ln_g", at + k), V("ln_b", at + k), ALU.mult, ALU.add)
                done(last, "x_ready")

            def swiglu(tag):
                n, base = SW[tag]
                first = INDEX[f"{tag}.0"]
                moe = tag.startswith("moe")

                def one(j, wait_silu, wait_free, expert):
                    dve.wait_ge(S("silu_ready"), wait_silu)
                    if wait_free is not None:
                        dve.wait_ge(slot_free, wait_free)
                    s = W(SW_SILU + (j % 2) * T, T)
                    if moe:
                        if isinstance(expert, int):
                            g = W(SW_G + expert * T, T)
                        else:
                            g = work[:, bass.ds(expert * T + SW_G, T)]
                        tt_(s, s, g, ALU.mult).then_inc(S("gated"), 1)
                        dve.wait_ge(S("gated"), wait_silu - SW["moe0"][1])
                    tt_(W(SW_ACT + (j % 2) * T, T), s, bank(4 + j % 4, T, T), ALU.mult).then_inc(S("hid_ready"), 1)
                for j in range(RING):
                    one(j, base + j + 1, first + j - 1 if j >= 2 else None, 0)
                rounds = n // RING
                with dve.Fori(1, rounds) as r:
                    for j in range(RING):
                        one(j, r * RING + (base + j + 1), r * RING + (first + j - 1), r)
                for j in range(rounds * RING, n):
                    one(j, base + j + 1, first + j - 1, rounds)
                dve.wait_ge(slot_free, first + n)

            def attention(phase):
                items, base = ITEMS[phase], IT0[phase]
                s_of, _, stat = att_place(items, ABASE[phase])
                n = len(items)
                scale = SCALE[phase]

                def cuts(i):
                    return ((0, NCMP), (NCMP, 2 * NCMP)) if items[i]["kind"] == "cmp" else ((0, P), (P, ATT))

                def maxima(i):
                    cmp_ = items[i]["kind"] == "cmp"
                    w = 2 * NCMP if cmp_ else ATT
                    line.next("score_ready")
                    if i >= 2:
                        dve.wait_ge(S("turned"), base + i - 1)
                    s = s_of(i)
                    done(stt(s[:, 0:w], bank(i % 2, w), scale, score_bias(phase, items[i]), ALU.mult, ALU.add))
                    for k, (lo, hi) in enumerate(cuts(i)):
                        last = v.tensor_reduce(stat(i, 0)[:, k:k + 1], s[:, lo:hi], AX.X, ALU.max, negate=True)
                    if cmp_:
                        done(last)
                        last = ts_(stat(i, 0), stat(i, 0), -0.1 * NEG, None, ALU.min)
                    done(last, "max_ready")

                def normalise(i):
                    line.next("exp_ready")
                    it = items[i]
                    if it["kind"] == "cmp":
                        done(ts_(stat(i, 1), stat(i, 1), 1e-30, None, ALU.max))
                    done(v.reciprocal(stat(i, 2), stat(i, 1)))
                    if phase == "c":
                        g = W(C_G, 48).rearrange("p (t g) -> p t g", t=2)
                        c = 8 * it["branch"] + it["h"]
                        done(tt_(stat(i, 2), stat(i, 2), g[:, :, c:c + 1].squeeze(2), ALU.mult))
                    s = s_of(i)
                    for k, (lo, hi) in enumerate(cuts(i)):
                        last = ts_(s[:, lo:hi], s[:, lo:hi], stat(i, 2)[:, k:k + 1], None, ALU.mult)
                    done(last, "prob_ready")

                for step in range(n + 1):
                    if step < n:
                        maxima(step)
                    if step >= 1:
                        normalise(step - 1)

            def mla():
                rms("mla")
                dve.wait_ge(slot_free, INDEX["mla_in.1"] + 1)
                v.tensor_copy(W(M_LAT, 1024), PS[:, 0:2, :].rearrange("p b t -> p (b t)"))
                v.tensor_copy(W(M_LAT + 1024, T), bank(2, T))
                done(v.tensor_copy(W(M_KR, T, 64, 96), bank(2, T, T, 64, 96)), "lat_copied")
                line.next("std_ready")
                r = W(M_TMP + 1536, 2 * T)
                done(v.reciprocal(r, r))
                lat = tiles(W(M_LAT, 5 * T))
                for i in range(5):
                    g = V("q_norm", i) if i < 3 else V("kv_norm", i - 3)
                    last = stt(lat[:, i, :], lat[:, i, :], g, r[:, 0:T] if i < 3 else r[:, T:2 * T], ALU.mult,
                               ALU.mult)
                done(last, "lat_ready")
                at = CONST["cos"][0]
                cos, sin = const[64:96, at:at + T], const[64:96, at + T:at + 2 * T]
                q = W(M_Q, 16 * T, 64, 96)
                t = W(M_TMP, 8 * T, 64, 96)
                for g in range(2):
                    line.next("rot_ready")
                    ps = PS[64:96, 4 - 4 * g:8 - 4 * g, :].rearrange("p b (h t) -> p (b h) t", t=T)
                    done(tt_(tiles(t), ps, over_tiles(sin), ALU.mult), "rot_read")
                    qg = tiles(q)[:, 8 * g:8 * g + 8, :]
                    done(tt_(qg, qg, over_tiles(cos), ALU.mult))
                    done(tt_(qg, qg, tiles(t), ALU.add))
                line.next("rot_ready")
                kr = W(M_KR, T, 64, 96)
                tt_(t[:, 0:T], bank(4, T, 0, 64, 96), sin, ALU.mult)
                done(tt_(kr, kr, cos, ALU.mult))
                k16 = tiles(W(M_K, 16 * T, 64, 96))
                done(tt_(k16, over_tiles(kr, 16), over_tiles(t[:, 0:T], 16), ALU.add), "qk_ready")
                attention("mla")
                dve.wait_ge(S("att_out"), 16)
                dve.wait_ge(slot_free, INDEX["mla_out.1"] + 1)
                residual()

            BODY = {"mla": mla}
            def banks4(b0):
                return PS[:, b0:b0 + 4, :].rearrange("p b t -> p (b t)")

            def rwkv():
                rms("rwkv")
                xx = tiles(unit(0))
                tt_(xx[:, :, 1:T], h3[:, :, 0:T - 1], h3[:, :, 1:T], ALU.subtract)
                done(ts_(xx[:, :, 0:1], h3[:, :, 0:1], -1.0, None, ALU.mult))
                ld = unit(3)
                for n, mu in enumerate((3, 4, 5, 0, 1, 2)):
                    if n in (2, 3):
                        dve.wait_ge(S("xs_used"), n - 1)
                    if n == 4:
                        dve.wait_ge(slot_free, INDEX["rwkv_lora1"] + 1)
                    if n == 5:
                        dve.wait_ge(slot_free, INDEX["rwkv_r.1"] + 1)
                    xs = tiles(unit(1 + n % 2))
                    for k in range(KT):
                        last = stt(xs[:, k, :], xx[:, k, :], V("mu", 8 * mu + k), h3[:, k, :], ALU.mult, ALU.add)
                    done(last, "xs_ready")
                    if n == 3:
                        dve.wait_ge(S("proj_copied"), 1)
                        done(ts_(ld, ld, -math.exp(-0.5), None, ALU.mult))
                        done(v.memset(unit(10), 1.0))
                        done(v.memset(tiles(unit(10), P)[:, :, 0:1], 0.0))
                cum = tiles(unit(0), P)
                done(v.tensor_tensor_scan(unit(0), unit(10), ld, 0.0, ALU.mult, ALU.add))
                mid, f = small[:, 16:32], small[:, 0:8]
                done(v.tensor_copy(mid.unsqueeze(2), cum[:, :, 63:64]))
                end = cum[:, 0:16:2, P - 1:P].squeeze(2)
                done(tt_(f, end, mid[:, 0:16:2], ALU.subtract))
                tt_(f, f, mid[:, 1:16:2], ALU.add)
                done(tt_(cum, cum, mid.unsqueeze(2).broadcast_to([P, 16, P]), ALU.subtract))
                done(tt_(unit(11), unit(0), ld, ALU.subtract), "cum_ready")
                dve.wait_ge(S("proj_copied"), 5)
                for k in range(KT):
                    last = ts_(tiles(unit(1))[:, k, :], tiles(unit(7))[:, k, :], V("k_k", k), None, ALU.mult)
                done(last, "kk_ready")
                line.next("hs_ready")
                hst = small[0:16, T:2 * T]
                done(ts_(hst, bank(7, T, 0, 0, 16), 1e-24, None, ALU.max), "hmax_ready")
                line.next("hstd_ready")
                done(v.reciprocal(hst, hst), "hb_in")
                line.next("hb_ready")
                done(tt_(unit(1), unit(1), banks4(0), ALU.mult))
                for k in range(KT):
                    last = ts_(tiles(unit(9))[:, k, :], tiles(unit(4))[:, k, :], 1.0, V("k_a", k), ALU.subtract,
                               ALU.mult)
                done(last)
                done(stt(unit(7), unit(9), 1.0, unit(7), ALU.add, ALU.mult))
                done(tt_(unit(9), unit(6), unit(7), ALU.mult))
                for k in range(KT):
                    u9 = tiles(unit(9))[:, k, :]
                    last = ts_(u9, u9, V("r_k", k), None, ALU.mult)
                done(last, "hs_in_dve")
                line.next("decay_ready")
                done(tt_(unit(4), unit(1), unit(4), ALU.mult))
                tt_(unit(4), unit(4), unit(12), ALU.mult)
                tt_(unit(7), unit(7), unit(12), ALU.mult)
                tt_(unit(6), unit(6), unit(10), ALU.mult)
                done(stt(unit(1), unit(1), -1.0, unit(11), ALU.mult, ALU.mult))
                line.next("hs_ready")
                done(v.tensor_copy(hst, bank(7, T, 0, 0, 16)), "hb_in")
                line.next("hb_ready")
                dve.wait_ge(S("proj_copied"), 6)
                done(tt_(hT[:, :], unit(8), banks4(0), ALU.mult))
                done(v.memset(W(10 * U + 1024, 1024), 0.0), "tilde_ready")
                spad = W(10 * U + 1024, 1024)
                strict = C("strict").unsqueeze(1).broadcast_to([P, 4, P])
                incl = C("incl").unsqueeze(1).broadcast_to([P, 4, P])
                for tt in range(2):
                    for pair in range(2):
                        for ln in range(2):
                            line.next("pair_scores")
                            ak, rk = RL(ln, "AK"), RL(ln, "RK")
                            for par in range(2):
                                b = 4 * ln + 2 * par
                                tt_(tiles(ak[:, par * 512:(par + 1) * 512], P), tiles(bank(b), P), strict, ALU.mult)
                                last = tt_(tiles(rk[:, par * 512:(par + 1) * 512], P), tiles(bank(b + 1), P), incl,
                                           ALU.mult)
                            done(last, "ak_ready")
                        for ln in range(2):
                            line.next("lvl_ready")
                            done(tt_(tiles(RL(ln, "XT"), P), tiles(RL(ln, "MTL"), P),
                                     ident.unsqueeze(1).broadcast_to([P, 4, P]), ALU.add), "xt_ready")
                        for lvl in range(1, 7):
                            for ln in range(2):
                                line.next("z_ready")
                                if lvl < 6:
                                    tt_(RL(ln, "X"), RL(ln, "X"), bank(RB[ln]["z"]), ALU.add)
                                done(tt_(RL(ln, "XT"), RL(ln, "XT"), bank(RB[ln]["zt"]), ALU.add), "x_upd")
                        line.seen["lvl_ready"] += 12
                        if tt == 0:
                            for ln in range(2):
                                line.next("s_ready")
                                for j in range(4):
                                    q = 2 * pair + ln
                                    h, k, lo = 4 * q + j, 2 * q + j // 2, 64 * (j % 2)
                                    last = ts_(spad[lo:lo + 64, h * 64:(h + 1) * 64],
                                               bank(RB[ln]["zt"], 64, j * 64, lo, lo + 64), f[lo:lo + 64, k:k + 1],
                                               None, ALU.mult)
                                done(last, "s_copied")
                y = unit(12)
                line.next("hs_ready")
                done(ts_(hst, bank(7, T, 0, 0, 16), 1.0 / 64, None, ALU.mult), "hb_in")
                line.next("hb_ready")
                done(tt_(y, y, banks4(0), ALU.subtract), "gn_centred")
                line.next("hstd_ready")
                done(v.reciprocal(hst, hst), "hb_in")
                line.next("hb_ready")
                done(tt_(y, y, banks4(0), ALU.mult))
                for k in range(KT):
                    yk = tiles(y)[:, k, :]
                    last = ts_(yk, yk, V("gn_w", k), V("gn_b", k), ALU.mult, ALU.add)
                done(last)
                done(tt_(y, y, hT[:, :], ALU.add))
                done(tt_(y, y, unit(5), ALU.mult), "mix_ready")
                dve.wait_ge(slot_free, INDEX["rwkv_out.1"] + 1)
                residual()

            BODY["rwkv"] = rwkv

            def bias_banks():
                return PS[:, 0:6, :].rearrange("p b t -> p (b t)").rearrange("p (h c) -> p h c", c=ATT)

            def ab():
                def ls(at, n, hi=P):
                    return W(A_LS + at, n, 0, hi)

                raw = W(A_RAW, 8 * 259).rearrange("p (i t) -> p i t", t=259)
                done(v.memset(raw[:, :, 0:3], 0.0))
                dve.wait_ge(S("ab_copied"), 5)
                qk = tiles(W(A_BQ, 2048))
                for j in range(4):
                    for i in range(8):
                        w = V("conv", 8 * j + i)
                        if j == 0:
                            last = ts_(qk[:, i, :], raw[:, i, 0:T], w, None, ALU.mult)
                        else:
                            last = stt(qk[:, i, :], raw[:, i, j:j + T], w, qk[:, i, :], ALU.mult, ALU.add)
                    done(last, "conv_ready" if j == 3 else None)
                line.next("softlog_ready")
                g = ls(0, 16).rearrange("p (t g) -> p t g", t=2)
                sl = ls(160, 16).rearrange("p (t g) -> p t g", t=2)
                lf = ls(16, 8).rearrange("p (t h) -> p t h", t=2)
                done(ts_(lf, g[:, :, 4:8], 0.0, None, ALU.min))
                done(tt_(lf, lf, sl[:, :, 4:8], ALU.subtract), "lf_ready")
                line.next("bias_flipped")
                done(tt_(W(A_BM, 8 * ATT).rearrange("p (h c) -> p h c", c=ATT), bias_banks(),
                         C("dilated").unsqueeze(1).broadcast_to([P, 8, ATT]), ALU.add), "bias_used")
                attention("ab")
                line.next("cumsum_ready")
                b, bl, gi = ls(24, 8), ls(32, 8), ls(40, 8)
                v.tensor_copy(b, bank(6, 8))
                done(v.tensor_copy(bl, bank(6, 8, 8)))
                done(tt_(gi.rearrange("p (t h) -> p t h", t=2), g[:, :, 0:4], b.rearrange("p (t h) -> p t h", t=2),
                         ALU.subtract))
                dd = ls(256, 1024)
                for i in range(8):
                    last = ts_(dd[:, i * P:(i + 1) * P], ident, gi[:, i:i + 1], None, ALU.mult)
                done(last, "diag_ready")
                line.next("rowbc_ready")
                causal = C("causal")[:, 0:P]
                for i in range(8):
                    last = stt(dd[:, i * P:(i + 1) * P], bank(7 if i >= 4 else 2, P, (i % 4) * P), b[:, i:i + 1], causal,
                               ALU.add, ALU.add)
                m1 = ls(96, 4)
                done(v.tensor_reduce(m1, tiles(bank(2), P), AX.X, ALU.max))
                done(stt(m1, m1, 0.0, bl[:, 0:4], ALU.max, ALU.add))
                mx, inter, nmt, sc = ls(48, 8), ls(56, 8), ls(64, 8), ls(72, 8)
                v.tensor_copy(inter[:, 0:4], b[:, 0:4])
                tt_(inter[:, 4:8], b[:, 4:8], m1, ALU.add)
                done(v.tensor_reduce(mx, tiles(dd, P), AX.X, ALU.max))
                done(tt_(mx, mx, inter, ALU.max))
                ts_(nmt, mx, -1.0, None, ALU.mult)
                wk = ls(100, 4)
                tt_(wk, gi[:, 0:4], bl[:, 0:4], ALU.add)
                done(tt_(sc, inter, mx, ALU.subtract))
                done(tt_(wk, wk, m1, ALU.subtract), "stab_ready")
                line.next("lexp_ready")
                line.next("ktok_ready")
                kw = ls(3328, 512)
                for h in range(4):
                    last = ts_(kw[:, h * P:(h + 1) * P], bank(3, P, h * P), wk[:, h:h + 1], None, ALU.mult)
                done(last, "kw_ready")
                line.next("lqk_ready")
                ss = ls(1280, 1024)
                for tt in range(2):
                    last = stt(ss[:, tt * 512:(tt + 1) * 512], bank(tt), P ** -0.5, dd[:, tt * 512:(tt + 1) * 512],
                               ALU.mult, ALU.mult)
                done(last, "lprob_ready")
                den = ls(88, 8)
                done(v.tensor_reduce(den, tiles(ss, P), AX.X, ALU.add))
                hh = ls(4352, 1024)
                line.next("lnum_copied")
                line.next("linter_ready")
                done(ts_(sc, sc, P ** -0.5, None, ALU.mult))
                for h in range(4):
                    hs = slice((4 + h) * P, (5 + h) * P)
                    stt(hh[:, hs], bank(2, P, h * P), sc[:, 4 + h:5 + h], hh[:, hs], ALU.mult, ALU.add)
                tmp = ls(112, 8)
                done(tt_(tmp[:, 0:4], bank(6, 4, 32), sc[:, 4:8], ALU.mult))
                done(tt_(den[:, 4:8], den[:, 4:8], tmp[:, 0:4], ALU.add))
                done(ts_(tmp, den, -1.0, None, ALU.mult))
                done(tt_(den, den, tmp, ALU.max))
                done(tt_(den, den, ls(80, 8), ALU.max))
                done(v.reciprocal(den, den))
                h8 = tiles(hh, P)

                def each(s):
                    return s.unsqueeze(2).broadcast_to([P, 8, P])
                done(tt_(h8, h8, each(den), ALU.mult))
                done(v.tensor_reduce(tmp, h8, AX.X, ALU.add))
                done(ts_(tmp, tmp, 1.0 / P, None, ALU.mult))
                done(tt_(h8, h8, each(tmp), ALU.subtract), "lcentred")
                line.next("lsq_ready")
                var = ls(120, 8)
                done(v.tensor_reduce(var, tiles(ls(5376, 1024), P), AX.X, ALU.add), "lvar_ready")
                line.next("lstd_ready")
                done(v.reciprocal(var, var))
                done(tt_(h8, h8, each(var), ALU.mult), "lnormed")
                line.next("lout_ready")
                for h in range(4):
                    last = stt(tiles(W(A_Y, U))[:, 4 + h, :], bank(4 + h // 2, T, (h % 2) * T), V("head_norm", h),
                               tiles(W(A_BO, 1024))[:, h, :], ALU.mult, ALU.mult)
                done(last, "mix_ready")
                dve.wait_ge(slot_free, INDEX["ab_out.1"] + 1)
                layer_norm(0)

            def first_max(onehot, x, mx, tmp):
                iota = C("iota").unsqueeze(1).broadcast_to([P, 2, 4])
                done(v.tensor_reduce(mx, x, AX.X, ALU.max))
                done(tt_(tmp, x, mx.unsqueeze(2).broadcast_to([P, 2, 4]), ALU.is_equal))
                done(ts_(onehot, iota, -4.0, None, ALU.add))
                done(tt_(tmp, tmp, onehot, ALU.mult))
                idx = W(R_AT + 150, 2)
                done(v.tensor_reduce(idx, tmp, AX.X, ALU.min))
                done(tt_(onehot, onehot, idx.unsqueeze(2).broadcast_to([P, 2, 4]), ALU.is_equal))

            def moe(l):
                def run():
                    ph = f"moe{l}"

                    def r(at, n):
                        return W(R_AT + at, n)

                    def by4(ap):
                        return ap.rearrange("p (t g) -> p t g", g=4)
                    done(v.tensor_copy(tiles(W(R_PICK, 2048, 0, 16), P),
                                       ident[0:16, 0:16].unsqueeze(2).broadcast_to([16, 16, P])), "pick_ready")
                    dve.wait_ge(slot_free, INDEX[f"router{l}"] + 1)
                    lg = r(40, 40).rearrange("p (t g) -> p t g", t=2)
                    done(v.tensor_copy(r(40, 40), bank(7, 40)))
                    gate_, oh, oh1, oh2, tmp = r(0, 32), by4(r(110, 8)), by4(r(118, 8)), by4(r(126, 8)), by4(r(134, 8))
                    gm, m1, m2 = r(142, 2), r(144, 2), r(146, 2)
                    first_max(oh, lg[:, :, 0:4], gm, tmp)
                    ex = r(96, 8)
                    done(tt_(by4(ex), lg[:, :, 0:4], gm.unsqueeze(2).broadcast_to([P, 2, 4]), ALU.subtract))
                    w = r(160, 32).rearrange("p (t g e) -> p t g e", t=2, g=4)
                    le = lg[:, :, 4:20].rearrange("p t (g e) -> p t g e", g=4)
                    for t in range(2):
                        last = tt_(w[:, t], le[:, t], oh[:, t, :].unsqueeze(2).broadcast_to([P, 4, 4]), ALU.mult)
                    done(last)
                    es = by4(r(192, 8))
                    for t in range(2):
                        last = v.tensor_reduce(es[:, t, :], w[:, t].rearrange("p g e -> p e g"), AX.X, ALU.add)
                    done(last)
                    first_max(oh1, es, m1, tmp)
                    done(stt(es, oh1, NEG, es, ALU.mult, ALU.add))
                    first_max(oh2, es, m2, tmp)
                    done(tt_(r(104, 2), m2, m1, ALU.subtract), "route_in")
                    line.next("route_exp")
                    gw, w1, w2 = r(200, 2), r(202, 2), r(204, 2)
                    done(v.tensor_reduce(gw, by4(ex), AX.X, ALU.add))
                    done(ts_(w1, r(104, 2), 1.0, None, ALU.add))
                    done(tt_(w1, w1, gw, ALU.mult))
                    done(v.reciprocal(w1, w1))
                    done(tt_(w2, w1, r(104, 2), ALU.mult))
                    done(tt_(oh1, oh1, w1.unsqueeze(2).broadcast_to([P, 2, 4]), ALU.mult))
                    done(tt_(oh2, oh2, w2.unsqueeze(2).broadcast_to([P, 2, 4]), ALU.mult))
                    done(tt_(oh1, oh1, oh2, ALU.add))
                    g4 = gate_.rearrange("p (t g e) -> p t g e", t=2, g=4)
                    for t in range(2):
                        last = tt_(g4[:, t], oh[:, t, :].unsqueeze(2).broadcast_to([P, 4, 4]),
                                   oh1[:, t:t + 1, :].broadcast_to([P, 4, 4]), ALU.mult)
                    done(last, "gates_ready")
                    swiglu(ph)
                    layer_norm(16 * l + 8)
                return run

            def c():
                dve.wait_ge(S("c_copied"), 3)
                for kv in range(2):
                    dst = W(C_CMPB + 960 * kv, 960).rearrange("p (i g n) -> p i g n", g=2, n=NCMP)
                    for g in range(2):
                        src = W(C_SRC + (2 * kv + g) * T, T).rearrange("p (n r) -> p r n", r=16)
                        for a in range(2):
                            pos = V("cmp_pos", 32 * kv + 16 * a, 16).unsqueeze(2).broadcast_to([P, 16, NCMP])
                            last = tt_(dst[:, 16 * a:16 * a + 16, g, :], src[:, :, a:a + NCMP], pos, ALU.add)
                done(last, "cmpb_ready")
                line.next("bias_flipped")
                raw = bias_banks()
                bm = W(C_BM, 8 * ATT).rearrange("p (h c) -> p h c", c=ATT)
                bc = W(C_BC, 240).rearrange("p (h t n) -> p h t n", h=8, t=2)
                done(v.memset(W(C_BC, 240), 0.0))
                v.tensor_copy(bc[:, :, 0, 0:7], raw[:, :, 31:P:16])
                done(v.tensor_copy(bc[:, :, 1, :], raw[:, :, P + 31:ATT:16]))
                done(tt_(W(C_BC, 240).rearrange("p (h c) -> p h c", h=8), W(C_BC, 240).rearrange("p (h c) -> p h c", h=8),
                         C("cmpmask").unsqueeze(1).broadcast_to([P, 8, 2 * NCMP]), ALU.add))
                done(tt_(bm, raw, C("causal").unsqueeze(1).broadcast_to([P, 8, ATT]), ALU.add), "bias_used")
                dve.wait_ge(S("c_copied"), 6)
                attention("c")
                dve.wait_ge(slot_free, INDEX["c_out.1"] + 1)
                layer_norm(16)

            BODY.update(ab=ab, moe0=moe(0), c=c, moe1=moe(1))
            for ph in order[:n_stop]:
                if ph == "ffn0":
                    ada(0)
                if ph == "ffn2":
                    ada(1)
                if ph.startswith("ffn"):
                    rms(ph)
                    swiglu(ph)
                    residual()
                elif ph == "final":
                    rms(ph)
                else:
                    BODY[ph]()

        @block.gpsimd
        def _(pool):
            line = Line(pool, "pool_chain")
            mul = nc.gpsimd.tensor_tensor

            def rwkv():
                levels = C("level").rearrange("p (l t) -> p l t", t=P)
                for tt in range(2):
                    for pair in range(2):
                        for lvl in range(7):
                            for ln in range(2):
                                if lvl == 0:
                                    line.next("ak_ready")
                                elif lvl == 1:
                                    line.next("xt_ready")
                                else:
                                    line.next("y_ready")
                                m = RL(ln, "AK").rearrange("p (e c t) -> p e c t", e=2, t=P)[:, :, 0:2, :]
                                o = RL(ln, "MTL").rearrange("p (e c t) -> p e c t", e=2, t=P)
                                for e in range(2):
                                    last = mul(o[:, e], m[:, e],
                                               levels[:, lvl:lvl + 1, :].broadcast_to([P, 2, P]), ALU.mult)
                                last.then_inc(S("lvl_ready"), 1)
                        line.next("y_ready", 2)

            if "rwkv" in order[:n_stop]:
                rwkv()




def bucket(dist):
    n = np.maximum(dist, 0)
    nf = np.maximum(n, 1).astype(np.float32)
    large = 16 + (np.log(nf / 16) / math.log(2048 / 16) * 16).astype(np.int32)
    return np.where(n < 16, n, np.minimum(large, 31))


def constants():
    c = np.zeros((P, NCONST), np.float32)

    def put(name, value, lo=0):
        value = np.asarray(value, np.float32)
        value = value.reshape(value.shape[0], -1)
        at, n = CONST[name]
        assert value.shape[1] == n, name
        c[lo:lo + value.shape[0], at:at + n] = value

    i = np.arange(P)
    put("ident", np.eye(P))
    put("flip", np.eye(P)[::-1])
    put("ones", np.ones((P, P)))
    r = np.arange(32)
    put("rot", (r[:, None] == (r[None, :] + 16) % 32), 64)
    inv = np.float32(10000.0) ** (-np.arange(0, 32, 2, dtype=np.float32) / np.float32(32))
    ang = (np.arange(T, dtype=np.float32)[:, None] * inv[None, :]).astype(np.float32).T
    put("cos", np.concatenate([np.cos(ang)] * 2), 64)
    put("sin", np.concatenate([-np.sin(ang), np.sin(ang)]), 64)
    dist = np.concatenate([i[:, None] - i[None, :], (i[:, None] + P) - np.arange(T)[None, :]], 1)
    put("causal", np.where(dist >= 0, 0.0, NEG))
    times = ((dist >= 0) & (dist <= 128)).astype(int) + ((dist >= 0) & (dist % 4 == 0)) + ((dist >= 0) & (dist % 16 == 0))
    put("dilated", np.where(times > 0, np.log(np.maximum(times, 1)), NEG))
    s, t = i[:, None], i[None, :]
    put("strict", s < t)
    put("incl", s <= t)
    put("level", np.concatenate([(t // b % 2 == 1) & (s // b == t // b - 1) for b in (1, 2, 4, 8, 16, 32, 64)], 1))
    k, h = np.arange(KT), np.arange(16)
    sel = h[None, None, :] == 2 * k[None, :, None] + i[:, None, None] // 64
    put("hsel", sel)
    put("hselT", sel.transpose(2, 1, 0))
    put("dist", np.arange(32)[:, None] == bucket(255 - np.arange(512))[None, :])
    tok = i[:, None, None] + P * np.arange(2)[None, :, None]
    put("cmpmask", np.where(tok >= 16 * np.arange(NCMP) + 31, 0.0, NEG))
    put("iota", np.broadcast_to(np.arange(4), (P, 4)))
    put("eps", np.broadcast_to([1e-6, 1e-5, 64e-5], (P, 3)))
    return c


def pack(a):
    stream = np.zeros((len(STREAM), P, SLOT), np.float32)

    def put(name, value):
        value = value.reshape(value.shape[0], -1)
        stream[INDEX[name], :value.shape[0], :value.shape[1]] = value

    def rows(w):
        return w.reshape(-1, P, w.shape[1]).transpose(1, 0, 2)

    def put_cols(tag, w, width=512):
        for i in range(w.shape[1] // width):
            put(f"{tag}.{i}", rows(w[:, i * width:(i + 1) * width]))

    def put_swiglu(tag, n, gate, up, down):
        g, u, d = rows(gate), rows(up), rows(down)
        for m in range(n):
            i = INDEX[f"{tag}.{m}"]
            dst = stream[i, :, 0:2048].reshape(P, KT, 2, P)
            dst[:, :, 0] = g[:, :, m * P:(m + 1) * P]
            dst[:, :, 1] = u[:, :, m * P:(m + 1) * P]
            stream[i, :, 2048:3072] = d[:, m]

    for l in range(2):
        put_cols(f"ada{l}", a["ada_w"][l])
        for j in range(2):
            w = a["ffn_w_in"][l, j]
            put_swiglu(f"ffn{2 * l + j}", FF_TILES, w[:, :2816], w[:, 2816:], a["ffn_w_out"][l, j])
    w = a["mla_w_in"][0]
    put("mla_in.0", rows(w[:, :512]))
    put("mla_in.1", rows(np.concatenate([w[:, 512:640], np.zeros((D, 64), np.float32), w[:, 640:]], 1)))
    for i in range(2):
        put(f"mla_uq.{i}", rows(a["mla_w_uq"][0][:, 768 * i:768 * (i + 1)]))
    w = a["mla_w_ukv"][0].reshape(256, 16, 2, 64).transpose(0, 2, 1, 3).reshape(256, 2, D)
    put("mla_ukv", np.concatenate([rows(w[:, 0]).reshape(P, -1), rows(w[:, 1]).reshape(P, -1)], 1))
    put_cols("mla_out", a["mla_w_out"][0])
    put("rwkv_lora1", rows(np.concatenate([a["rwkv_wd1"][0], a["rwkv_wa1"][0], a["rwkv_wg1"][0]], 1)))
    i = INDEX["rwkv_lora2"]
    stream[i, :64, 0:1024] = a["rwkv_wd2"][0]
    stream[i, :64, 1024:2048] = a["rwkv_wa2"][0]
    stream[i, :, 2048:3072] = a["rwkv_wg2"][0][:128]
    stream[i, :32, 3072:4096] = a["rwkv_wg2"][0][128:]
    for n, tag in enumerate(("rwkv_r", "rwkv_k", "rwkv_v")):
        put_cols(tag, a["rwkv_w_rkv"][0, n])
    put_cols("rwkv_out", a["rwkv_w_out"][0])
    w = a["ab_w_in_2"][0]
    put_cols("ab_in", w[:, :3584])
    put("ab_gates", rows(w[:, 3584:]))
    put_cols("ab_out", a["ab_w_out_2"][0])
    w = a["c_w_in_2"][0]
    put_cols("c_in", w[:, :2560])
    put("c_gates", rows(w[:, 2560:]))
    for kv in range(2):
        w = a["c_cmp_w1_2"][0, kv].reshape(32, P, 256).transpose(1, 0, 2)
        for half in range(2):
            put(f"cmp_w1.{2 * kv + half}", w[:, 16 * half:16 * half + 16])
    put("cmp_w2", np.concatenate([rows(a["c_cmp_w2_2"][0, kv]).reshape(P, -1) for kv in range(2)], 1))
    put_cols("c_out", a["c_w_out_2"][0])
    for l in range(2):
        w = np.concatenate([a["moe_wr_g_2"][l], a["moe_wr_e_2"][l].transpose(1, 0, 2).reshape(D, 16)], 1)
        put(f"router{l}", rows(w))
        for e in range(EXPERTS):
            g, u, d = (rows(a[n][l, e]) for n in ("moe_w_gate_2", "moe_w_up_2", "moe_w_down_2"))
            for m in range(E_TILES):
                i = INDEX[f"moe{l}.{e * E_TILES + m}"]
                dst = stream[i, :, 0:2048].reshape(P, KT, 2, P)
                dst[:, :, 0] = g[:, :, m * P:(m + 1) * P]
                dst[:, :, 1] = u[:, :, m * P:(m + 1) * P]
                stream[i, :, 2048:3072] = d[:, m]

    vec = np.zeros((P, NVEC), np.float32)

    def col(name, value):
        at, n = VEC[name]
        vec[:, at:at + n] = np.ascontiguousarray(value).reshape(n, P).T

    def row(name, value):
        at, n = VEC[name]
        value = value.reshape(-1, n)
        vec[:value.shape[0], at:at + n] = value

    for name, key in (("c", "c"), ("ada_b", "ada_b"), ("norm_g", "norm_g"), ("final_g", "final_g"),
                      ("q_norm", "mla_q_norm"), ("kv_norm", "mla_kv_norm"), ("mu", "rwkv_mu"), ("w0", "rwkv_w0"),
                      ("a0", "rwkv_a0"), ("k_k", "rwkv_k_k"), ("k_a", "rwkv_k_a"), ("r_k", "rwkv_r_k"),
                      ("gn_w", "rwkv_gn_w"), ("gn_b", "rwkv_gn_b"), ("ln_g", "ln_g_2"), ("ln_b", "ln_b_2"),
                      ("conv", "ab_conv_2"), ("head_norm", "ab_head_norm_2"), ("cmp_pos", "c_cmp_pos_2")):
        col(name, a[key])
    row("rel_bias", a["rel_bias_2"])
    row("ab_gate_b", a["ab_gate_b_2"])
    row("c_gate_b", a["c_gate_b_2"])
    row("moe_b", np.concatenate([a["moe_br_g_2"], a["moe_br_e_2"].reshape(2, 16)], 1))
    return stream, vec


def kernel(**inputs):
    import concourse.bacc as bacc
    from concourse.bass_utils import run_bass_kernel_spmd

    a = {k: np.asarray(v) for k, v in inputs.items()}
    stream, vec = pack(a)
    x = np.ascontiguousarray(a["x"][0].reshape(T, KT, P).transpose(2, 1, 0)).reshape(P, KT * T)
    arrays = {"stream": stream, "const_tables": constants(), "vectors": vec, "x_in": x}
    nc = bacc.Bacc("TRN2", target_bir_lowering=False, num_devices=1)
    args = [nc.dram_tensor(n, v.shape, F32, kind="ExternalInput").ap() for n, v in arrays.items()]
    out = nc.dram_tensor("out", (P, KT * T), F32, kind="ExternalOutput").ap()
    scratch = nc.dram_tensor("bias_scratch", (8, 512), F32).ap()
    build(nc, *args, out, scratch)
    r = run_bass_kernel_spmd(nc, [arrays], core_ids=[0])
    got = r.results[0]["out"]
    return np.ascontiguousarray(got.reshape(P, KT, T).transpose(2, 1, 0)).reshape(1, T, D)
```

```python
import math
from contextlib import ExitStack

import numpy as np

import concourse.bass as bass
from concourse import mybir

F32 = mybir.dt.float32
F32R = mybir.dt.float32r
ALU = mybir.AluOpType
ACT = mybir.ActivationFunctionType
AX = mybir.AxisListType

P = 128
T = 256
D = 1024
KT = D // P
FF_TILES = 2816 // P
EXPERTS = 16
E_TILES = 512 // P
RING = 4
SLOT = 4096
NEG = -1.0e30
ALPHA = (2.0 * 2) ** 0.25
ATT = 384
NCMP = 15

ADA_PIECES = 2 * 9 * D // 512
ADA_HEAD = 4
ADA_CARRIED = (ADA_PIECES - ADA_HEAD) // 2



def stream_plan():
    def swiglu(tag, n):
        return [(f"{tag}.{m}", 3072) for m in range(n)]

    def cols(tag, widths):
        return [(f"{tag}.{i}", 8 * w) for i, w in enumerate(widths)]

    def with_ada(tag, first):
        tiles_, n = swiglu(tag, FF_TILES), ADA_CARRIED
        return [q for j in range(n) for q in (tiles_[j], ada[first + j])] + tiles_[n:]

    ada = cols("ada", [512] * ADA_PIECES)
    p = ada[:ADA_HEAD] + with_ada("ffn0", ADA_HEAD)
    p += [("mla_in.0", 4096), ("mla_in.1", 8 * 224), ("mla_uq.0", 2304), ("mla_uq.1", 2304), ("mla_ukv", 4096)]
    p += cols("mla_out", [512] * 2) + with_ada("ffn1", ADA_HEAD + ADA_CARRIED)
    p += swiglu("ffn2", FF_TILES)
    p += [("rwkv_lora1", 8 * 288), ("rwkv_lora2", 4096)]
    p += cols("rwkv_r", [512] * 2) + cols("rwkv_k", [512] * 2) + cols("rwkv_v", [512] * 2)
    p += cols("rwkv_out", [512] * 2) + swiglu("ffn3", FF_TILES)
    p += cols("ab_in", [512] * 6) + [("ab_in.6", 8 * 512), ("ab_gates", 8 * 8)] + cols("ab_out", [512] * 2)
    p += [("router0", 160)] + swiglu("moe0", EXPERTS * E_TILES)
    p += cols("c_in", [512] * 5) + [("c_gates", 8 * 24)]
    p += [("cmp_w1.0", 4096), ("cmp_w1.1", 4096), ("cmp_w1.2", 4096), ("cmp_w1.3", 4096), ("cmp_w2", 512)]
    p += cols("c_out", [512] * 2)
    p += [("router1", 160)] + swiglu("moe1", EXPERTS * E_TILES)
    return p


STREAM = stream_plan()
INDEX = {name: i for i, (name, _) in enumerate(STREAM)}


def by_vector(name):
    return name.startswith(("ada", "ffn", "moe"))


FREED, _n = {}, [0, 0]
for _name, _ in STREAM:
    _n[by_vector(_name)] += 1
    FREED[_name] = _n[by_vector(_name)]

CONST_PLAN = [("ident", P), ("flip", P), ("ones", P), ("rot", 32), ("causal", ATT), ("dilated", ATT),
              ("strict", P), ("incl", P), ("level", 7 * P), ("hsel", KT * 16), ("hselT", KT * P),
              ("dist", 512), ("cmpmask", 2 * NCMP), ("iota", 4), ("eps", 3)]
VEC_PLAN = [("c", 8), ("ada_b", 144), ("norm_g", 48), ("final_g", 8), ("q_norm", 3), ("kv_norm", 2), ("mu", 48),
            ("w0", 8), ("a0", 8), ("k_k", 8), ("k_a", 8), ("r_k", 8), ("gn_w", 8), ("gn_b", 8),
            ("ln_g", 32), ("ln_b", 32), ("conv", 32), ("head_norm", 4), ("cmp_pos", 64), ("rel_bias", 8),
            ("ab_gate_b", 8), ("c_gate_b", 24), ("moe_b", 40)]


def offsets(plan):
    out, at = {}, 0
    for name, n in plan:
        out[name] = (at, n)
        at += n
    return out, at


CONST, NCONST = offsets(CONST_PLAN)
CONST["cos"], CONST["sin"] = (CONST["hselT"][0], T), (CONST["hselT"][0] + T, T)
VEC, NVEC = offsets(VEC_PLAN)


def build(nc, stream, const_d, vec_d, x_d, out_d, bias_scratch):
    with ExitStack() as ctx:
        def sb(name, n):
            return ctx.enter_context(nc.sbuf_tensor(name, [P, n], F32))

        ring = [sb(f"ring{i}", SLOT) for i in range(RING)]
        const = sb("const", NCONST)
        vec = sb("vec", NVEC)
        xT = sb("xT", KT * T)
        hT = sb("hT", KT * T)
        mods = sb("mods", 144)
        cact = sb("cact", 8)
        gain = sb("gain", 8)
        gate = sb("gate", 8)
        small = sb("small", 512)
        zeros = sb("zeros", 512)
        WORK = 26880
        with nc.sbuf_tensor("work", [P, WORK], F32) as work:
            pass
        SW_LOW = 5120
        with ExitStack() as over:
            over.enter_context(nc.sbuf_tensor("work_low", [P, SW_LOW], F32))

            def split(name, n):
                return [over.enter_context(nc.sbuf_tensor(f"{name}_{part}", [P, n], F32R)) for part in ("hi", "lo")]
            w_up = [split(f"w_up{i}", 2048) for i in range(2)]
            w_down = [split(f"w_down{i}", 1024) for i in range(2)]
            x_parts = split("x_part", KT * T)
            hid = [split(f"hid{i}", T) for i in range(2)]
        PS = ctx.enter_context(nc.psum_tensor("PS", [P, 8, 512], F32))

        sems = {}

        def S(name):
            if name not in sems:
                sems[name] = ctx.enter_context(nc.semaphore(name))
            return sems[name]

        slot_full = [S(f"slot_full{i}") for i in range(RING)]
        slot_free = S("slot_free")
        dve_free = S("dve_free")

        def C(name, rows=P, lo=0):
            at, n = CONST[name]
            return const[lo:rows, at:at + n]

        def V(name, i=0, n=1, rows=P):
            at, _ = VEC[name]
            return vec[0:rows, at + i:at + i + n]

        def tiles(ap, n=T):
            return ap.rearrange("p (k t) -> p k t", t=n)

        x3, h3 = tiles(xT[:, :]), tiles(hT[:, :])
        ident = C("ident")
        ones = C("ones")

        def W(at, n, lo=0, hi=P):
            assert at + n <= WORK, (at, n)
            return work[lo:hi, at:at + n]

        U = KT * T

        def unit(i, n=U):
            return W(i * U, n)

        def bank(b, n=512, at=0, lo=0, hi=P):
            return PS[lo:hi, b, at:at + n]

        def out_tile(m):
            return bank(m // 2, T, (m % 2) * T)

        def piece(name):
            return ring[INDEX[name] % RING]

        def arrived(name):
            i = INDEX[name]
            return slot_full[i % RING], 16 * (i // RING + 1)

        class Line:

            def __init__(self, eng, chain):
                self.eng, self.chain, self.added, self.seen = eng, chain, {}, {}

            def done(self, ins, name=None):
                name = name or self.chain
                self.added[name] = self.added.get(name, 0) + 1
                ins.then_inc(S(name), 1)
                self.eng.wait_ge(S(name), self.added[name])

            def next(self, name, k=1):
                self.seen[name] = self.seen.get(name, 0) + k
                self.eng.wait_ge(S(name), self.seen[name])

        mla_items = [dict(h=h, kind="full", first=True, last=True) for h in range(16)]
        ab_items = [dict(h=h, kind="full", first=True, last=True) for h in range(8)]
        c_items = [dict(h=h, kind=k, first=(b == 0), last=(b == 2), branch=b)
                   for h in range(8) for b, k in enumerate(("cmp", "full", "full"))]

        RW_LORA = 9 * U
        RL_AT = ({"AK": 0, "RK": 1024, "X": 2 * U, "XT": 2 * U + 512, "Y": 2 * U + 1024, "MTL": 2 * U + 1536},
                 {"AK": 3 * U, "RK": 3 * U + 1024, "X": 8 * U, "XT": 8 * U + 512, "Y": 8 * U + 1024,
                  "MTL": 8 * U + 1536})
        RB = ({"y": 4, "z": 5, "zt": 6}, {"y": 7, "z": 2, "zt": 3})

        def RL(lane, name):
            return W(RL_AT[lane][name], 1024 if name in ("AK", "RK") else 512)

        M_LAT, M_KR, M_Q, M_K, M_V, M_O, M_TMP, M_ATT = 0, 1280, 1536, 5632, 9728, 11776, 13824, 17920
        A_Q, A_K, A_V, A_BQ, A_BK, A_BV, A_BO, A_RAW, A_BM, A_Y = (
            0, 1024, 2048, 3072, 4096, 5120, 6144, 7168, 9248, 12320)
        A_LS, A_ATT = 14368, 25000
        C_Q, C_KV, C_BM, C_BC, C_CMPB, C_HID, C_KC, C_VC, C_G, C_O = (
            0, 2048, 5120, 8192, 8448, 14400, 10432, 10464, 10720, 10784)
        C_SRC, C_RAW = 4096, 14528
        C_ATT = 12832
        R_AT, R_GT, R_PICK = 8192, 9216, 10240
        ATT_SIZE = 2 * ATT + 2 * ATT + 16

        def att_place(items, base, o_banks=(4, 5)):
            def s(i):
                return W(base + (i % 2) * ATT, ATT)

            def pt(i):
                return W(base + 2 * ATT + (i % 2) * ATT, ATT)

            def stat(i, k):
                return W(base + 4 * ATT + (i % 2) * 8 + 2 * k, 2)
            return s, pt, stat

        def operands(phase, it):
            h = it["h"]
            if phase == "mla":
                q = tiles(W(M_Q, 16 * T, 0, 96))[:, h, :]
                k = tiles(W(M_K, 16 * T, 0, 96))[:, h, :]
                v = W(M_V, 2 * D).rearrange("p (s c) -> p s c", s=2)[:, :, h * 64:(h + 1) * 64]
                lo = 64 * (h % 2)
                o = tiles(W(M_O, U))[lo:lo + 64, h // 2, :]
                return q, k, v, o, lo, 64
            if phase == "ab":
                lo = 64 * (h % 2)
                q = tiles(W(A_Q, 4 * T))[lo:lo + 64, h // 2, :]
                k = tiles(W(A_K, 4 * T))[lo:lo + 64, h // 2, :]
                v = W(A_V, 2 * 512).rearrange("p (s c) -> p s c", s=2)[:, :, h * 64:(h + 1) * 64]
                o = tiles(W(A_Y, U))[lo:lo + 64, h // 2, :]
                return q, k, v, o, lo, 64
            g = h // 4
            q = tiles(W(C_Q, U))[:, h, :]
            o = tiles(W(C_O, U))[:, h, :]
            if it["kind"] == "cmp":
                k = W(C_KC, 2 * NCMP)[:, g * NCMP:(g + 1) * NCMP]
                v = W(C_VC, 2 * P, 0, NCMP).rearrange("p (g c) -> p g c", g=2)[:, g:g + 1, :]
                return q, k, v, o, 0, P
            b = it["branch"]
            k = tiles(W(C_KV + 512 * (b - 1), 2 * T))[:, g, :]
            v = W(C_KV + 1024 + 512 * (b - 1), 4 * P).rearrange("p (s c) -> p s c", s=2)[:, :, g * P:(g + 1) * P]
            return q, k, v, o, 0, P

        def score_bias(phase, it):
            if phase == "mla":
                return C("causal")
            if phase == "ab":
                return W(A_BM + ATT * it["h"], ATT)
            if it["kind"] == "cmp":
                return W(C_BC + 2 * NCMP * it["h"], 2 * NCMP)
            return W(C_BM + ATT * it["h"], ATT)

        SCALE = {"mla": 96 ** -0.5, "ab": 64 ** -0.5, "c": P ** -0.5}
        ITEMS = {"mla": mla_items, "ab": ab_items, "c": c_items}
        IT0 = {"mla": 0, "ab": 16, "c": 24}
        EV0 = {"mla": 0, "ab": 16, "c": 24}
        ABASE = {"mla": M_ATT, "ab": A_ATT, "c": C_ATT}
        SW = {"ffn0": (FF_TILES, 0), "ffn1": (FF_TILES, 22), "ffn2": (FF_TILES, 44), "ffn3": (FF_TILES, 66),
              "moe0": (64, 88), "moe1": (64, 152)}
        SW_SILU, SW_G, SW_ADA = 0, 1024, 1024
        NSQ, NTMP = W(WORK - 2 * U, U), W(WORK - U, U)
        STD, RSTD = small[:, 0:T], small[:, T:2 * T]

        order = ["ffn0", "mla", "ffn1", "ffn2", "rwkv", "ffn3", "final", "ab", "moe0", "c", "moe1"]

        XR = {ph: n for n, ph in enumerate(order)}
        XR["end"] = len(order)

        CARRY = {"ffn0": (ADA_HEAD, ADA_CARRIED), "ffn1": (ADA_HEAD + ADA_CARRIED, ADA_CARRIED)}

        def run_rounds(eng, n, carried, step):
            def straight(lo, hi):
                for j in range(lo, hi):
                    step(j, 0, 0)

            def looped(lo, hi, rate):
                if hi > lo:
                    with eng.Fori(0, (hi - lo) // RING) as r:
                        for j in range(lo, lo + RING):
                            step(j, r, rate)
            straight(0, RING)
            if carried:
                looped(RING, carried, 2)
                straight(carried, carried + RING)
                looped(carried + RING, n // RING * RING, 1)
            else:
                looped(RING, n // RING * RING, 1)
            straight(n // RING * RING, n + 1)

        block = ctx.enter_context(nc.Block())

        @block.sync
        def _(sp):
            def load(i):
                w = STREAM[i][1]
                if i >= RING:
                    old = STREAM[i - RING][0]
                    sp.wait_ge(dve_free if by_vector(old) else slot_free, FREED[old])
                sp.dma_start(ring[i % RING][:, 0:w], stream[i, :, 0:w]).then_inc(slot_full[i % RING], 16)

            def load_run(first, n, period=RING):
                for i in range(first, first + period):
                    load(i)
                rounds = n // period
                with sp.Fori(1, rounds) as r:
                    for j in range(period):
                        i, w = first + j, STREAM[first + j][1]
                        sp.wait_ge(dve_free, r * period + (FREED[STREAM[i][0]] - RING))
                        sp.dma_start(ring[i % RING][:, 0:w],
                                     stream[bass.ds(r * period + i, 1), :, 0:w].rearrange("a p n -> (a p) n")
                                     ).then_inc(slot_full[i % RING], 16)
                for i in range(first + rounds * period, first + n):
                    load(i)

            end = len(STREAM)
            i = 0
            while i < end:
                tag = STREAM[i][0].split(".")[0]
                carried = ADA_CARRIED if STREAM[i][0] in ("ffn0.0", "ffn1.0") else 0
                if carried:
                    load_run(i, 2 * carried, 2 * RING)
                    i += 2 * carried
                    continue
                n = 1
                while i + n < end and STREAM[i + n][0].split(".")[0] == tag and STREAM[i + n][1] == STREAM[i][1]:
                    n += 1
                if n >= 2 * RING:
                    load_run(i, n)
                else:
                    for j in range(i, i + n):
                        load(j)
                i += n
            sp.wait_ge(S("x_ready"), XR["end"])
            sp.dma_start(out_d[:, :], xT[:, :]).then_inc(S("out_stored"), 16)
            sp.wait_ge(S("out_stored"), 16)

        def piece_cols(name, k, lo, n, width=512):
            return piece(name)[:, k * width + lo:k * width + lo + n]

        @block.tensor
        def _(pe):
            mm = nc.tensor.matmul
            line = Line(pe, "pe_chain")

            def take(name):
                sem, value = arrived(name)
                pe.wait_ge(sem, value)

            def sums(parts, at=0, name="ss_ready"):
                for i, ap in enumerate(parts):
                    last = mm(bank(7, T, at), ones, ap, start=(i == 0), stop=(i == len(parts) - 1))
                last.then_inc(S(name), 1)

            def norm_sums():
                line.next("sq_ready")
                sq = tiles(NSQ)
                sums([sq[:, k, :] for k in range(KT)])

            def layer_norm_sums():
                line.next("pre_ready")
                sums([x3[:, k, :] for k in range(KT)], name="mean_ready")
                line.next("sq_ready")
                sq = tiles(NSQ)
                sums([sq[:, k, :] for k in range(KT)])

            def ada_sum(p, b, count):
                pe.wait_ge(S("ada_part"), count)
                z = W(SW_ADA + 512 * (p % 2), 512)
                for m in range(4):
                    last = mm(bank(b + p % 2, 4)[:, m:m + 1], z[:, m * P:(m + 1) * P], ones[:, 0:1], start=True,
                              stop=True)
                last.then_inc(S("ada_sum"), 1)

            def ada(lo, hi):
                for p in range(lo, hi):
                    ada_sum(p, 6, p + 1)
                pe.wait_ge(S("ada_read"), hi)

            def swiglu(tag):
                n, base = SW[tag]
                line.next("x_split")

                def products(out, w, lo, x, at, start, stop, skip=False):
                    for i, (a, b) in enumerate(((0, 0), (0, 1), (1, 0))):
                        last = mm(out, w[a][:, lo:lo + P], x[b][:, at:at + T], start=start and i == 0,
                                  stop=stop and i == 2, skip_group_check=skip)
                    return last

                def up(j, wait_w):
                    pe.wait_ge(S("up_split"), wait_w)
                    for half in range(2):
                        for k in range(KT):
                            last = products(bank(4 + j % 2, T, half * T), w_up[j % 2], k * 256 + half * P, x_parts,
                                            k * T, k == 0, k == KT - 1)
                    last.then_inc(S("gu_ready"), 1)

                def down(j, wait_hid, wait_w):
                    pe.wait_ge(S("hid_ready"), wait_hid)
                    pe.wait_ge(dve_free, wait_w)
                    for m in range(KT):
                        last = products(out_tile(m), w_down[j % 2], m * P, hid[j % 2], 0, False, False, True)
                    last.then_inc(S("down_done"), 1)

                for b in range(4):
                    mm(bank(b), zeros[0:1, 0:P], zeros[0:1, 0:512], start=True, stop=False, skip_group_check=True)

                p0, carried = CARRY.get(tag, (0, 0))

                def step(j, r, rate):
                    if j < n:
                        up(j, r * RING + (base + j + 1))
                    if j >= 1:
                        down(j - 1, r * RING + (base + j), r * (RING * rate) + FREED[f"{tag}.{j - 1}"])
                    if 0 <= j - 1 < carried:
                        p = p0 + j - 1
                        ada_sum(p, 6, r * RING + (p + 1))
                run_rounds(pe, n, carried, step)
                if carried:
                    pe.wait_ge(S("ada_read"), p0 + carried)

            def project(name, i0, rhs, mtiles, width=512, lo=0, rows=P, free=True):
                for j, m in enumerate(mtiles):
                    for k in range(KT):
                        last = mm(bank(m // 2, T, (m % 2) * T, 0, rows), piece_cols(name, k, lo + j * P, rows, width),
                                  rhs[:, k, :], start=(k == 0), stop=(k == KT - 1))
                if free:
                    last.then_inc(slot_free, 1)
                return last

            def out_proj(tag, src):
                for i in range(2):
                    take(f"{tag}.{i}")
                    project(f"{tag}.{i}", i, src, range(4 * i, 4 * i + 4))

            def attention(phase):
                items, base, ev0 = ITEMS[phase], IT0[phase], EV0[phase]
                s_of, pt_of, _ = att_place(items, ABASE[phase])
                n = len(items)

                def scores(i):
                    q, k, v, o, lo, dv = operands(phase, items[i])
                    b = i % 2
                    if items[i]["kind"] == "cmp":
                        for tt in range(2):
                            last = mm(bank(b, NCMP, tt * NCMP), q[:, tt * P:(tt + 1) * P], k, start=True, stop=True)
                    else:
                        mm(bank(b, P), q[:, 0:P], k[:, 0:P], start=True, stop=True)
                        last = mm(bank(b, T, P), q[:, P:T], k, start=True, stop=True)
                    last.then_inc(S("score_ready"), 1)

                def turn(i):
                    pe.wait_ge(S("prob_ready"), base + i + 1)
                    b, pr = 2 + i % 2, s_of(i)
                    if items[i]["kind"] == "cmp":
                        for tt in range(2):
                            last = nc.tensor.transpose(bank(b, P, tt * P, 0, NCMP), pr[:, tt * NCMP:(tt + 1) * NCMP],
                                                       ident)
                    else:
                        for c in range(3):
                            last = nc.tensor.transpose(bank(b, P, c * P), pr[:, c * P:(c + 1) * P], ident)
                    last.then_inc(S("turned"), 1)

                def values(i):
                    pe.wait_ge(S("pt_ready"), base + i + 1)
                    it = items[i]
                    q, k, v, o, lo, dv = operands(phase, it)
                    b = 4 + it["h"] % 2
                    if it["first"] and it["h"] >= 2:
                        pe.wait_ge(S("att_out"), ev0 + it["h"] - 1)
                    pt = pt_of(i)
                    if it["kind"] == "cmp":
                        last = mm(bank(b, T, 0, lo, lo + dv), v[:, 0, :], pt[0:NCMP, 0:T], start=it["first"],
                                  stop=it["last"])
                    else:
                        mm(bank(b, T, 0, lo, lo + dv), v[:, 0, :], pt[:, 0:T], start=it["first"], stop=False)
                        last = mm(bank(b, P, P, lo, lo + dv), v[:, 1, :], pt[:, T:T + P], start=False,
                                  stop=it["last"])
                    last.then_inc(S("pv_ready"), 1)

                for step in range(n + 2):
                    if step < n:
                        scores(step)
                    if 1 <= step <= n:
                        turn(step - 1)
                    if step >= 2:
                        values(step - 2)

            def mla():
                norm_sums()
                line.next("h_ready")
                take("mla_in.0")
                project("mla_in.0", 0, h3, range(0, 4))
                take("mla_in.1")
                project("mla_in.1", 0, h3, [4], width=224, free=False)
                last = project("mla_in.1", 0, h3, [5], width=224, lo=P, rows=96)
                lat = tiles(W(M_LAT, 5 * T))
                line.next("lat_sq_ready")
                sq = tiles(W(M_TMP, 5 * T))
                for i in range(3):
                    mm(bank(7, T), ones, sq[:, i, :], start=(i == 0), stop=(i == 2))
                for i in range(2):
                    last = mm(bank(7, T, T), ones, sq[:, 3 + i, :], start=(i == 0), stop=(i == 1))
                last.then_inc(S("ss_ready"), 1)
                line.next("lat_ready")
                for half in range(2):
                    name = f"mla_uq.{half}"
                    take(name)
                    for h in range(8):
                        for k in range(3):
                            last = mm(bank(4 * half + h // 2, T, (h % 2) * T, 0, 96),
                                      piece(name)[:, k * 768 + h * 96:k * 768 + (h + 1) * 96], lat[:, k, :],
                                      start=(k == 0), stop=(k == 2))
                    last.then_inc(slot_free, 1)
                take("mla_ukv")
                for half in range(2):
                    line.next("q_copied")
                    for h in range(8):
                        for k in range(2):
                            c = k * D + (8 * half + h) * 64
                            last = mm(bank(4 * half + h // 2, T, (h % 2) * T, 0, 64), piece("mla_ukv")[:, c:c + 64],
                                      lat[:, 3 + k, :], start=(k == 0), stop=(k == 1))
                    last.then_inc(S("k_ready"), 1)
                line.next("k_copied")
                for tt in range(2):
                    for c in range(2):
                        for k in range(2):
                            at = 2 * D + k * D + c * 512
                            last = mm(bank(2 * tt + c), lat[:, 3 + k, tt * P:(tt + 1) * P],
                                      piece("mla_ukv")[:, at:at + 512], start=(k == 0), stop=(k == 1))
                last.then_inc(slot_free, 1)
                line.next("k_copied")
                rot = const[64:96, CONST["rot"][0]:CONST["rot"][0] + 32]
                qr = W(M_Q, 16 * T, 64, 96)
                for g in range(4):
                    last = mm(bank(4 + g, 512, 0, 64, 96), rot, qr[:, g * 512:(g + 1) * 512], start=True, stop=True)
                last.then_inc(S("rot_ready"), 1)
                line.next("v_copied")
                for g in range(4):
                    last = mm(bank(g, 512, 0, 64, 96), rot, qr[:, (4 + g) * 512:(5 + g) * 512], start=True, stop=True)
                last.then_inc(S("rot_ready"), 1)
                line.next("rot_read")
                mm(bank(4, T, 0, 64, 96), rot, W(M_KR, T, 64, 96), start=True,
                   stop=True).then_inc(S("rot_ready"), 1)
                line.next("qk_ready")
                attention("mla")
                pe.wait_ge(S("att_out"), 16)
                out_proj("mla_out", tiles(W(M_O, U)))

            BODY = {}
            BODY["mla"] = mla
            def head_sums(src):
                sel = C("hsel").rearrange("p (k h) -> p k h", h=16)
                s3 = tiles(src)
                for k in range(KT):
                    last = mm(bank(7, T, 0, 0, 16), sel[:, k, :], s3[:, k, :], start=(k == 0), stop=(k == KT - 1))
                last.then_inc(S("hs_ready"), 1)

            def head_spread():
                line.next("hb_in")
                at = CONST["hselT"][0]
                for k in range(KT):
                    last = mm(out_tile(k), const[0:16, at + k * P:at + (k + 1) * P], small[0:16, T:2 * T],
                              start=True, stop=True)
                last.then_inc(S("hb_ready"), 1)

            def rwkv():
                norm_sums()
                line.next("h_ready")
                take("rwkv_lora1")
                w1 = piece("rwkv_lora1")
                xs = [tiles(unit(1)), tiles(unit(2))]

                def low(c0, n, b, x):
                    for k in range(KT):
                        last = mm(bank(b, T, 0, 0, n), w1[:, k * 288 + c0:k * 288 + c0 + n], x[:, k, :],
                                  start=(k == 0), stop=(k == KT - 1))
                    return last
                line.next("xs_ready")
                low(0, 64, 0, xs[0]).then_inc(S("xs_used"), 1)
                line.next("xs_ready")
                low(64, 64, 1, xs[1]).then_inc(S("xs_used"), 1)
                line.next("xs_ready")
                low(128, P, 2, xs[0])
                low(256, 32, 3, xs[0]).then_inc(slot_free, 1)
                take("rwkv_lora2")
                w2 = piece("rwkv_lora2")
                la = RW_LORA
                line.next("lora_act")
                for m in range(KT):
                    last = mm(out_tile(8 + m), w2[0:64, m * P:(m + 1) * P], W(la, T, 0, 64), start=True, stop=True)
                last.then_inc(S("lora2_ready"), 1)
                line.next("lora_act", 2)
                for m in range(KT):
                    last = mm(out_tile(m), w2[0:64, D + m * P:D + (m + 1) * P], W(la + T, T, 0, 64), start=True,
                              stop=True)
                last.then_inc(S("lora2_ready"), 1)
                line.next("proj_copied")
                for m in range(KT):
                    mm(out_tile(8 + m), w2[:, 2 * D + m * P:2 * D + (m + 1) * P], W(la + 2 * T, T), start=True,
                       stop=False)
                    last = mm(out_tile(8 + m), w2[0:32, 3 * D + m * P:3 * D + (m + 1) * P], W(la + 3 * T, T, 0, 32),
                              start=False, stop=True)
                last.then_inc(slot_free, 1)
                for n, (tag, b0) in enumerate((("rwkv_r", 0), ("rwkv_k", 8), ("rwkv_v", 0))):
                    line.next("proj_copied")
                    line.next("xs_ready")
                    for i in range(2):
                        take(f"{tag}.{i}")
                        project(f"{tag}.{i}", i, xs[(n + 1) % 2], range(b0 + 4 * i, b0 + 4 * i + 4))
                line.next("proj_copied", 2)
                line.next("hs_in")
                head_sums(unit(9))
                head_spread()
                line.next("hs_in_dve")
                head_sums(unit(9))
                head_spread()
                line.next("tilde_ready")
                for n, (u, tts, b0) in enumerate(((8, (0, 1), 4), (4, (0,), 0), (7, (0,), 2))):
                    src = tiles(unit(u))
                    for tt in tts:
                        for k in range(KT):
                            last = nc.tensor.transpose(bank(b0 + 2 * tt + k // 4, P, (k % 4) * P),
                                                       src[:, k, tt * P:(tt + 1) * P], ident)
                    last.then_inc(S("tok_ready"), 1)
                line.next("tok_copied", 3)
                til = {n: tiles(unit(u)) for n, u in (("a", 1), ("r", 6), ("b", 4), ("k", 7))}
                vtok = unit(9).rearrange("p (s c) -> p s c", s=2)
                btok, ktok, spad = W(10 * U, 1024), W(11 * U, 1024), W(10 * U + 1024, 1024)
                for tt in range(2):
                    ts = slice(tt * P, (tt + 1) * P)
                    for pair in range(2):
                        lanes = [(ln, 2 * pair + ln) for ln in range(2)]
                        if tt or pair:
                            line.next("yt_copied", 2)
                            if tt == 0 or pair == 0:
                                line.next("s_copied", 2)
                        for ln, q in lanes:
                            for j in range(4):
                                lo, k, h2 = 64 * (j % 2), 2 * q + j // 2, j // 2
                                for o, (l, r) in enumerate((("b", "a"), ("k", "a"), ("b", "r"), ("k", "r"))):
                                    last = mm(bank(4 * ln + 2 * (j % 2) + o // 2, P, (o % 2) * T + h2 * P),
                                              til[l][lo:lo + 64, k, ts], til[r][lo:lo + 64, k, ts], start=True,
                                              stop=True)
                            last.then_inc(S("pair_scores"), 1)
                        for ln, q in lanes:
                            line.next("xt_ready")
                            xt = RL(ln, "XT")
                            for c in range(4):
                                last = nc.tensor.transpose(bank(RB[ln]["y"], P, c * P), xt[:, c * P:(c + 1) * P], ident)
                            last.then_inc(S("x1_ready"), 1)
                        line.next("lvl_ready", 2)
                        for lvl in range(1, 7):
                            for ln, q in lanes:
                                line.next("lvl_ready")
                                line.next("x_copied" if lvl == 1 else "x_upd")
                                mt, x = RL(ln, "MTL"), RL(ln, "X")
                                for c in range(4):
                                    last = mm(bank(RB[ln]["y"], P, c * P), mt[:, c * P:(c + 1) * P],
                                              x[:, c * P:(c + 1) * P], start=True, stop=True)
                                last.then_inc(S("y_ready"), 1)
                            for ln, q in lanes:
                                line.next("y_copied")
                                y, xt = RL(ln, "Y"), RL(ln, "XT")
                                if lvl < 6:
                                    for c in range(4):
                                        mm(bank(RB[ln]["z"], P, c * P), xt[:, c * P:(c + 1) * P],
                                           y[:, c * P:(c + 1) * P], start=True, stop=True)
                                for c in range(4):
                                    last = mm(bank(RB[ln]["zt"], P, c * P), y[:, c * P:(c + 1) * P],
                                              xt[:, c * P:(c + 1) * P], start=True, stop=True)
                                last.then_inc(S("z_ready"), 1)
                        for ln, q in lanes:
                            for j in range(4):
                                h, k, c = 4 * q + j, 2 * q + j // 2, (j % 2) * 2 + j // 2
                                ka = RL(ln, "AK")[:, (j % 2) * 512 + T + (j // 2) * P:][:, 0:P]
                                last = mm(bank(ln, 64, c * 64), ka, vtok[:, tt, h * 64:(h + 1) * 64], start=True,
                                          stop=(tt == 0))
                                if tt:
                                    last = mm(bank(ln, 64, c * 64), til["a"][:, k, ts], spad[:, h * 64:(h + 1) * 64],
                                              start=False, stop=True)
                            last.then_inc(S("t1_ready"), 1)
                        for ln, q in lanes:
                            line.next("t1_copied")
                            line.next("x_upd")
                            xt, y = RL(ln, "XT"), RL(ln, "Y")
                            for c in range(4):
                                last = mm(bank(ln, 64, T + c * 64), xt[:, c * P:(c + 1) * P], y[:, c * 64:(c + 1) * 64],
                                          start=True, stop=True)
                            last.then_inc(S("u_ready"), 1)
                        for ln, q in lanes:
                            line.next("u_copied")
                            y = RL(ln, "Y")
                            for j in range(4):
                                if tt:
                                    break
                                h, k, c = 4 * q + j, 2 * q + j // 2, (j % 2) * 2 + j // 2
                                mm(bank(RB[ln]["zt"], 64, j * 64), btok[:, k * P:(k + 1) * P],
                                   y[:, T + c * 64:T + (c + 1) * 64], start=True, stop=False)
                                last = mm(bank(RB[ln]["zt"], 64, j * 64), ktok[:, k * P:(k + 1) * P],
                                          vtok[:, 0, h * 64:(h + 1) * 64], start=False, stop=True)
                            if tt == 0:
                                last.then_inc(S("s_ready"), 1)
                            for j in range(4):
                                h, k, c, lo = 4 * q + j, 2 * q + j // 2, (j % 2) * 2 + j // 2, 64 * (j % 2)
                                br = RL(ln, "RK")[:, (j % 2) * 512 + (j // 2) * P:][:, 0:P]
                                kr = RL(ln, "RK")[:, (j % 2) * 512 + T + (j // 2) * P:][:, 0:P]
                                o = bank(RB[ln]["z"], P, (j // 2) * P, lo, lo + 64)
                                mm(o, vtok[:, tt, h * 64:(h + 1) * 64], kr, start=True, stop=False)
                                if tt:
                                    mm(o, spad[:, h * 64:(h + 1) * 64], til["r"][:, k, ts], start=False, stop=False)
                                last = mm(o, y[:, T + c * 64:T + (c + 1) * 64], br, start=False, stop=True)
                            last.then_inc(S("yt_ready"), 1)
                line.next("yt_copied", 2)
                head_sums(unit(12))
                head_spread()
                line.next("hs_in")
                head_sums(unit(9))
                head_spread()
                line.next("mix_ready")
                out_proj("rwkv_out", tiles(unit(12)))

            BODY["rwkv"] = rwkv

            def row_bias(out, name, at, n):
                a = VEC[name][0] + at
                return mm(out, ones[0:1, :], vec[0:1, a:a + n], start=False, stop=True)

            def by_token(name, b0, lo, n, width=512, step=None, bias=None):
                for tt in range(2):
                    o = bank(b0 + tt, n) if step is None else bank(b0, n, tt * step)
                    for k in range(KT):
                        last = mm(o, x3[:, k, tt * P:(tt + 1) * P], piece_cols(name, k, lo, n, width),
                                  start=(k == 0), stop=(k == KT - 1 and bias is None))
                    if bias is not None:
                        last = row_bias(o, bias[0], bias[1], n)
                return last

            def flip_bias(at, landed):
                pe.wait_ge(S("bias_in"), landed)
                for b in range(6):
                    last = mm(bank(b), C("flip"), W(at + b * 512, 512), start=True, stop=True)
                last.then_inc(S("bias_flipped"), 1)
                line.next("bias_used")

            def ab():
                pe.wait_ge(S("x_ready"), XR["ab"])
                mm(bank(7, 512, 0, 0, 8), V("rel_bias", 0, 8, 32), C("dist", 32), start=True,
                   stop=True).then_inc(S("bias_ready"), 1)
                for i in range(7):
                    name = f"ab_in.{i}"
                    take(name)
                    if i == 3:
                        pe.wait_ge(S("bias_copied"), 1)
                    if i >= 4:
                        pe.wait_ge(S("ab_copied"), i - 3)
                    if i in (2, 5):
                        by_token(name, (2 * i) % 8, 0, 512).then_inc(slot_free, 1)
                    else:
                        project(name, i, x3, range((4 * i) % 16, (4 * i) % 16 + 4))
                take("ab_gates")
                pe.wait_ge(S("ab_copied"), 4)
                by_token("ab_gates", 6, 0, 8, 8, 8, ("ab_gate_b", 0)).then_inc(slot_free, 1)
                pe.wait_ge(S("ab_copied"), 7)
                flip_bias(A_BM, 32)
                attention("ab")
                def ls(at, n, hi=P):
                    return W(A_LS + at, n, 0, hi)
                line.next("lf_ready")
                lf = ls(16, 8)
                mm(bank(6, 8), C("incl"), lf, start=True, stop=True)
                mm(bank(6, 8, 8), ones, lf, start=True, stop=True).then_inc(S("cumsum_ready"), 1)
                line.next("diag_ready")
                dd = ls(256, 1024)
                for tt in range(2):
                    last = mm(bank(7 if tt else 2), ones, dd[:, tt * 512:(tt + 1) * 512], start=True, stop=True)
                last.then_inc(S("rowbc_ready"), 1)
                pe.wait_ge(S("bqk_ready"), 1)
                q, k = tiles(W(A_BQ, 1024)), tiles(W(A_BK, 1024))
                for tt in range(2):
                    for h in range(4):
                        last = mm(bank(tt, P, h * P), q[:, h, tt * P:(tt + 1) * P], k[:, h, tt * P:(tt + 1) * P],
                                  start=True, stop=True)
                last.then_inc(S("lqk_ready"), 1)
                for h in range(4):
                    last = nc.tensor.transpose(bank(3, P, h * P), k[:, h, 0:P], ident)
                last.then_inc(S("ktok_ready"), 1)
                line.next("lprob_ready")
                ss, st = ls(1280, 1024), ls(2304, 1024)
                for i in range(8):
                    last = nc.tensor.transpose(bank(4 + i // 4, P, (i % 4) * P), ss[:, i * P:(i + 1) * P], ident)
                last.then_inc(S("lturned"), 1)
                bv = W(A_BV, 1024).rearrange("p (s c) -> p s c", s=2)
                kw, cc, nn = ls(3328, 512), ls(3840, 512), ls(104, 4)
                line.next("kw_ready")
                for h in range(4):
                    mm(bank(7, P, h * P), kw[:, h * P:(h + 1) * P], bv[:, 0, h * P:(h + 1) * P], start=True, stop=True)
                for h in range(4):
                    last = mm(bank(6, 1, 16 + h), kw[:, h * P:(h + 1) * P], ones[:, 0:1], start=True, stop=True)
                last.then_inc(S("state_ready"), 1)
                line.next("lt_copied")
                for tt in range(2):
                    for h in range(4):
                        last = mm(bank(tt, P, h * P), st[:, (4 * tt + h) * P:(4 * tt + h + 1) * P],
                                  bv[:, tt, h * P:(h + 1) * P], start=True, stop=True)
                last.then_inc(S("lnum_ready"), 1)
                line.next("state_copied")
                for h in range(4):
                    mm(bank(2, P, h * P), q[:, h, P:T], cc[:, h * P:(h + 1) * P], start=True, stop=True)
                for h in range(4):
                    last = mm(bank(6, 1, 32 + h), q[:, h, P:T], nn[:, h:h + 1], start=True, stop=True)
                last.then_inc(S("linter_ready"), 1)
                line.next("lnormed")
                hh = ls(4352, 1024)
                for tt in range(2):
                    for h in range(4):
                        last = nc.tensor.transpose(bank(4 + h // 2, P, (h % 2) * T + tt * P),
                                                   hh[:, (4 * tt + h) * P:(4 * tt + h + 1) * P], ident)
                last.then_inc(S("lout_ready"), 1)
                line.next("mix_ready")
                pe.wait_ge(S("att_out"), 24)
                out_proj("ab_out", tiles(W(A_Y, U)))
                layer_norm_sums()

            def moe(l):
                def run():
                    ph = f"moe{l}"
                    pe.wait_ge(S("x_ready"), XR[ph])
                    take(f"router{l}")
                    by_token(f"router{l}", 7, 0, 20, 20, 20, ("moe_b", 20 * l)).then_inc(slot_free, 1)
                    line.next("gates_ready")
                    g = W(R_AT, 32)
                    for tt in range(2):
                        last = nc.tensor.transpose(bank(7, P, tt * P, 0, 16), g[:, tt * 16:(tt + 1) * 16], ident)
                    last.then_inc(S("gates_turned"), 1)
                    line.next("gates_copied")
                    line.next("pick_ready")
                    gt, pick = W(R_GT, T, 0, 16), tiles(W(R_PICK, 2048, 0, 16), P)
                    for half in range(2):
                        for e in range(8):
                            last = mm(out_tile(8 * half + e), pick[:, 8 * half + e, :], gt, start=True, stop=True)
                        last.then_inc(S("spread_ready"), 1)
                    line.next("g_copied", 2)
                    swiglu(ph)
                    layer_norm_sums()
                return run

            def c():
                pe.wait_ge(S("x_ready"), XR["c"])
                for i in range(5):
                    name = f"c_in.{i}"
                    take(name)
                    if i < 3:
                        project(name, i, x3, range(4 * i, 4 * i + 4))
                    else:
                        if i == 4:
                            pe.wait_ge(S("c_copied"), 1)
                        b = 6 if i == 3 else 0
                        project(name, i, x3, [2 * b, 2 * b + 1], free=False)
                        by_token(name, b + 1, T, T, 512, T).then_inc(slot_free, 1)
                take("c_gates")
                pe.wait_ge(S("c_copied"), 2)
                by_token("c_gates", 2, 0, 24, 24, 24, ("c_gate_b", 0)).then_inc(slot_free, 1)
                pe.wait_ge(S("c_copied"), 4)
                line.next("cmpb_ready")
                for kv in range(2):
                    b3 = W(C_CMPB + 960 * kv, 960).rearrange("p (i n) -> p i n", n=2 * NCMP)
                    for half in range(2):
                        name = f"cmp_w1.{2 * kv + half}"
                        take(name)
                        for i in range(16):
                            last = mm(bank(4 + 2 * kv, T, T, 0, 2 * NCMP), b3[:, 16 * half + i, :],
                                      piece(name)[:, i * T:(i + 1) * T], start=(half == 0 and i == 0),
                                      stop=(half == 1 and i == 15))
                        last.then_inc(slot_free, 1)
                for kv in range(2):
                    line.next("cmp_raw")
                    for m in range(2):
                        last = nc.tensor.transpose(bank(4 + 2 * kv + m, 2 * NCMP),
                                                   W(C_RAW + kv * T + m * P, P, 0, 2 * NCMP),
                                                   ident[0:2 * NCMP, 0:2 * NCMP])
                last.then_inc(S("cmp_turned"), 1)
                take("cmp_w2")
                w2 = piece("cmp_w2").rearrange("p (a n) -> p a n", n=P)
                line.next("hid_gelu")
                hid = W(C_HID, 120).rearrange("p (a n) -> p a n", n=2 * NCMP)
                for m in range(2):
                    mm(bank(3, 2 * NCMP), w2[:, m, :], hid[:, m, :], start=(m == 0), stop=(m == 1))
                for g in range(2):
                    for m in range(2):
                        last = mm(bank(3, P, P + g * P, 0, NCMP), hid[:, 2 + m, g * NCMP:(g + 1) * NCMP], w2[:, 2 + m, :],
                                  start=(m == 0), stop=(m == 1))
                last.then_inc(slot_free, 1)
                pe.wait_ge(S("cmp_copied"), 1)
                pe.wait_ge(S("c_copied"), 6)
                flip_bias(C_BM, 64)
                attention("c")
                pe.wait_ge(S("att_out"), 32)
                out_proj("c_out", tiles(W(C_O, U)))
                layer_norm_sums()

            BODY.update(ab=ab, moe0=moe(0), c=c, moe1=moe(1))
            for ph in order:
                if ph == "ffn0":
                    pe.wait_ge(S("const_in"), 32)
                    ada(0, ADA_HEAD)
                    pe.wait_ge(S("zeroed"), 1)
                if ph.startswith("ffn"):
                    norm_sums()
                    line.next("h_ready")
                    swiglu(ph)
                elif ph == "final":
                    norm_sums()
                else:
                    BODY[ph]()

        @block.scalar
        def _(act):
            fn = nc.scalar.activation
            line = Line(act, "act_chain")
            act.dma_start(vec[:, :], vec_d[:, :]).then_inc(S("vec_in"), 16)
            act.dma_start(const[:, :], const_d[:, :]).then_inc(S("const_in"), 16)
            act.dma_start(xT[:, :], x_d[:, :]).then_inc(S("const_in"), 16)
            act.wait_ge(S("vec_in"), 16)
            fn(cact[:, :], V("c", 0, 8), ACT.Silu).then_inc(S("cact_ready"), 1)
            act.wait_ge(S("const_in"), 32)

            def eps(i):
                return C("eps")[:, i:i + 1]

            def rms(ph):
                if XR[ph]:
                    act.wait_ge(S("x_ready"), XR[ph])
                fn(NSQ, xT[:, :], ACT.Square).then_inc(S("sq_ready"), 1)
                line.next("ss_ready")
                fn(STD, bank(7, T), ACT.Sqrt, bias=eps(0), scale=1.0 / D).then_inc(S("std_ready"), 1)

            def layer_norm():
                line.next("centred")
                fn(NSQ, xT[:, :], ACT.Square).then_inc(S("sq_ready"), 1)
                line.next("ss_ready")
                fn(STD, bank(7, T), ACT.Sqrt, bias=eps(1), scale=1.0 / D).then_inc(S("std_ready"), 1)

            def swiglu(tag, source):
                n, base = SW[tag]
                fn(x_parts[0][:, :], source, ACT.Copy).then_inc(S("x_rounded"), 1)

                def up_high(j, wait_full, wait_up):
                    s = INDEX[f"{tag}.{j}"] % RING
                    act.wait_ge(slot_full[s], wait_full)
                    if wait_up is not None:
                        act.wait_ge(S("gu_ready"), wait_up)
                    fn(w_up[j % 2][0][:, :], ring[s][:, 0:2048], ACT.Copy).then_inc(S("up_rounded"), 1)

                def silu(j, wait_gu, wait_hid):
                    act.wait_ge(S("gu_ready"), wait_gu)
                    if wait_hid is not None:
                        act.wait_ge(S("hid_ready"), wait_hid)
                    fn(W(SW_SILU + (j % 2) * T, T), bank(4 + j % 2, T), ACT.Silu).then_inc(S("silu_ready"), 1)

                def down_high(j, wait_down):
                    if wait_down is not None:
                        act.wait_ge(S("down_done"), wait_down)
                    fn(w_down[j % 2][0][:, :], piece(f"{tag}.{j}")[:, 2048:3072],
                       ACT.Copy).then_inc(S("down_rounded"), 1)

                carried = CARRY.get(tag, (0, 0))[1]

                def step(j, r, rate):
                    if j < n:
                        i = INDEX[f"{tag}.{j}"]
                        up_high(j, r * (16 * rate) + 16 * (i // RING + 1),
                                r * RING + (base + j - 1) if base + j >= 2 else None)
                    if j >= 1:
                        silu(j - 1, r * RING + (base + j), r * RING + (base + j - 2) if base + j > 2 else None)
                    if j < n:
                        down_high(j, r * RING + (base + j - 1) if base + j > 1 else None)
                run_rounds(act, n, carried, step)

            def attention(phase):
                items, base, ev0 = ITEMS[phase], IT0[phase], EV0[phase]
                s_of, pt_of, stat = att_place(items, ABASE[phase])
                n = len(items)

                def exps(i):
                    act.wait_ge(S("max_ready"), base + i + 1)
                    s = s_of(i)
                    w = (NCMP, 2 * NCMP) if items[i]["kind"] == "cmp" else (P, ATT)
                    for tt, (lo, hi) in enumerate(((0, w[0]), w)):
                        last = fn(s[:, lo:hi], s[:, lo:hi], ACT.Exp, bias=stat(i, 0)[:, tt:tt + 1],
                                  accum_out=stat(i, 1)[:, tt:tt + 1])
                    last.then_inc(S("exp_ready"), 1)

                def copy_turned(i):
                    act.wait_ge(S("turned"), base + i + 1)
                    if i >= 2:
                        act.wait_ge(S("pv_ready"), base + i - 1)
                    n_, hi = (T, NCMP) if items[i]["kind"] == "cmp" else (ATT, P)
                    fn(pt_of(i)[0:hi, 0:n_], bank(2 + i % 2, n_, 0, 0, hi), ACT.Copy).then_inc(S("pt_ready"), 1)

                def output(i):
                    it = items[i]
                    if not it["last"]:
                        return
                    act.wait_ge(S("pv_ready"), base + i + 1)
                    _, _, _, o, lo, dv = operands(phase, it)
                    line.done(fn(o, bank(4 + it["h"] % 2, T, 0, lo, lo + dv), ACT.Copy), "att_out")

                for step in range(n + 2):
                    if step < n:
                        exps(step)
                    if 1 <= step <= n:
                        copy_turned(step - 1)
                    if step >= 2:
                        output(step - 2)

            def mla():
                rms("mla")
                line.next("h_ready")
                line.next("lat_copied")
                fn(W(M_TMP, 5 * T), W(M_LAT, 5 * T), ACT.Square).then_inc(S("lat_sq_ready"), 1)
                line.next("ss_ready")
                fn(W(M_TMP + 1536, T), bank(7, T), ACT.Sqrt, bias=eps(0), scale=1.0 / 384)
                fn(W(M_TMP + 1536 + T, T), bank(7, T, T), ACT.Sqrt, bias=eps(0),
                   scale=1.0 / 256).then_inc(S("std_ready"), 1)
                q = W(M_Q, 16 * T, 0, 96)
                for half in range(2):
                    act.wait_ge(slot_free, FREED[f"mla_uq.{half}"])
                    fn(q[:, half * 2048:(half + 1) * 2048], PS[0:96, 4 * half:4 * half + 4, :].rearrange(
                        "p b t -> p (b t)"), ACT.Copy).then_inc(S("q_copied"), 1)
                k = W(M_K, 16 * T, 0, 64)
                for half in range(2):
                    line.next("k_ready")
                    fn(k[:, half * 2048:(half + 1) * 2048], PS[0:64, 4 * half:4 * half + 4, :].rearrange(
                        "p b t -> p (b t)"), ACT.Copy).then_inc(S("k_copied"), 1)
                act.wait_ge(slot_free, FREED["mla_ukv"])
                fn(W(M_V, 2 * D), PS[:, 0:4, :].rearrange("p b t -> p (b t)"), ACT.Copy).then_inc(S("v_copied"), 1)
                attention("mla")

            BODY = {"mla": mla}
            def head_sqrt(scale, bias):
                src = bank(7, T, 0, 0, 16) if bias is not None else small[0:16, T:2 * T]
                fn(small[0:16, T:2 * T], src, ACT.Sqrt, scale=scale,
                   **({"bias": bias} if bias is not None else {})).then_inc(S("hstd_ready"), 1)

            def rwkv():
                rms("rwkv")
                line.next("h_ready")
                la = RW_LORA
                act.wait_ge(S("xs_used"), 1)
                fn(W(la, T, 0, 64), bank(0, T, 0, 0, 64), ACT.Tanh).then_inc(S("lora_act"), 1)
                act.wait_ge(S("xs_used"), 2)
                fn(W(la + T, T, 0, 64), bank(1, T, 0, 0, 64), ACT.Copy).then_inc(S("lora_act"), 1)
                act.wait_ge(slot_free, FREED["rwkv_lora1"])
                fn(W(la + 2 * T, T), bank(2, T), ACT.Sigmoid)
                fn(W(la + 3 * T, T, 0, 32), bank(3, T, 0, 0, 32), ACT.Sigmoid).then_inc(S("lora_act"), 1)
                for u, name, b0 in ((3, "w0", 8), (4, "a0", 0)):
                    line.next("lora2_ready")
                    for m in range(KT):
                        last = fn(tiles(unit(u))[:, m, :], out_tile(b0 + m), ACT.Sigmoid, bias=V(name, m))
                    last.then_inc(S("proj_copied"), 1)
                for u, name, b0 in ((5, "rwkv_lora2", 4), (6, "rwkv_r.1", 0), (7, "rwkv_k.1", 4), (8, "rwkv_v.1", 0)):
                    act.wait_ge(slot_free, FREED[name])
                    fn(unit(u), PS[:, b0:b0 + 4, :].rearrange("p b t -> p (b t)"),
                       ACT.Copy).then_inc(S("proj_copied"), 1)
                line.next("kk_ready")
                fn(unit(9), unit(1), ACT.Square).then_inc(S("hs_in"), 1)
                line.next("hmax_ready")
                head_sqrt(1.0, None)
                line.next("cum_ready")
                fn(unit(10), unit(0), ACT.Exp)
                fn(unit(11), unit(11), ACT.Exp)
                fn(small[:, 0:8], small[:, 0:8], ACT.Exp)
                fn(unit(12), unit(0), ACT.Exp, scale=-1.0).then_inc(S("decay_ready"), 1)
                for n, (u, b0, w) in enumerate(((9, 4, U), (10, 0, 1024), (11, 2, 1024))):
                    line.next("tok_ready")
                    fn(unit(u)[:, 0:w], PS[:, b0:b0 + w // 512, :].rearrange("p b t -> p (b t)"),
                       ACT.Copy).then_inc(S("tok_copied"), 1)
                y12 = tiles(unit(12))
                for tt in range(2):
                    for pair in range(2):
                        for ln in range(2):
                            line.next("x1_ready")
                            fn(RL(ln, "X"), bank(RB[ln]["y"]), ACT.Copy).then_inc(S("x_copied"), 1)
                        for lvl in range(1, 7):
                            for ln in range(2):
                                line.next("y_ready")
                                fn(RL(ln, "Y"), bank(RB[ln]["y"]), ACT.Copy).then_inc(S("y_copied"), 1)
                        for ln in range(2):
                            line.next("t1_ready")
                            fn(RL(ln, "Y")[:, 0:T], bank(ln, T), ACT.Copy).then_inc(S("t1_copied"), 1)
                        for ln in range(2):
                            line.next("u_ready")
                            fn(RL(ln, "Y")[:, T:2 * T], bank(ln, T, T), ACT.Copy).then_inc(S("u_copied"), 1)
                        for ln in range(2):
                            q = 2 * pair + ln
                            line.next("yt_ready")
                            fn(y12[:, 2 * q:2 * q + 2, tt * P:(tt + 1) * P], tiles(bank(RB[ln]["z"], T), P),
                               ACT.Copy).then_inc(S("yt_copied"), 1)
                line.next("gn_centred")
                fn(unit(9), unit(12), ACT.Square).then_inc(S("hs_in"), 1)
                act.wait_ge(S("hs_ready"), 4)
                head_sqrt(1.0 / 64, C("eps", 16)[:, 2:3])

            BODY["rwkv"] = rwkv

            def flat(b0, n=1, width=512, lo=0):
                return PS[:, b0:b0 + n, lo:lo + width] if width < 512 else PS[:, b0:b0 + n, :].rearrange(
                    "p b t -> p (b t)")

            def load_bias(at):
                dst = W(at, 8 * ATT).rearrange("p (h c) -> p h c", c=ATT)
                for lo, hi, tok in ((0, P, 0), (P, ATT, P)):
                    src = bass.AP(tensor=bias_scratch.tensor, offset=P - tok, ap=[[1, P], [512, 8], [1, hi - lo]])
                    act.dma_start(dst[:, :, lo:hi], src).then_inc(S("bias_in"), 16)

            def ab():
                act.wait_ge(S("x_ready"), XR["ab"])
                line.next("bias_ready")
                row = W(A_LS + 512, 512, 0, 8)
                line.done(fn(row, bank(7, 512, 0, 0, 8), ACT.Copy), "bias_copied")
                act.dma_start(bias_scratch[:, :], row).then_inc(S("bias_stored"), 16)
                raw = W(A_RAW, 8 * 259).rearrange("p (i t) -> p i t", t=259)
                dst = {0: W(A_Q, 1024), 1: W(A_K, 1024), 2: W(A_V, 1024), 5: W(A_BV, 1024), 6: W(A_BO, 1024)}
                for i in range(7):
                    act.wait_ge(slot_free, FREED[f"ab_in.{i}"])
                    b = (2 * i) % 8
                    if i == 1:
                        act.wait_ge(S("bias_stored"), 16)
                        load_bias(A_BM)
                    if i in dst:
                        last = fn(dst[i], flat(b, 2), ACT.Sigmoid if i == 6 else ACT.Copy)
                    else:
                        src = PS[:, b:b + 2, :].rearrange("p b (c t) -> p (b c) t", t=T)
                        last = fn(raw[:, 4 * (i - 3):4 * (i - 3) + 4, 3:259], src, ACT.Copy)
                    last.then_inc(S("ab_copied"), 1)
                act.wait_ge(slot_free, FREED["ab_gates"])

                def ls(at, n, hi=P):
                    return W(A_LS + at, n, 0, hi)
                g, t = ls(0, 16), ls(160, 16)
                line.done(fn(g, bank(6, 16), ACT.Copy))
                line.done(fn(t, g, ACT.Abs))
                line.done(fn(t, t, ACT.Exp, scale=-1.0))
                fn(t, t, ACT.Ln, bias=ones[:, 0:1]).then_inc(S("softlog_ready"), 1)
                line.next("conv_ready")
                fn(W(A_BQ, 2048), W(A_BQ, 2048), ACT.Silu).then_inc(S("bqk_ready"), 1)
                attention("ab")
                line.next("stab_ready")
                dd = ls(256, 1024)
                for i in range(8):
                    fn(dd[:, i * P:(i + 1) * P], dd[:, i * P:(i + 1) * P], ACT.Exp, bias=ls(64 + i, 1))
                fn(ls(72, 8), ls(72, 8), ACT.Exp)
                fn(ls(80, 8), ls(64, 8), ACT.Exp)
                fn(ls(100, 4), ls(100, 4), ACT.Exp).then_inc(S("lexp_ready"), 1)
                line.next("state_ready")
                fn(ls(3840, 512), bank(7), ACT.Copy)
                fn(ls(104, 4), bank(6, 4, 16), ACT.Copy).then_inc(S("state_copied"), 1)
                line.next("lturned")
                fn(ls(2304, 1024), flat(4, 2), ACT.Copy).then_inc(S("lt_copied"), 1)
                line.next("lnum_ready")
                fn(ls(4352, 1024), flat(0, 2), ACT.Copy).then_inc(S("lnum_copied"), 1)
                line.next("lcentred")
                fn(ls(5376, 1024), ls(4352, 1024), ACT.Square).then_inc(S("lsq_ready"), 1)
                line.next("lvar_ready")
                fn(ls(120, 8), ls(120, 8), ACT.Sqrt, bias=eps(1), scale=1.0 / P).then_inc(S("lstd_ready"), 1)
                layer_norm()

            def moe(l):
                def run():
                    act.wait_ge(S("x_ready"), XR[f"moe{l}"])
                    line.next("route_in")
                    fn(W(R_AT + 96, 10), W(R_AT + 96, 10), ACT.Exp).then_inc(S("route_exp"), 1)
                    line.next("gates_turned")
                    fn(W(R_GT, T, 0, 16), bank(7, T, 0, 0, 16), ACT.Copy).then_inc(S("gates_copied"), 1)
                    for half in range(2):
                        line.next("spread_ready")
                        fn(W(SW_G + 2048 * half, 2048), flat(4 * half, 4), ACT.Copy).then_inc(S("g_copied"), 1)
                    swiglu(f"moe{l}", xT[:, :])
                    layer_norm()
                return run

            def c():
                act.wait_ge(S("x_ready"), XR["c"])
                load_bias(C_BM)
                for i, (dst, b) in enumerate(((W(C_Q, 1024), 0), (W(C_Q + 1024, 1024), 2), (W(C_SRC, 1024), 4))):
                    act.wait_ge(slot_free, FREED[f"c_in.{i}"])
                    fn(dst, flat(b, 2), ACT.Copy).then_inc(S("c_copied"), 1)
                for i, b in ((3, 6), (4, 0)):
                    act.wait_ge(slot_free, FREED[f"c_in.{i}"])
                    fn(W(C_KV + 512 * (i - 3), 512), bank(b), ACT.Copy)
                    fn(W(C_KV + 1024 + 512 * (i - 3), 512), bank(b + 1), ACT.Copy).then_inc(S("c_copied"), 1)
                act.wait_ge(slot_free, FREED["c_gates"])
                fn(W(C_G, 48), bank(2, 48), ACT.Sigmoid).then_inc(S("c_copied"), 1)
                for kv in range(2):
                    act.wait_ge(slot_free, FREED[f"cmp_w1.{2 * kv + 1}"])
                    fn(W(C_RAW + kv * T, T, 0, 2 * NCMP), bank(4 + 2 * kv, T, T, 0, 2 * NCMP),
                       ACT.Copy).then_inc(S("cmp_raw"), 1)
                act.wait_ge(S("cmp_turned"), 1)
                for m in range(4):
                    last = fn(W(C_HID + 30 * m, 30), bank(4 + m, 30), ACT.Gelu_apprx_tanh)
                last.then_inc(S("hid_gelu"), 1)
                act.wait_ge(slot_free, FREED["cmp_w2"])
                fn(W(C_KC, 30), bank(3, 30), ACT.Copy)
                fn(W(C_VC, 256, 0, NCMP), bank(3, 256, P, 0, NCMP), ACT.Copy).then_inc(S("cmp_copied"), 1)
                attention("c")
                layer_norm()

            BODY.update(ab=ab, moe0=moe(0), c=c, moe1=moe(1))
            for ph in order:
                if ph.startswith("ffn"):
                    rms(ph)
                    line.next("h_ready")
                    swiglu(ph, hT[:, :])
                elif ph == "final":
                    rms(ph)
                else:
                    BODY[ph]()

        @block.vector
        def _(dve):
            v = nc.vector
            line = Line(dve, "dve_chain")
            done = line.done
            tt_, ts_, stt = v.tensor_tensor, v.tensor_scalar, v.scalar_tensor_tensor

            def over_tiles(ap, n=KT):
                return ap.unsqueeze(1).broadcast_to([ap.shape[0], n, ap.shape[1]])

            def mod(layer, sub, which):
                at = ((layer * 3 + sub) * 3 + which) * 8
                return mods[:, at:at + 8]

            WHERE = {"ffn0": (0, 0), "mla": (0, 1), "ffn1": (0, 2), "ffn2": (1, 0), "rwkv": (1, 1), "ffn3": (1, 2)}

            done(v.memset(zeros[:, :], 0.0), "zeroed")

            def ada_part(p, r=0, rate=0):
                i = INDEX[f"ada.{p}"]
                dve.wait_ge(slot_full[i % RING], r * (16 * rate) + 16 * (i // RING + 1))
                z = W(SW_ADA + 512 * (p % 2), 512)
                for k in range(KT):
                    w = ring[i % RING][:, k * 512:(k + 1) * 512]
                    if k == 0:
                        ins = ts_(z, w, cact[:, 0:1], None, ALU.mult)
                    else:
                        ins = stt(z, w, cact[:, k:k + 1], z, ALU.mult, ALU.add)
                    if k < KT - 1:
                        ins.then_inc(S("ada_chain"), 1)
                        dve.wait_ge(S("ada_chain"), r * (7 * RING) + (7 * p + k + 1))
                ins.then_inc(S("ada_part"), 1)
                dve.wait_ge(S("ada_part"), r * RING + (p + 1))
                dve.sem_inc(dve_free, 1)

            def ada_finish(p, r=0):
                dve.wait_ge(S("ada_sum"), r * RING + (p + 1))
                bias, at = VEC["ada_b"][0], 4 * p
                if isinstance(r, int):
                    a, b = mods[:, at:at + 4], vec[:, bias + at:bias + at + 4]
                else:
                    a, b = mods[:, bass.ds(r * 16 + at, 4)], vec[:, bass.ds(r * 16 + (at + bias), 4)]
                tt_(a, bank(6 + p % 2, 4), b, ALU.add).then_inc(S("ada_read"), 1)

            def ada(lo, hi):
                for p in range(lo, hi):
                    ada_part(p)
                    if p > lo:
                        ada_finish(p - 1)
                ada_finish(hi - 1)
                dve.wait_ge(S("ada_read"), hi)

            def residual_gate(ph):
                layer, sub = WHERE[ph]
                done(ts_(gate[:, :], mod(layer, sub, 2), 1.0 if sub == 1 else 0.5, None, ALU.mult))

            def rms(ph):
                if ph != "final":
                    layer, sub = WHERE[ph]
                    at = (layer * 3 + sub) * 8
                    done(stt(gain[:, :], mod(layer, sub, 1), 1.0, V("norm_g", at, 8), ALU.add, ALU.mult))
                    if sub == 1:
                        residual_gate(ph)
                line.next("std_ready")
                done(v.reciprocal(RSTD, STD))
                done(tt_(tiles(NTMP), x3, over_tiles(RSTD), ALU.mult))
                tmp = tiles(NTMP)
                for k in range(KT):
                    if ph == "final":
                        last = ts_(x3[:, k, :], tmp[:, k, :], V("final_g", k), None, ALU.mult)
                    else:
                        last = ts_(h3[:, k, :], tmp[:, k, :], gain[:, k:k + 1], mod(layer, sub, 0)[:, k:k + 1],
                                   ALU.mult, ALU.add)
                done(last, "x_ready" if ph == "final" else "h_ready")

            def residual():
                for m in range(KT):
                    last = stt(x3[:, m, :], out_tile(m), gate[:, m:m + 1], x3[:, m, :], ALU.mult, ALU.add)
                done(last, "x_ready")

            def layer_norm(at):
                for b in range(4):
                    last = stt(xT[:, b * 512:(b + 1) * 512], xT[:, b * 512:(b + 1) * 512], ALPHA, bank(b), ALU.mult,
                               ALU.add)
                done(last, "pre_ready")
                line.next("mean_ready")
                done(ts_(RSTD, bank(7, T), 1.0 / D, None, ALU.mult))
                done(tt_(x3, x3, over_tiles(RSTD), ALU.subtract), "centred")
                line.next("std_ready")
                done(v.reciprocal(RSTD, STD))
                done(tt_(x3, x3, over_tiles(RSTD), ALU.mult))
                for k in range(KT):
                    last = ts_(x3[:, k, :], x3[:, k, :], V("ln_g", at + k), V("ln_b", at + k), ALU.mult, ALU.add)
                done(last, "x_ready")

            def swiglu(tag, source):
                n, base = SW[tag]
                moe = tag.startswith("moe")
                line.next("x_rounded")
                tt_(x_parts[1][:, :], source, x_parts[0][:, :].bitcast(F32), ALU.subtract).then_inc(S("x_split"), 1)

                def up_low(j, wait):
                    dve.wait_ge(S("up_rounded"), wait)
                    hi, lo = w_up[j % 2]
                    tt_(lo[:, :], piece(f"{tag}.{j}")[:, 0:2048], hi[:, :].bitcast(F32),
                        ALU.subtract).then_inc(S("up_split"), 1)

                def hidden(j, wait_silu, wait_down, expert):
                    dve.wait_ge(S("silu_ready"), wait_silu)
                    s = W(SW_SILU + (j % 2) * T, T)
                    if moe:
                        if isinstance(expert, int):
                            g = W(expert, T)
                        else:
                            g = work[:, bass.ds(expert, T)]
                        tt_(s, s, g, ALU.mult).then_inc(S("gated"), 1)
                        dve.wait_ge(S("gated"), wait_silu - SW["moe0"][1])
                    tt_(s, s, bank(4 + j % 2, T, T), ALU.mult).then_inc(S("hid_full"), 1)
                    dve.wait_ge(S("hid_full"), wait_silu)
                    if wait_down is not None:
                        dve.wait_ge(S("down_done"), wait_down)
                    hi, lo = hid[j % 2]
                    v.tensor_copy(hi[:, :], s).then_inc(S("hid_rounded"), 1)
                    dve.wait_ge(S("hid_rounded"), wait_silu)
                    tt_(lo[:, :], s, hi[:, :].bitcast(F32), ALU.subtract).then_inc(S("hid_ready"), 1)

                def down_low(j, wait):
                    dve.wait_ge(S("down_rounded"), wait)
                    hi, lo = w_down[j % 2]
                    tt_(lo[:, :], piece(f"{tag}.{j}")[:, 2048:3072], hi[:, :].bitcast(F32),
                        ALU.subtract).then_inc(dve_free, 1)

                p0, carried = CARRY.get(tag, (0, 0))

                def step(j, r, rate):
                    if j < n:
                        up_low(j, r * RING + (base + j + 1))
                    if j >= 1:
                        at = (j - 1) // E_TILES * T + SW_G
                        hidden(j - 1, r * RING + (base + j),
                               r * RING + (base + j - 2) if base + j > 2 else None,
                               at if isinstance(r, int) else r * T + at)
                    if j < n:
                        down_low(j, r * RING + (base + j + 1))
                    if 0 <= j - 2 < carried:
                        ada_finish(p0 + j - 2, r)
                    if j < carried:
                        ada_part(p0 + j, r, rate)
                run_rounds(dve, n, carried, step)
                if carried:
                    dve.wait_ge(S("ada_read"), p0 + carried)
                if tag in WHERE:
                    residual_gate(tag)
                dve.wait_ge(S("down_done"), base + n)

            def attention(phase):
                items, base = ITEMS[phase], IT0[phase]
                s_of, _, stat = att_place(items, ABASE[phase])
                n = len(items)
                scale = SCALE[phase]

                def cuts(i):
                    return ((0, NCMP), (NCMP, 2 * NCMP)) if items[i]["kind"] == "cmp" else ((0, P), (P, ATT))

                def maxima(i):
                    cmp_ = items[i]["kind"] == "cmp"
                    w = 2 * NCMP if cmp_ else ATT
                    line.next("score_ready")
                    if i >= 2:
                        dve.wait_ge(S("turned"), base + i - 1)
                    s = s_of(i)
                    done(stt(s[:, 0:w], bank(i % 2, w), scale, score_bias(phase, items[i]), ALU.mult, ALU.add))
                    for k, (lo, hi) in enumerate(cuts(i)):
                        last = v.tensor_reduce(stat(i, 0)[:, k:k + 1], s[:, lo:hi], AX.X, ALU.max, negate=True)
                    if cmp_:
                        done(last)
                        last = ts_(stat(i, 0), stat(i, 0), -0.1 * NEG, None, ALU.min)
                    done(last, "max_ready")

                def normalise(i):
                    line.next("exp_ready")
                    it = items[i]
                    if it["kind"] == "cmp":
                        done(ts_(stat(i, 1), stat(i, 1), 1e-30, None, ALU.max))
                    done(v.reciprocal(stat(i, 2), stat(i, 1)))
                    if phase == "c":
                        g = W(C_G, 48).rearrange("p (t g) -> p t g", t=2)
                        c = 8 * it["branch"] + it["h"]
                        done(tt_(stat(i, 2), stat(i, 2), g[:, :, c:c + 1].squeeze(2), ALU.mult))
                    s = s_of(i)
                    for k, (lo, hi) in enumerate(cuts(i)):
                        last = ts_(s[:, lo:hi], s[:, lo:hi], stat(i, 2)[:, k:k + 1], None, ALU.mult)
                    done(last, "prob_ready")

                for step in range(n + 1):
                    if step < n:
                        maxima(step)
                    if step >= 1:
                        normalise(step - 1)

            def mla():
                rms("mla")
                dve.wait_ge(slot_free, FREED["mla_in.1"])
                v.tensor_copy(W(M_LAT, 1024), PS[:, 0:2, :].rearrange("p b t -> p (b t)"))
                v.tensor_copy(W(M_LAT + 1024, T), bank(2, T))
                done(v.tensor_copy(W(M_KR, T, 64, 96), bank(2, T, T, 64, 96)), "lat_copied")
                line.next("std_ready")
                r = W(M_TMP + 1536, 2 * T)
                done(v.reciprocal(r, r))
                lat = tiles(W(M_LAT, 5 * T))
                for i in range(5):
                    g = V("q_norm", i) if i < 3 else V("kv_norm", i - 3)
                    last = stt(lat[:, i, :], lat[:, i, :], g, r[:, 0:T] if i < 3 else r[:, T:2 * T], ALU.mult,
                               ALU.mult)
                done(last, "lat_ready")
                at = CONST["cos"][0]
                cos, sin = const[64:96, at:at + T], const[64:96, at + T:at + 2 * T]
                q = W(M_Q, 16 * T, 64, 96)
                t = W(M_TMP, 8 * T, 64, 96)
                for g in range(2):
                    line.next("rot_ready")
                    ps = PS[64:96, 4 - 4 * g:8 - 4 * g, :].rearrange("p b (h t) -> p (b h) t", t=T)
                    done(tt_(tiles(t), ps, over_tiles(sin), ALU.mult), "rot_read")
                    qg = tiles(q)[:, 8 * g:8 * g + 8, :]
                    done(tt_(qg, qg, over_tiles(cos), ALU.mult))
                    done(tt_(qg, qg, tiles(t), ALU.add))
                line.next("rot_ready")
                kr = W(M_KR, T, 64, 96)
                tt_(t[:, 0:T], bank(4, T, 0, 64, 96), sin, ALU.mult)
                done(tt_(kr, kr, cos, ALU.mult))
                k16 = tiles(W(M_K, 16 * T, 64, 96))
                done(tt_(k16, over_tiles(kr, 16), over_tiles(t[:, 0:T], 16), ALU.add), "qk_ready")
                attention("mla")
                dve.wait_ge(S("att_out"), 16)
                dve.wait_ge(slot_free, FREED["mla_out.1"])
                residual()

            BODY = {"mla": mla}
            def banks4(b0):
                return PS[:, b0:b0 + 4, :].rearrange("p b t -> p (b t)")

            def rwkv():
                rms("rwkv")
                xx = tiles(unit(0))
                tt_(xx[:, :, 1:T], h3[:, :, 0:T - 1], h3[:, :, 1:T], ALU.subtract)
                done(ts_(xx[:, :, 0:1], h3[:, :, 0:1], -1.0, None, ALU.mult))
                ld = unit(3)
                for n, mu in enumerate((3, 4, 5, 0, 1, 2)):
                    if n in (2, 3):
                        dve.wait_ge(S("xs_used"), n - 1)
                    if n == 4:
                        dve.wait_ge(slot_free, FREED["rwkv_lora1"])
                    if n == 5:
                        dve.wait_ge(slot_free, FREED["rwkv_r.1"])
                    xs = tiles(unit(1 + n % 2))
                    for k in range(KT):
                        last = stt(xs[:, k, :], xx[:, k, :], V("mu", 8 * mu + k), h3[:, k, :], ALU.mult, ALU.add)
                    done(last, "xs_ready")
                    if n == 3:
                        dve.wait_ge(S("proj_copied"), 1)
                        done(ts_(ld, ld, -math.exp(-0.5), None, ALU.mult))
                        done(v.memset(unit(10), 1.0))
                        done(v.memset(tiles(unit(10), P)[:, :, 0:1], 0.0))
                cum = tiles(unit(0), P)
                done(v.tensor_tensor_scan(unit(0), unit(10), ld, 0.0, ALU.mult, ALU.add))
                mid, f = small[:, 16:32], small[:, 0:8]
                done(v.tensor_copy(mid.unsqueeze(2), cum[:, :, 63:64]))
                end = cum[:, 0:16:2, P - 1:P].squeeze(2)
                done(tt_(f, end, mid[:, 0:16:2], ALU.subtract))
                tt_(f, f, mid[:, 1:16:2], ALU.add)
                done(tt_(cum, cum, mid.unsqueeze(2).broadcast_to([P, 16, P]), ALU.subtract))
                done(tt_(unit(11), unit(0), ld, ALU.subtract), "cum_ready")
                dve.wait_ge(S("proj_copied"), 5)
                for k in range(KT):
                    last = ts_(tiles(unit(1))[:, k, :], tiles(unit(7))[:, k, :], V("k_k", k), None, ALU.mult)
                done(last, "kk_ready")
                line.next("hs_ready")
                hst = small[0:16, T:2 * T]
                done(ts_(hst, bank(7, T, 0, 0, 16), 1e-24, None, ALU.max), "hmax_ready")
                line.next("hstd_ready")
                done(v.reciprocal(hst, hst), "hb_in")
                line.next("hb_ready")
                done(tt_(unit(1), unit(1), banks4(0), ALU.mult))
                for k in range(KT):
                    last = ts_(tiles(unit(9))[:, k, :], tiles(unit(4))[:, k, :], 1.0, V("k_a", k), ALU.subtract,
                               ALU.mult)
                done(last)
                done(stt(unit(7), unit(9), 1.0, unit(7), ALU.add, ALU.mult))
                done(tt_(unit(9), unit(6), unit(7), ALU.mult))
                for k in range(KT):
                    u9 = tiles(unit(9))[:, k, :]
                    last = ts_(u9, u9, V("r_k", k), None, ALU.mult)
                done(last, "hs_in_dve")
                line.next("decay_ready")
                done(tt_(unit(4), unit(1), unit(4), ALU.mult))
                tt_(unit(4), unit(4), unit(12), ALU.mult)
                tt_(unit(7), unit(7), unit(12), ALU.mult)
                tt_(unit(6), unit(6), unit(10), ALU.mult)
                done(stt(unit(1), unit(1), -1.0, unit(11), ALU.mult, ALU.mult))
                line.next("hs_ready")
                done(v.tensor_copy(hst, bank(7, T, 0, 0, 16)), "hb_in")
                line.next("hb_ready")
                dve.wait_ge(S("proj_copied"), 6)
                done(tt_(hT[:, :], unit(8), banks4(0), ALU.mult))
                done(v.memset(W(10 * U + 1024, 1024), 0.0), "tilde_ready")
                spad = W(10 * U + 1024, 1024)
                strict = C("strict").unsqueeze(1).broadcast_to([P, 4, P])
                incl = C("incl").unsqueeze(1).broadcast_to([P, 4, P])
                for tt in range(2):
                    for pair in range(2):
                        for ln in range(2):
                            line.next("pair_scores")
                            ak, rk = RL(ln, "AK"), RL(ln, "RK")
                            for par in range(2):
                                b = 4 * ln + 2 * par
                                tt_(tiles(ak[:, par * 512:(par + 1) * 512], P), tiles(bank(b), P), strict, ALU.mult)
                                last = tt_(tiles(rk[:, par * 512:(par + 1) * 512], P), tiles(bank(b + 1), P), incl,
                                           ALU.mult)
                            done(last, "ak_ready")
                        for ln in range(2):
                            line.next("lvl_ready")
                            done(tt_(tiles(RL(ln, "XT"), P), tiles(RL(ln, "MTL"), P),
                                     ident.unsqueeze(1).broadcast_to([P, 4, P]), ALU.add), "xt_ready")
                        for lvl in range(1, 7):
                            for ln in range(2):
                                line.next("z_ready")
                                if lvl < 6:
                                    tt_(RL(ln, "X"), RL(ln, "X"), bank(RB[ln]["z"]), ALU.add)
                                done(tt_(RL(ln, "XT"), RL(ln, "XT"), bank(RB[ln]["zt"]), ALU.add), "x_upd")
                        line.seen["lvl_ready"] += 12
                        if tt == 0:
                            for ln in range(2):
                                line.next("s_ready")
                                for j in range(4):
                                    q = 2 * pair + ln
                                    h, k, lo = 4 * q + j, 2 * q + j // 2, 64 * (j % 2)
                                    last = ts_(spad[lo:lo + 64, h * 64:(h + 1) * 64],
                                               bank(RB[ln]["zt"], 64, j * 64, lo, lo + 64), f[lo:lo + 64, k:k + 1],
                                               None, ALU.mult)
                                done(last, "s_copied")
                y = unit(12)
                line.next("hs_ready")
                done(ts_(hst, bank(7, T, 0, 0, 16), 1.0 / 64, None, ALU.mult), "hb_in")
                line.next("hb_ready")
                done(tt_(y, y, banks4(0), ALU.subtract), "gn_centred")
                line.next("hstd_ready")
                done(v.reciprocal(hst, hst), "hb_in")
                line.next("hb_ready")
                done(tt_(y, y, banks4(0), ALU.mult))
                for k in range(KT):
                    yk = tiles(y)[:, k, :]
                    last = ts_(yk, yk, V("gn_w", k), V("gn_b", k), ALU.mult, ALU.add)
                done(last)
                done(tt_(y, y, hT[:, :], ALU.add))
                done(tt_(y, y, unit(5), ALU.mult), "mix_ready")
                dve.wait_ge(slot_free, FREED["rwkv_out.1"])
                residual()

            BODY["rwkv"] = rwkv

            def bias_banks():
                return PS[:, 0:6, :].rearrange("p b t -> p (b t)").rearrange("p (h c) -> p h c", c=ATT)

            def ab():
                def ls(at, n, hi=P):
                    return W(A_LS + at, n, 0, hi)

                raw = W(A_RAW, 8 * 259).rearrange("p (i t) -> p i t", t=259)
                done(v.memset(raw[:, :, 0:3], 0.0))
                dve.wait_ge(S("ab_copied"), 5)
                qk = tiles(W(A_BQ, 2048))
                for j in range(4):
                    for i in range(8):
                        w = V("conv", 8 * j + i)
                        if j == 0:
                            last = ts_(qk[:, i, :], raw[:, i, 0:T], w, None, ALU.mult)
                        else:
                            last = stt(qk[:, i, :], raw[:, i, j:j + T], w, qk[:, i, :], ALU.mult, ALU.add)
                    done(last, "conv_ready" if j == 3 else None)
                line.next("softlog_ready")
                g = ls(0, 16).rearrange("p (t g) -> p t g", t=2)
                sl = ls(160, 16).rearrange("p (t g) -> p t g", t=2)
                lf = ls(16, 8).rearrange("p (t h) -> p t h", t=2)
                done(ts_(lf, g[:, :, 4:8], 0.0, None, ALU.min))
                done(tt_(lf, lf, sl[:, :, 4:8], ALU.subtract), "lf_ready")
                line.next("bias_flipped")
                done(tt_(W(A_BM, 8 * ATT).rearrange("p (h c) -> p h c", c=ATT), bias_banks(),
                         C("dilated").unsqueeze(1).broadcast_to([P, 8, ATT]), ALU.add), "bias_used")
                attention("ab")
                line.next("cumsum_ready")
                b, bl, gi = ls(24, 8), ls(32, 8), ls(40, 8)
                v.tensor_copy(b, bank(6, 8))
                done(v.tensor_copy(bl, bank(6, 8, 8)))
                done(tt_(gi.rearrange("p (t h) -> p t h", t=2), g[:, :, 0:4], b.rearrange("p (t h) -> p t h", t=2),
                         ALU.subtract))
                dd = ls(256, 1024)
                for i in range(8):
                    last = ts_(dd[:, i * P:(i + 1) * P], ident, gi[:, i:i + 1], None, ALU.mult)
                done(last, "diag_ready")
                line.next("rowbc_ready")
                causal = C("causal")[:, 0:P]
                for i in range(8):
                    last = stt(dd[:, i * P:(i + 1) * P], bank(7 if i >= 4 else 2, P, (i % 4) * P), b[:, i:i + 1], causal,
                               ALU.add, ALU.add)
                m1 = ls(96, 4)
                done(v.tensor_reduce(m1, tiles(bank(2), P), AX.X, ALU.max))
                done(stt(m1, m1, 0.0, bl[:, 0:4], ALU.max, ALU.add))
                mx, inter, nmt, sc = ls(48, 8), ls(56, 8), ls(64, 8), ls(72, 8)
                v.tensor_copy(inter[:, 0:4], b[:, 0:4])
                tt_(inter[:, 4:8], b[:, 4:8], m1, ALU.add)
                done(v.tensor_reduce(mx, tiles(dd, P), AX.X, ALU.max))
                done(tt_(mx, mx, inter, ALU.max))
                ts_(nmt, mx, -1.0, None, ALU.mult)
                wk = ls(100, 4)
                tt_(wk, gi[:, 0:4], bl[:, 0:4], ALU.add)
                done(tt_(sc, inter, mx, ALU.subtract))
                done(tt_(wk, wk, m1, ALU.subtract), "stab_ready")
                line.next("lexp_ready")
                line.next("ktok_ready")
                kw = ls(3328, 512)
                for h in range(4):
                    last = ts_(kw[:, h * P:(h + 1) * P], bank(3, P, h * P), wk[:, h:h + 1], None, ALU.mult)
                done(last, "kw_ready")
                line.next("lqk_ready")
                ss = ls(1280, 1024)
                for tt in range(2):
                    last = stt(ss[:, tt * 512:(tt + 1) * 512], bank(tt), P ** -0.5, dd[:, tt * 512:(tt + 1) * 512],
                               ALU.mult, ALU.mult)
                done(last, "lprob_ready")
                den = ls(88, 8)
                done(v.tensor_reduce(den, tiles(ss, P), AX.X, ALU.add))
                hh = ls(4352, 1024)
                line.next("lnum_copied")
                line.next("linter_ready")
                done(ts_(sc, sc, P ** -0.5, None, ALU.mult))
                for h in range(4):
                    hs = slice((4 + h) * P, (5 + h) * P)
                    stt(hh[:, hs], bank(2, P, h * P), sc[:, 4 + h:5 + h], hh[:, hs], ALU.mult, ALU.add)
                tmp = ls(112, 8)
                done(tt_(tmp[:, 0:4], bank(6, 4, 32), sc[:, 4:8], ALU.mult))
                done(tt_(den[:, 4:8], den[:, 4:8], tmp[:, 0:4], ALU.add))
                done(ts_(tmp, den, -1.0, None, ALU.mult))
                done(tt_(den, den, tmp, ALU.max))
                done(tt_(den, den, ls(80, 8), ALU.max))
                done(v.reciprocal(den, den))
                h8 = tiles(hh, P)

                def each(s):
                    return s.unsqueeze(2).broadcast_to([P, 8, P])
                done(tt_(h8, h8, each(den), ALU.mult))
                done(v.tensor_reduce(tmp, h8, AX.X, ALU.add))
                done(ts_(tmp, tmp, 1.0 / P, None, ALU.mult))
                done(tt_(h8, h8, each(tmp), ALU.subtract), "lcentred")
                line.next("lsq_ready")
                var = ls(120, 8)
                done(v.tensor_reduce(var, tiles(ls(5376, 1024), P), AX.X, ALU.add), "lvar_ready")
                line.next("lstd_ready")
                done(v.reciprocal(var, var))
                done(tt_(h8, h8, each(var), ALU.mult), "lnormed")
                line.next("lout_ready")
                for h in range(4):
                    last = stt(tiles(W(A_Y, U))[:, 4 + h, :], bank(4 + h // 2, T, (h % 2) * T), V("head_norm", h),
                               tiles(W(A_BO, 1024))[:, h, :], ALU.mult, ALU.mult)
                done(last, "mix_ready")
                dve.wait_ge(slot_free, FREED["ab_out.1"])
                layer_norm(0)

            def first_max(onehot, x, mx, tmp):
                iota = C("iota").unsqueeze(1).broadcast_to([P, 2, 4])
                done(v.tensor_reduce(mx, x, AX.X, ALU.max))
                done(tt_(tmp, x, mx.unsqueeze(2).broadcast_to([P, 2, 4]), ALU.is_equal))
                done(ts_(onehot, iota, -4.0, None, ALU.add))
                done(tt_(tmp, tmp, onehot, ALU.mult))
                idx = W(R_AT + 150, 2)
                done(v.tensor_reduce(idx, tmp, AX.X, ALU.min))
                done(tt_(onehot, onehot, idx.unsqueeze(2).broadcast_to([P, 2, 4]), ALU.is_equal))

            def moe(l):
                def run():
                    ph = f"moe{l}"

                    def r(at, n):
                        return W(R_AT + at, n)

                    def by4(ap):
                        return ap.rearrange("p (t g) -> p t g", g=4)
                    done(v.tensor_copy(tiles(W(R_PICK, 2048, 0, 16), P),
                                       ident[0:16, 0:16].unsqueeze(2).broadcast_to([16, 16, P])), "pick_ready")
                    dve.wait_ge(slot_free, FREED[f"router{l}"])
                    lg = r(40, 40).rearrange("p (t g) -> p t g", t=2)
                    done(v.tensor_copy(r(40, 40), bank(7, 40)))
                    gate_, oh, oh1, oh2, tmp = r(0, 32), by4(r(110, 8)), by4(r(118, 8)), by4(r(126, 8)), by4(r(134, 8))
                    gm, m1, m2 = r(142, 2), r(144, 2), r(146, 2)
                    first_max(oh, lg[:, :, 0:4], gm, tmp)
                    ex = r(96, 8)
                    done(tt_(by4(ex), lg[:, :, 0:4], gm.unsqueeze(2).broadcast_to([P, 2, 4]), ALU.subtract))
                    w = r(160, 32).rearrange("p (t g e) -> p t g e", t=2, g=4)
                    le = lg[:, :, 4:20].rearrange("p t (g e) -> p t g e", g=4)
                    for t in range(2):
                        last = tt_(w[:, t], le[:, t], oh[:, t, :].unsqueeze(2).broadcast_to([P, 4, 4]), ALU.mult)
                    done(last)
                    es = by4(r(192, 8))
                    for t in range(2):
                        last = v.tensor_reduce(es[:, t, :], w[:, t].rearrange("p g e -> p e g"), AX.X, ALU.add)
                    done(last)
                    first_max(oh1, es, m1, tmp)
                    done(stt(es, oh1, NEG, es, ALU.mult, ALU.add))
                    first_max(oh2, es, m2, tmp)
                    done(tt_(r(104, 2), m2, m1, ALU.subtract), "route_in")
                    line.next("route_exp")
                    gw, w1, w2 = r(200, 2), r(202, 2), r(204, 2)
                    done(v.tensor_reduce(gw, by4(ex), AX.X, ALU.add))
                    done(ts_(w1, r(104, 2), 1.0, None, ALU.add))
                    done(tt_(w1, w1, gw, ALU.mult))
                    done(v.reciprocal(w1, w1))
                    done(tt_(w2, w1, r(104, 2), ALU.mult))
                    done(tt_(oh1, oh1, w1.unsqueeze(2).broadcast_to([P, 2, 4]), ALU.mult))
                    done(tt_(oh2, oh2, w2.unsqueeze(2).broadcast_to([P, 2, 4]), ALU.mult))
                    done(tt_(oh1, oh1, oh2, ALU.add))
                    g4 = gate_.rearrange("p (t g e) -> p t g e", t=2, g=4)
                    for t in range(2):
                        last = tt_(g4[:, t], oh[:, t, :].unsqueeze(2).broadcast_to([P, 4, 4]),
                                   oh1[:, t:t + 1, :].broadcast_to([P, 4, 4]), ALU.mult)
                    done(last, "gates_ready")
                    swiglu(ph, xT[:, :])
                    layer_norm(16 * l + 8)
                return run

            def c():
                dve.wait_ge(S("c_copied"), 3)
                for kv in range(2):
                    dst = W(C_CMPB + 960 * kv, 960).rearrange("p (i g n) -> p i g n", g=2, n=NCMP)
                    for g in range(2):
                        src = W(C_SRC + (2 * kv + g) * T, T).rearrange("p (n r) -> p r n", r=16)
                        for a in range(2):
                            pos = V("cmp_pos", 32 * kv + 16 * a, 16).unsqueeze(2).broadcast_to([P, 16, NCMP])
                            last = tt_(dst[:, 16 * a:16 * a + 16, g, :], src[:, :, a:a + NCMP], pos, ALU.add)
                done(last, "cmpb_ready")
                line.next("bias_flipped")
                raw = bias_banks()
                bm = W(C_BM, 8 * ATT).rearrange("p (h c) -> p h c", c=ATT)
                bc = W(C_BC, 240).rearrange("p (h t n) -> p h t n", h=8, t=2)
                done(v.memset(W(C_BC, 240), 0.0))
                v.tensor_copy(bc[:, :, 0, 0:7], raw[:, :, 31:P:16])
                done(v.tensor_copy(bc[:, :, 1, :], raw[:, :, P + 31:ATT:16]))
                done(tt_(W(C_BC, 240).rearrange("p (h c) -> p h c", h=8), W(C_BC, 240).rearrange("p (h c) -> p h c", h=8),
                         C("cmpmask").unsqueeze(1).broadcast_to([P, 8, 2 * NCMP]), ALU.add))
                done(tt_(bm, raw, C("causal").unsqueeze(1).broadcast_to([P, 8, ATT]), ALU.add), "bias_used")
                dve.wait_ge(S("c_copied"), 6)
                attention("c")
                dve.wait_ge(slot_free, FREED["c_out.1"])
                layer_norm(16)

            BODY.update(ab=ab, moe0=moe(0), c=c, moe1=moe(1))
            for ph in order:
                if ph == "ffn0":
                    dve.wait_ge(S("vec_in"), 16)
                    dve.wait_ge(S("cact_ready"), 1)
                    ada(0, ADA_HEAD)
                    dve.wait_ge(S("const_in"), 32)
                if ph.startswith("ffn"):
                    rms(ph)
                    swiglu(ph, hT[:, :])
                    residual()
                elif ph == "final":
                    rms(ph)
                else:
                    BODY[ph]()

        @block.gpsimd
        def _(pool):
            line = Line(pool, "pool_chain")
            mul = nc.gpsimd.tensor_tensor

            def rwkv():
                levels = C("level").rearrange("p (l t) -> p l t", t=P)
                for tt in range(2):
                    for pair in range(2):
                        for lvl in range(7):
                            for ln in range(2):
                                if lvl == 0:
                                    line.next("ak_ready")
                                elif lvl == 1:
                                    line.next("xt_ready")
                                else:
                                    line.next("y_ready")
                                m = RL(ln, "AK").rearrange("p (e c t) -> p e c t", e=2, t=P)[:, :, 0:2, :]
                                o = RL(ln, "MTL").rearrange("p (e c t) -> p e c t", e=2, t=P)
                                for e in range(2):
                                    last = mul(o[:, e], m[:, e],
                                               levels[:, lvl:lvl + 1, :].broadcast_to([P, 2, P]), ALU.mult)
                                last.then_inc(S("lvl_ready"), 1)
                        line.next("y_ready", 2)

            rwkv()




def bucket(dist):
    n = np.maximum(dist, 0)
    nf = np.maximum(n, 1).astype(np.float32)
    large = 16 + (np.log(nf / 16) / math.log(2048 / 16) * 16).astype(np.int32)
    return np.where(n < 16, n, np.minimum(large, 31))


def constants():
    c = np.zeros((P, NCONST), np.float32)

    def put(name, value, lo=0):
        value = np.asarray(value, np.float32)
        value = value.reshape(value.shape[0], -1)
        at, n = CONST[name]
        assert value.shape[1] == n, name
        c[lo:lo + value.shape[0], at:at + n] = value

    i = np.arange(P)
    put("ident", np.eye(P))
    put("flip", np.eye(P)[::-1])
    put("ones", np.ones((P, P)))
    r = np.arange(32)
    put("rot", (r[:, None] == (r[None, :] + 16) % 32), 64)
    inv = np.float32(10000.0) ** (-np.arange(0, 32, 2, dtype=np.float32) / np.float32(32))
    ang = (np.arange(T, dtype=np.float32)[:, None] * inv[None, :]).astype(np.float32).T
    put("cos", np.concatenate([np.cos(ang)] * 2), 64)
    put("sin", np.concatenate([-np.sin(ang), np.sin(ang)]), 64)
    dist = np.concatenate([i[:, None] - i[None, :], (i[:, None] + P) - np.arange(T)[None, :]], 1)
    put("causal", np.where(dist >= 0, 0.0, NEG))
    times = ((dist >= 0) & (dist <= 128)).astype(int) + ((dist >= 0) & (dist % 4 == 0)) + ((dist >= 0) & (dist % 16 == 0))
    put("dilated", np.where(times > 0, np.log(np.maximum(times, 1)), NEG))
    s, t = i[:, None], i[None, :]
    put("strict", s < t)
    put("incl", s <= t)
    put("level", np.concatenate([(t // b % 2 == 1) & (s // b == t // b - 1) for b in (1, 2, 4, 8, 16, 32, 64)], 1))
    k, h = np.arange(KT), np.arange(16)
    sel = h[None, None, :] == 2 * k[None, :, None] + i[:, None, None] // 64
    put("hsel", sel)
    put("hselT", sel.transpose(2, 1, 0))
    put("dist", np.arange(32)[:, None] == bucket(255 - np.arange(512))[None, :])
    tok = i[:, None, None] + P * np.arange(2)[None, :, None]
    put("cmpmask", np.where(tok >= 16 * np.arange(NCMP) + 31, 0.0, NEG))
    put("iota", np.broadcast_to(np.arange(4), (P, 4)))
    put("eps", np.broadcast_to([1e-6, 1e-5, 64e-5], (P, 3)))
    return c


def pack(a):
    stream = np.zeros((len(STREAM), P, SLOT), np.float32)

    def put(name, value):
        value = value.reshape(value.shape[0], -1)
        stream[INDEX[name], :value.shape[0], :value.shape[1]] = value

    def rows(w):
        return w.reshape(-1, P, w.shape[1]).transpose(1, 0, 2)

    def put_cols(tag, w, width=512):
        for i in range(w.shape[1] // width):
            put(f"{tag}.{i}", rows(w[:, i * width:(i + 1) * width]))

    def put_swiglu(tag, n, gate, up, down):
        g, u, d = rows(gate), rows(up), rows(down)
        for m in range(n):
            i = INDEX[f"{tag}.{m}"]
            dst = stream[i, :, 0:2048].reshape(P, KT, 2, P)
            dst[:, :, 0] = g[:, :, m * P:(m + 1) * P]
            dst[:, :, 1] = u[:, :, m * P:(m + 1) * P]
            stream[i, :, 2048:3072] = d[:, m]

    put_cols("ada", np.concatenate([a["ada_w"][0], a["ada_w"][1]], 1))
    for l in range(2):
        for j in range(2):
            w = a["ffn_w_in"][l, j]
            put_swiglu(f"ffn{2 * l + j}", FF_TILES, w[:, :2816], w[:, 2816:], a["ffn_w_out"][l, j])
    w = a["mla_w_in"][0]
    put("mla_in.0", rows(w[:, :512]))
    put("mla_in.1", rows(np.concatenate([w[:, 512:640], np.zeros((D, 64), np.float32), w[:, 640:]], 1)))
    for i in range(2):
        put(f"mla_uq.{i}", rows(a["mla_w_uq"][0][:, 768 * i:768 * (i + 1)]))
    w = a["mla_w_ukv"][0].reshape(256, 16, 2, 64).transpose(0, 2, 1, 3).reshape(256, 2, D)
    put("mla_ukv", np.concatenate([rows(w[:, 0]).reshape(P, -1), rows(w[:, 1]).reshape(P, -1)], 1))
    put_cols("mla_out", a["mla_w_out"][0])
    put("rwkv_lora1", rows(np.concatenate([a["rwkv_wd1"][0], a["rwkv_wa1"][0], a["rwkv_wg1"][0]], 1)))
    i = INDEX["rwkv_lora2"]
    stream[i, :64, 0:1024] = a["rwkv_wd2"][0]
    stream[i, :64, 1024:2048] = a["rwkv_wa2"][0]
    stream[i, :, 2048:3072] = a["rwkv_wg2"][0][:128]
    stream[i, :32, 3072:4096] = a["rwkv_wg2"][0][128:]
    for n, tag in enumerate(("rwkv_r", "rwkv_k", "rwkv_v")):
        put_cols(tag, a["rwkv_w_rkv"][0, n])
    put_cols("rwkv_out", a["rwkv_w_out"][0])
    w = a["ab_w_in_2"][0]
    put_cols("ab_in", w[:, :3584])
    put("ab_gates", rows(w[:, 3584:]))
    put_cols("ab_out", a["ab_w_out_2"][0])
    w = a["c_w_in_2"][0]
    put_cols("c_in", w[:, :2560])
    put("c_gates", rows(w[:, 2560:]))
    for kv in range(2):
        w = a["c_cmp_w1_2"][0, kv].reshape(32, P, 256).transpose(1, 0, 2)
        for half in range(2):
            put(f"cmp_w1.{2 * kv + half}", w[:, 16 * half:16 * half + 16])
    put("cmp_w2", np.concatenate([rows(a["c_cmp_w2_2"][0, kv]).reshape(P, -1) for kv in range(2)], 1))
    put_cols("c_out", a["c_w_out_2"][0])
    for l in range(2):
        w = np.concatenate([a["moe_wr_g_2"][l], a["moe_wr_e_2"][l].transpose(1, 0, 2).reshape(D, 16)], 1)
        put(f"router{l}", rows(w))
        for e in range(EXPERTS):
            g, u, d = (rows(a[n][l, e]) for n in ("moe_w_gate_2", "moe_w_up_2", "moe_w_down_2"))
            for m in range(E_TILES):
                i = INDEX[f"moe{l}.{e * E_TILES + m}"]
                dst = stream[i, :, 0:2048].reshape(P, KT, 2, P)
                dst[:, :, 0] = g[:, :, m * P:(m + 1) * P]
                dst[:, :, 1] = u[:, :, m * P:(m + 1) * P]
                stream[i, :, 2048:3072] = d[:, m]

    vec = np.zeros((P, NVEC), np.float32)

    def col(name, value):
        at, n = VEC[name]
        vec[:, at:at + n] = np.ascontiguousarray(value).reshape(n, P).T

    def row(name, value):
        at, n = VEC[name]
        value = value.reshape(-1, n)
        vec[:value.shape[0], at:at + n] = value

    for name, key in (("c", "c"), ("ada_b", "ada_b"), ("norm_g", "norm_g"), ("final_g", "final_g"),
                      ("q_norm", "mla_q_norm"), ("kv_norm", "mla_kv_norm"), ("mu", "rwkv_mu"), ("w0", "rwkv_w0"),
                      ("a0", "rwkv_a0"), ("k_k", "rwkv_k_k"), ("k_a", "rwkv_k_a"), ("r_k", "rwkv_r_k"),
                      ("gn_w", "rwkv_gn_w"), ("gn_b", "rwkv_gn_b"), ("ln_g", "ln_g_2"), ("ln_b", "ln_b_2"),
                      ("conv", "ab_conv_2"), ("head_norm", "ab_head_norm_2"), ("cmp_pos", "c_cmp_pos_2")):
        col(name, a[key])
    row("rel_bias", a["rel_bias_2"])
    row("ab_gate_b", a["ab_gate_b_2"])
    row("c_gate_b", a["c_gate_b_2"])
    row("moe_b", np.concatenate([a["moe_br_g_2"], a["moe_br_e_2"].reshape(2, 16)], 1))
    return stream, vec


def kernel(**inputs):
    import concourse.bacc as bacc
    from concourse.bass_utils import run_bass_kernel_spmd

    a = {k: np.asarray(v) for k, v in inputs.items()}
    stream, vec = pack(a)
    x = np.ascontiguousarray(a["x"][0].reshape(T, KT, P).transpose(2, 1, 0)).reshape(P, KT * T)
    arrays = {"stream": stream, "const_tables": constants(), "vectors": vec, "x_in": x}
    nc = bacc.Bacc("TRN2", target_bir_lowering=False, num_devices=1)
    args = [nc.dram_tensor(n, v.shape, F32, kind="ExternalInput").ap() for n, v in arrays.items()]
    out = nc.dram_tensor("out", (P, KT * T), F32, kind="ExternalOutput").ap()
    scratch = nc.dram_tensor("bias_scratch", (8, 512), F32).ap()
    build(nc, *args, out, scratch)
    r = run_bass_kernel_spmd(nc, [arrays], core_ids=[0])
    got = r.results[0]["out"]
    return np.ascontiguousarray(got.reshape(P, KT, T).transpose(2, 1, 0)).reshape(1, T, D)
```
